# Optimizing a Trainium2 kernel written in Bass

```python
import jax
import jax.numpy as jnp
from jax import lax
import numpy as np

D_MODEL = 2048
BATCH = 1
SEQ = 256
DEPTH = 1

CHUNK = 64
NORM_EPS = 1e-6

RET_HEADS = 4
RET_DK = 256
RET_DV = 256
RET_QK = RET_HEADS * RET_DK
RET_WIDTH = RET_HEADS * RET_DV
ROPE_BASE = 10000.0

RWKV_HEAD = 64
RWKV_WIDTH = D_MODEL // 2
RWKV_HEADS = RWKV_WIDTH // RWKV_HEAD
DECAY_LORA = 64
AAA_LORA = 64
GATE_LORA = 128
RWKV_COLS = 3 * RWKV_WIDTH + DECAY_LORA + AAA_LORA + GATE_LORA
RWKV_GN_EPS = 64e-5

IN_COLS = 2 * RET_QK + 2 * RET_WIDTH + RWKV_COLS + 2 * D_MODEL

PEER_HEADS = 8
PEER_NKEYS = 128
PEER_NEXPERTS = PEER_NKEYS * PEER_NKEYS
PEER_DQ = 256
PEER_TOPK = 16
PEER_BLOCK = 128

kernel_name = 'hybrid_retention_rwkv7_peer_block'

def _split(z, sizes):
    idx = [int(s) for s in np.cumsum(sizes)[:-1]]
    return jnp.split(z, idx, axis=-1)

def rms_norm(x, w):
    xf = x.astype(jnp.float32)
    y = xf * lax.rsqrt(jnp.mean(xf * xf, axis=-1, keepdims=True) + NORM_EPS)
    return (y * w.astype(jnp.float32)).astype(x.dtype)

def head_norm(z, w, b, eps):
    h, d = z.shape[-2], z.shape[-1]
    zf = z.astype(jnp.float32)
    mu = jnp.mean(zf, axis=-1, keepdims=True)
    var = jnp.mean(jnp.square(zf - mu), axis=-1, keepdims=True)
    y = (zf - mu) * lax.rsqrt(var + eps)
    y = y * w.reshape(h, d).astype(jnp.float32) + b.reshape(h, d).astype(jnp.float32)
    return y.astype(z.dtype)

def rotary(z, pos):
    d = z.shape[-1]
    half = d // 2
    inv_freq = ROPE_BASE ** (-jnp.arange(half, dtype=jnp.float32) * 2.0 / d)
    ang = pos.astype(jnp.float32)[:, None] * inv_freq[None, :]
    cos = jnp.cos(ang)[None, :, None, :]
    sin = jnp.sin(ang)[None, :, None, :]
    zf = z.astype(jnp.float32)
    z1, z2 = zf[..., :half], zf[..., half:]
    return jnp.concatenate([z1 * cos - z2 * sin, z2 * cos + z1 * sin], axis=-1).astype(z.dtype)

def retention_chunkwise(q, k, v):
    b, t, h, dk = q.shape
    nc = t // CHUNK
    log_g = jnp.log(1.0 - jnp.exp2(-5.0 - jnp.arange(h, dtype=jnp.float32)))
    n = jnp.arange(CHUNK, dtype=jnp.float32)
    d_intra = jnp.exp(log_g[:, None, None] * jnp.abs(n[:, None] - n[None, :]))
    q_decay = jnp.exp(log_g[:, None] * (n[None, :] + 1.0))
    k_decay = jnp.exp(log_g[:, None] * (CHUNK - 1.0 - n[None, :]))
    chunk_decay = jnp.exp(log_g * CHUNK)

    def to_chunks(z):
        return z.reshape(b, nc, CHUNK, h, z.shape[-1]).transpose(0, 3, 1, 2, 4)

    qc, kc, vc = to_chunks(q), to_chunks(k), to_chunks(v)
    scores = jnp.einsum('bhcnd,bhcmd->bhcnm', qc, kc) * d_intra[None, :, None].astype(q.dtype)
    o_intra = jnp.einsum('bhcnm,bhcme->bhcne', scores, vc)
    kv = jnp.einsum('bhcmd,bhcme->bhcde', kc * k_decay[None, :, None, :, None].astype(k.dtype), vc)
    kv = jnp.moveaxis(kv, 2, 0).astype(jnp.float32)

    def step(s, kv_c):
        return s * chunk_decay[None, :, None, None] + kv_c, s

    s0 = jnp.zeros((b, h, dk, vc.shape[-1]), jnp.float32)
    _, s_prev = lax.scan(step, s0, kv)
    o_inter = jnp.einsum('bhcnd,cbhde->bhcne', qc * q_decay[None, :, None, :, None].astype(q.dtype),
                         s_prev.astype(q.dtype))
    o = o_intra + o_inter
    return o.transpose(0, 2, 3, 1, 4).reshape(b, t, h, vc.shape[-1])

def rwkv7_time_mix(z, mix, w0, w_up, a0, a_up, g_up, k_k, k_a, r_k, ln_w, ln_b):
    b, t, _ = z.shape
    z_prev = jnp.pad(z, ((0, 0), (1, 0), (0, 0)))[:, :-1]
    z = z + (z_prev - z) * mix
    r, k, v, xw, xa, xg = _split(z, [RWKV_WIDTH, RWKV_WIDTH, RWKV_WIDTH, DECAY_LORA, AAA_LORA, GATE_LORA])
    w = -jax.nn.softplus(-(w0 + jnp.tanh(xw) @ w_up)) - 0.5
    a = jax.nn.sigmoid(a0 + xa @ a_up)
    g = jax.nn.sigmoid(xg) @ g_up

    def heads(u):
        return u.reshape(b, t, RWKV_HEADS, RWKV_HEAD)

    kk = heads(k * k_k)
    kkf = kk.astype(jnp.float32)
    kk = (kkf / jnp.maximum(jnp.sqrt(jnp.sum(kkf * kkf, axis=-1, keepdims=True)), 1e-12)).astype(k.dtype)
    k = k * (1.0 + (a - 1.0) * k_a)
    r, k, v, a = heads(r), heads(k), heads(v), heads(a)
    decay = jnp.exp(-jnp.exp(heads(w).astype(jnp.float32)))

    def step(s, inp):
        r_t, w_t, k_t, v_t, kk_t, a_t = inp
        sa = jnp.einsum('bhij,bhj->bhi', s, -kk_t)
        s = s * w_t[:, :, None, :] + sa[..., None] * (kk_t * a_t)[:, :, None, :] + v_t[..., None] * k_t[:, :, None, :]
        return s, jnp.einsum('bhij,bhj->bhi', s, r_t)

    xs = tuple(jnp.moveaxis(u, 1, 0).astype(jnp.float32) for u in (r, decay, k, v, kk, a))
    s0 = jnp.zeros((b, RWKV_HEADS, RWKV_HEAD, RWKV_HEAD), jnp.float32)
    _, y = lax.scan(step, s0, xs)
    y = jnp.moveaxis(y, 0, 1).astype(z.dtype)
    y = head_norm(y, ln_w, ln_b, RWKV_GN_EPS)
    y = y + jnp.sum(r * k * r_k, axis=-1, keepdims=True) * v
    return y.reshape(b, t, RWKV_WIDTH) * g

def peer(u, w_q, keys_1, keys_2, expert_u, expert_v):
    b, t, d = u.shape
    tok = u.reshape(b * t, d)
    ntok = b * t
    q = (tok @ w_q).reshape(ntok, PEER_HEADS, 2, PEER_DQ // 2)
    s1 = jnp.einsum('nhd,kd->nhk', q[:, :, 0], keys_1).astype(jnp.float32)
    s2 = jnp.einsum('nhd,kd->nhk', q[:, :, 1], keys_2).astype(jnp.float32)
    v1, i1 = lax.top_k(s1, PEER_TOPK)
    v2, i2 = lax.top_k(s2, PEER_TOPK)
    cand = (v1[..., :, None] + v2[..., None, :]).reshape(ntok, PEER_HEADS, PEER_TOPK * PEER_TOPK)
    top, idx = lax.top_k(cand, PEER_TOPK)
    e1 = jnp.take_along_axis(i1, idx // PEER_TOPK, axis=-1)
    e2 = jnp.take_along_axis(i2, idx % PEER_TOPK, axis=-1)
    experts = e1 * PEER_NKEYS + e2
    gates = jax.nn.softmax(top, axis=-1).astype(u.dtype)
    nb = ntok // PEER_BLOCK

    def block(args):
        xb, eb, gb = args
        ue = jnp.take(expert_u, eb, axis=0)
        act = jax.nn.gelu(jnp.einsum('nhkd,nd->nhk', ue, xb), approximate=False) * gb
        return jnp.einsum('nhk,nhkd->nd', act, jnp.take(expert_v, eb, axis=0))

    out = lax.map(block, (tok.reshape(nb, PEER_BLOCK, d),
                          experts.reshape(nb, PEER_BLOCK, PEER_HEADS, PEER_TOPK),
                          gates.reshape(nb, PEER_BLOCK, PEER_HEADS, PEER_TOPK)))
    return out.reshape(b, t, d)

def setup_inputs(seed: int = 0) -> dict:
    key = jax.random.key(seed)
    ks = jax.random.split(key, 32)
    f32 = jnp.float32
    L = DEPTH

    def nrm(k, shape, scale):
        return jax.random.normal(k, shape, f32) * scale

    return {
        'x': nrm(ks[0], (BATCH, SEQ, D_MODEL), 1.0),
        'norm1_w': 1.0 + nrm(ks[1], (L, D_MODEL), 0.02),
        'w_in': nrm(ks[2], (L, D_MODEL, IN_COLS), D_MODEL ** -0.5),
        'ret_gn_w': 1.0 + nrm(ks[3], (L, RET_WIDTH), 0.02),
        'ret_gn_b': nrm(ks[4], (L, RET_WIDTH), 0.02),
        'rwkv_mix': jax.random.uniform(ks[5], (L, RWKV_COLS), f32),
        'rwkv_w0': jax.random.uniform(ks[6], (L, RWKV_WIDTH), f32, -6.0, -1.0),
        'rwkv_w_up': nrm(ks[7], (L, DECAY_LORA, RWKV_WIDTH), 0.5 * DECAY_LORA ** -0.5),
        'rwkv_a0': nrm(ks[8], (L, RWKV_WIDTH), 0.1),
        'rwkv_a_up': nrm(ks[9], (L, AAA_LORA, RWKV_WIDTH), 0.5 * AAA_LORA ** -0.5),
        'rwkv_g_up': nrm(ks[10], (L, GATE_LORA, RWKV_WIDTH), GATE_LORA ** -0.5),
        'rwkv_k_k': 0.85 + nrm(ks[11], (L, RWKV_WIDTH), 0.02),
        'rwkv_k_a': 1.0 + nrm(ks[12], (L, RWKV_WIDTH), 0.02),
        'rwkv_r_k': nrm(ks[13], (L, RWKV_HEADS, RWKV_HEAD), 0.1),
        'rwkv_ln_w': 1.0 + nrm(ks[14], (L, RWKV_WIDTH), 0.02),
        'rwkv_ln_b': nrm(ks[15], (L, RWKV_WIDTH), 0.02),
        'w_ret_branch': nrm(ks[16], (L, RET_WIDTH, D_MODEL), RET_WIDTH ** -0.5),
        'w_rwkv_branch': nrm(ks[17], (L, RWKV_WIDTH, D_MODEL), RWKV_WIDTH ** -0.5),
        'w_out': nrm(ks[18], (L, D_MODEL, D_MODEL), D_MODEL ** -0.5),
        'norm2_w': 1.0 + nrm(ks[19], (L, D_MODEL), 0.02),
        'peer_w_q': nrm(ks[20], (L, D_MODEL, PEER_HEADS * PEER_DQ), D_MODEL ** -0.5),
        'peer_keys_1': nrm(ks[21], (L, PEER_NKEYS, PEER_DQ // 2), (PEER_DQ // 2) ** -0.5),
        'peer_keys_2': nrm(ks[22], (L, PEER_NKEYS, PEER_DQ // 2), (PEER_DQ // 2) ** -0.5),
        'peer_u': nrm(ks[23], (L, PEER_NEXPERTS, D_MODEL), D_MODEL ** -0.5),
        'peer_v': nrm(ks[24], (L, PEER_NEXPERTS, D_MODEL), 0.5),
        'final_norm_w': 1.0 + nrm(ks[25], (D_MODEL,), 0.02),
    }

def reference(x, norm1_w, w_in, ret_gn_w, ret_gn_b, rwkv_mix, rwkv_w0, rwkv_w_up, rwkv_a0,
              rwkv_a_up, rwkv_g_up, rwkv_k_k, rwkv_k_a, rwkv_r_k, rwkv_ln_w, rwkv_ln_b,
              w_ret_branch, w_rwkv_branch, w_out, norm2_w, peer_w_q, peer_keys_1, peer_keys_2,
              peer_u, peer_v, final_norm_w):
    b, t, _ = x.shape
    pos = jnp.arange(t, dtype=jnp.int32)
    for layer in range(DEPTH):
        h = rms_norm(x, norm1_w[layer])
        z = h @ w_in[layer]
        q, k, v, g_ret_out, z_rwkv, gate_ret, gate_rwkv = _split(
            z, [RET_QK, RET_QK, RET_WIDTH, RET_WIDTH, RWKV_COLS, D_MODEL, D_MODEL])
        q = rotary(q.reshape(b, t, RET_HEADS, RET_DK), pos)
        k = rotary(k.reshape(b, t, RET_HEADS, RET_DK), pos) * (RET_DK ** -0.5)
        o_ret = retention_chunkwise(q, k, v.reshape(b, t, RET_HEADS, RET_DV))
        o_ret = head_norm(o_ret, ret_gn_w[layer], ret_gn_b[layer], NORM_EPS).reshape(b, t, RET_WIDTH)
        o_ret = o_ret * jax.nn.silu(g_ret_out)
        o_rwkv = rwkv7_time_mix(z_rwkv, rwkv_mix[layer], rwkv_w0[layer], rwkv_w_up[layer], rwkv_a0[layer],
                                rwkv_a_up[layer], rwkv_g_up[layer], rwkv_k_k[layer], rwkv_k_a[layer],
                                rwkv_r_k[layer], rwkv_ln_w[layer], rwkv_ln_b[layer])
        merged = (jax.nn.sigmoid(gate_ret) * (o_ret @ w_ret_branch[layer])
                  + jax.nn.sigmoid(gate_rwkv) * (o_rwkv @ w_rwkv_branch[layer]))
        x = x + merged @ w_out[layer]
        h2 = rms_norm(x, norm2_w[layer])
        x = x + peer(h2, peer_w_q[layer], peer_keys_1[layer], peer_keys_2[layer], peer_u[layer], peer_v[layer])
    return rms_norm(x, final_norm_w)


_drawn_inputs = setup_inputs


def setup_inputs(seed=0):
    import zlib

    import numpy as np

    out = dict(_drawn_inputs(seed))
    spreads = {}
    factors = {'ret_gn_w': 23.422,
     'ret_gn_b': 23.303,
     'rwkv_w_up': 2.842,
     'rwkv_k_k': 39.667,
     'rwkv_k_a': 3.047,
     'rwkv_ln_w': 26.243,
     'rwkv_ln_b': 24.122,
     'final_norm_w': 20.214,
     'norm2_w': 7.912}
    for name, (base, spread) in spreads.items():
        noise = np.random.default_rng([zlib.crc32(name.encode()), seed]).standard_normal(out[name].shape)
        drawn = base * np.exp(spread * noise) if base else spread * noise
        out[name] = jnp.asarray(drawn.astype(out[name].dtype))
    for name, factor in factors.items():
        out[name] = (out[name] * factor).astype(out[name].dtype)
    return out
```

```python
import numpy as np
import concourse.bass as bass
from concourse import mybir
from contextlib import ExitStack

P = 128
TOK = 256
DM = 2048
KC = DM // P
HEADS = 4
NE = 16384
BLOCKS = NE // P
TOPK = 16
NORM_EPS = 1e-6
GN_EPS = 64e-5

IDENT, IOTA, S1MASK, BDMASK, LEVEL, ONES, COS, SIN = 0, 128, 256, 512, 640, 1408, 1536, 1792
NCONST = 2048

VEC_ROWS = [("norm1_w", 16), ("rwkv_mix", 26), ("ret_gn_w", 8), ("ret_gn_b", 8), ("rwkv_w0", 8), ("rwkv_a0", 8),
            ("rwkv_k_k", 8), ("rwkv_k_a", 8), ("rwkv_r_k", 8), ("rwkv_ln_w", 8), ("rwkv_ln_b", 8)]
VEC = {}
_at = 0
for _name, _rows in VEC_ROWS:
    VEC[_name] = (_at, _rows)
    _at += _rows
VROWS = _at
VEC["norm2_w"] = (VROWS, 16)
NVEC = VROWS + 16

SEG = {"main": (0, 0, 29, 4, 0), "gates": (116, 29, 16, 4, 0), "ret": (180, 45, 8, 2, 0), "rwkv": (196, 53, 8, 2, 8),
       "out": (212, 61, 8, 4, 0), "wq": (244, 69, 8, 4, 0)}
U0, V0 = 276, 532


class Chain:

    def __init__(self, eng, sem):
        self.eng, self.sem, self.n, self.offset = eng, sem, 0, 0

    def link(self, ins):
        self.n += 1
        ins.then_inc(self.sem, 1)
        self.eng.wait_ge(self.sem, self.offset + self.n)


def run_loop(eng, first, count, body):
    body(first)
    with eng.Fori(first + 1, count) as i:
        body(i)


def wait_past(eng, sem, value):
    if not (isinstance(value, int) and value <= 0):
        eng.wait_ge(sem, value)


def hybrid_block_kernel(nc, a):
    f32, f32r, u32 = mybir.dt.float32, mybir.dt.float32r, mybir.dt.uint32
    ALU, ACT, AX = mybir.AluOpType, mybir.ActivationFunctionType, mybir.AxisListType
    ds = bass.ds
    ctx = ExitStack()
    with ctx:
        def sb(name, shape, dt=f32):
            return ctx.enter_context(nc.sbuf_tensor(name, shape, dt))

        class Sems(dict):
            def __missing__(self, name):
                self[name] = ctx.enter_context(nc.semaphore("s_" + name))
                return self[name]

        S = Sems()

        big = sb("big", [P, P, TOK])
        act_hi = sb("act_hi", [P, KC, TOK], f32r)
        act_lo = sb("act_lo", [P, KC, TOK], f32r)
        raw = sb("raw", [P, 4, 1024])
        w_hi = sb("w_hi", [P, 2, 1024], f32r)
        w_lo = sb("w_lo", [P, 2, 1024], f32r)
        cst = sb("cst", [P, NCONST])
        vec = sb("vec", [P, NVEC])
        extra = sb("extra", [P, 1024])
        onehot2 = sb("onehot2", [P, 512])
        small = sb("small", [P, 96])
        PS = ctx.enter_context(nc.psum_tensor("PS", [P, 8, 512], f32))
        x1_dram = nc.dram_tensor("x1_scratch", [TOK, DM], f32, kind="Internal").ap()

        ident = cst[:, IDENT:IDENT + P]
        iota = cst[:, IOTA:IOTA + P]
        bdmask = cst[:, BDMASK:BDMASK + P]
        ones_bd = cst[:, ONES:ONES + P]

        def Z(lo, hi):
            return big[:, lo:hi, :]

        def flat(ap):
            return ap.rearrange("p c n -> p (c n)")

        def half(k):
            return PS[:, k, :].rearrange("p (j n) -> p j n", j=2)

        def per_token(name, lo=0, n=None):
            at, rows = VEC[name]
            n = rows if n is None else n
            return vec[:, at + lo:at + lo + n].unsqueeze(2).broadcast_to([P, n, TOK])

        def v1(name, k):
            return vec[:, VEC[name][0] + k:VEC[name][0] + k + 1]

        def bc(ap, n, axis=1):
            b = ap.unsqueeze(axis)
            shape = list(b.shape)
            shape[axis] = n
            return b.broadcast_to(shape)

        ss, rstd = small[:, 0:2], small[:, 2:4]
        bnst = small[:, 4:10]
        mv = small[:, 10:26].rearrange("p (k c) -> p k c", c=2)
        rs8 = small[:, 26:34]
        pend = small[:, 34:66]
        sums = small[:, 66:82]

        r1 = flat(Z(58, 90))
        r2 = flat(Z(16, 24))
        r3 = flat(Z(106, 114))
        r4 = flat(Z(126, 128))
        place = [
            dict(B1=r1[:, 0:1024], B2=r1[:, 1024:2048], AM=r1[:, 2048:3072], XW=r1[:, 3072:4096], V=r1[:, 4096:4608],
                 Xt=r1[:, 4608:5120], bn=r1[:, 5120:5632], kn=r1[:, 5632:6144], Lm=r1[:, 6144:6656], S=extra[:, 512:768]),
            dict(B1=r1[:, 6656:7680], V=r1[:, 7680:8192], B2=r2[:, 0:1024], AM=r2[:, 1024:2048], XW=r3[:, 0:1024],
                 Xt=r3[:, 1024:1536], bn=r3[:, 1536:2048], kn=r4, Lm=extra[:, 0:512], S=extra[:, 768:1024]),
        ]

        def two(ap):
            return ap.rearrange("p (n w c) -> p n w c", n=4, w=2)

        def one(ap):
            return ap.rearrange("p (n c) -> p n c", n=4)

        B1 = [two(d["B1"]) for d in place]
        B2 = [two(d["B2"]) for d in place]
        AM = [two(d["AM"]) for d in place]
        AS = [two(d["XW"]) for d in place]
        X = [one(d["XW"][:, 0:512]) for d in place]
        Wn = [one(d["XW"][:, 512:1024]) for d in place]
        beta_bd, kappa_bd = X, Wn
        Vn = [one(d["V"]) for d in place]
        Xt = [one(d["Xt"]) for d in place]
        v_bd = Xt
        alpha_bd = [AM[g][:, :, 1, :] for g in range(2)]
        bn_ = [one(d["bn"]) for d in place]
        kn_ = [one(d["kn"]) for d in place]
        Lm = [one(d["Lm"]) for d in place]
        St = [d["S"].rearrange("p (n c) -> p n c", n=2) for d in place]

        keysT = flat(Z(49, 50))
        SC = [flat(Z(50 + 8 * t, 58 + 8 * t)).rearrange("p (j k) -> p j k", k=P) for t in range(2)]
        eg = extra[:, 0:768].rearrange("p (w n) -> p w n", w=3)
        hotA = cst[:, S1MASK:S1MASK + 1024].rearrange("p (n e) -> p n e", n=8)
        hotB = [cst[:, S1MASK + 1024:S1MASK + 1536].rearrange("p (n e) -> p n e", n=4),
                onehot2[:, :].rearrange("p (n e) -> p n e", n=4)]
        gelu_t = cst[:, S1MASK:S1MASK + 512].rearrange("p (n e) -> p n e", n=2)

        block = ctx.enter_context(nc.Block())

        def seg_loop(eng, name, body):
            u0, g0, ng, ku, _ = SEG[name]

            def pair(t, count=2):
                for j in range(count):
                    body(t, t * 2 + j, t * (ku // 2) + u0 // 4 + (j if ku == 4 else 0), j)
            pair(0)
            with eng.Fori(1, ng // 2) as t:
                pair(t)
            if ng % 2:
                pair(ng // 2, 1)

        def unit_slot(ku, j, kq):
            return kq if ku == 4 else 2 * j + kq

        @block.sync
        def _(sp):
            sp.dma_start(flat(Z(90, 106)).rearrange("p (a n) -> p a n", a=2),
                         a["x"][0].rearrange("(a p) n -> p a n", p=P)).then_inc(S["x_in"], 16)
            at = 0
            for name, rows in VEC_ROWS:
                src = a[name].rearrange("l h w -> (l h w)") if name == "rwkv_r_k" else a[name].rearrange("l n -> (l n)")
                sp.dma_start(flat(Z(122, 123))[at:at + rows, 0:P], src.rearrange("(r c) -> r c", c=P)).then_inc(S["rows_in"], 16)
                at += rows
            sp.dma_start(flat(Z(122, 123))[0:16, P:2 * P],
                         a["norm2_w"].rearrange("l n -> (l n)").rearrange("(r c) -> r c", c=P)).then_inc(S["rows_in"], 16)
            sp.dma_start(cst[:, :], a["consts"]).then_inc(S["const_in"], 16)
            sp.dma_start(flat(Z(82, 90)), a["ret_decay"]).then_inc(S["decay_in"], 16)

            def load_seg(name, weight, col0):
                _, g0, _, ku, _ = SEG[name]
                w = weight.rearrange("(c p) n -> p c n", p=P)

                def body(t, g, m, j):
                    for kq in range(ku):
                        slot = unit_slot(ku, j, kq)
                        if not (name == "main" and isinstance(t, int) and t == 0 and j == 0):
                            sp.wait_ge(S["unit_split"], m * 8 + 2 * slot - 6)
                        sp.dma_start(raw[:, slot, :].rearrange("p (c n) -> p c n", c=4),
                                     w[:, 4 * kq:4 * kq + 4, ds(g * 256 + col0, 256)]).then_inc(S[f"raw_in{slot}"], 16)
                seg_loop(sp, name, body)

            w_in = a["w_in"][0]
            load_seg("main", w_in, 0)
            sp.wait_ge(S["st_done"], 4)
            sp.dma_start(flat(Z(84, 88))[0:64, :], a["rwkv_w_up"][0]).then_inc(S["up_in"], 16)
            sp.dma_start(flat(Z(84, 88))[64:128, :], a["rwkv_a_up"][0]).then_inc(S["up_in"], 16)
            sp.dma_start(flat(Z(122, 126)), a["rwkv_g_up"][0]).then_inc(S["gup_in"], 16)
            load_seg("gates", w_in, 58 * P)
            load_seg("ret", a["w_ret_branch"][0], 0)
            load_seg("rwkv", a["w_rwkv_branch"][0], 0)
            load_seg("out", a["w_out"][0], 0)
            sp.wait_ge(S["merged"], 1)
            sp.dma_start(flat(Z(90, 106)).rearrange("p (a n) -> p a n", a=2),
                         a["x"][0].rearrange("(a p) n -> p a n", p=P)).then_inc(S["x_again"], 16)
            sp.dma_start(flat(Z(48, 49))[:, 0:P], a["peer_keys_1"][0]).then_inc(S["keys_in"], 16)
            sp.dma_start(flat(Z(48, 49))[:, P:2 * P], a["peer_keys_2"][0]).then_inc(S["keys_in"], 16)
            load_seg("wq", a["peer_w_q"][0], 0)
            sp.wait_ge(S["x1_done"], 8)
            sp.dma_start(x1_dram.rearrange("(a p) n -> p a n", p=P),
                         flat(Z(90, 106)).rearrange("p (a n) -> p a n", a=2)).then_inc(S["x1_out"], 16)
            u_rows = a["peer_u"][0].rearrange("(b e) n -> b e n", e=P)
            v_rows = a["peer_v"][0].rearrange("(b e) n -> b e n", e=P)

            def load_experts(rows, it, sem, value):
                for k in range(4):
                    sp.wait_ge(S[sem], value(k))
                    sp.dma_start(raw[:, k, :], rows[ds(it * 2 + k // 2, 1), :, (k % 2) * 1024:(k % 2 + 1) * 1024]
                                 .rearrange("a e n -> e (a n)")).then_inc(S[f"raw_in{k}"], 16)
            load_experts(u_rows, 0, "unit_split", lambda k: 2 * (U0 + k) - 6)
            with sp.Fori(1, BLOCKS // 2) as it:
                load_experts(u_rows, it, "uT_bank", lambda k: it * 8 + 2 * k - 6)
            load_experts(v_rows, 0, "uT_bank", lambda k: 4 * BLOCKS + 2 * k - 6)
            with sp.Fori(1, BLOCKS // 2) as it:
                load_experts(v_rows, it, "unit_split", lambda k: it * 8 + (2 * (V0 + k) - 6))
            sp.wait_ge(S["unit_used"], V0 + 2 * 40)
            sp.wait_ge(S["x1_out"], 16)
            sp.dma_start(flat(Z(0, 16)).rearrange("p (a n) -> p a n", a=2),
                         x1_dram.rearrange("(a p) n -> p a n", p=P)).then_inc(S["x1_in"], 16)
            sp.dma_start(flat(Z(16, 24)), a["final_norm_w"].partition_broadcast(P)).then_inc(S["fw_in"], 16)
            for tt in range(2):
                sp.wait_ge(S["y_ready"], tt + 1)
                sp.dma_start(a["out"][0, tt * P:(tt + 1) * P, :], flat(Z(24 + 8 * tt, 32 + 8 * tt))).then_inc(S["stored"], 16)
            sp.wait_ge(S["stored"], 32)

        @block.tensor
        def _(pe):
            def mm3(out, wh, wl, xh, xl, start, stop):
                pe.matmul(out, wh, xh, start=start, stop=False)
                pe.matmul(out, wh, xl, start=False, stop=False)
                return pe.matmul(out, wl, xh, start=False, stop=stop)

            def project(name):
                u0, g0, ng, ku, koff = SEG[name]

                def body(t, g, m, j):
                    par = (g0 + j) % 2
                    if not (name == "main" and isinstance(t, int) and t == 0):
                        pe.wait_ge(S["proj_evac"], g + g0 - 1)
                    for kq in range(ku):
                        slot = unit_slot(ku, j, kq)
                        for hh in range(2):
                            pe.wait_ge(S["unit_split"], m * 8 + 2 * slot + hh + 1)
                            for c in (2 * hh, 2 * hh + 1):
                                kc = koff + 4 * kq + c
                                for jj in range(2):
                                    cols = slice(c * 256 + jj * P, c * 256 + (jj + 1) * P)
                                    last = mm3(PS[:, 2 * par + jj, 0:TOK], w_hi[:, slot % 2, cols], w_lo[:, slot % 2, cols],
                                               act_hi[:, kc, :], act_lo[:, kc, :],
                                               kq == 0 and c == 0, kq == ku - 1 and c == 3)
                        last.then_inc(S["unit_used"], 1)
                seg_loop(pe, name, body)

            pe.wait_ge(S["const_in"], 16)
            pe.wait_ge(S["rows_in"], 16 * 12)
            pe.transpose(PS[:, 7, 0:VROWS], flat(Z(122, 123))[0:VROWS, 0:P], ident[0:VROWS, 0:VROWS])
            pe.transpose(PS[:, 7, VROWS:NVEC], flat(Z(122, 123))[0:16, P:2 * P], ident[0:16, 0:16]).then_inc(S["vecT"], 1)
            xn = [flat(Z(106 + 8 * t, 114 + 8 * t)) for t in range(2)]

            def transpose_tokens(src, done, bank7_free):
                for gi in range(8):
                    tt, cg = gi // 4, gi % 4
                    if gi == 7:
                        bank7_free()
                    for c in range(4):
                        col = (4 * cg + c) * P
                        last = pe.transpose(PS[:, gi, c * P:(c + 1) * P], src[tt][:, col:col + P], ident)
                    last.then_inc(S[done], 1)
            pe.wait_ge(S["normed"], 2)
            transpose_tokens(xn, "xT_done", lambda: pe.wait_ge(S["vec_done"], 1))

            pe.wait_ge(S["act_split"], 4)
            project("main")

            pe.wait_ge(S["proj_evac"], 29)
            for bank in range(4):
                tt, q = bank // 2, bank % 2
                for c in range(4):
                    last = pe.transpose(PS[:, bank, c * P:(c + 1) * P], big[:, 16 + 4 * q + c, tt * P:(tt + 1) * P], ident)
                last.then_inc(S["vT_done"], 1)
            pe.wait_ge(S["rot_done"], 2)
            for h in range(HEADS):
                for mt in range(2):
                    for kc in range(2):
                        last = pe.matmul(half(4 + h)[:, mt, :], big[:, 8 + 2 * h + kc, mt * P:(mt + 1) * P],
                                         big[:, 2 * h + kc, :], start=kc == 0, stop=kc == 1)
                last.then_inc(S["sc_done"], 1)
            sT = Z(98, 106).rearrange("p (h m) n -> p h m n", m=2)
            vtok = Z(106, 114).rearrange("p (m h) n -> p m h n", m=2)
            pe.wait_ge(S["vtok"], 4)
            for h in range(HEADS):
                pe.wait_ge(S["st_done"], h + 1)
                for nt in range(2):
                    for mt in range(2):
                        last = pe.matmul(half(h)[:, nt, :], sT[:, h, mt, nt * P:(nt + 1) * P], vtok[:, mt, h, :],
                                         start=mt == 0, stop=mt == 1)
                last.then_inc(S["o_done"], 1)
            pe.wait_ge(S["on_done"], 8)
            for h in range(HEADS):
                for ec in range(2):
                    for nt in range(2):
                        last = pe.transpose(PS[:, 4 + h, ec * 256 + nt * P:ec * 256 + (nt + 1) * P],
                                            big[:, 58 + 2 * h + nt, ec * P:(ec + 1) * P], ident)
                last.then_inc(S["oT_done"], 1)

            up = flat(Z(84, 88))
            pe.wait_ge(S["up_in"], 32)
            pe.wait_ge(S["lora_in"], 1)
            for k in range(8):
                last = pe.matmul(half(k // 2)[:, k % 2, :], up[0:64, k * P:(k + 1) * P], big[0:64, 56, :], start=True, stop=True)
                if k % 2:
                    last.then_inc(S["lora_w"], 1)
            pe.wait_ge(S["oret_pre"], 8)
            for k in range(8):
                last = pe.matmul(half(4 + k // 2)[:, k % 2, :], up[64:128, k * P:(k + 1) * P], big[64:128, 56, :],
                                 start=True, stop=True)
                if k % 2:
                    last.then_inc(S["lora_a"], 1)
            pe.wait_ge(S["sq_done"], 1)
            pe.wait_ge(S["sg_done"], 8)
            for q in range(4):
                last = pe.matmul(PS[:, q, :], ones_bd, flat(Z(16 + 2 * q, 18 + 2 * q)), start=True, stop=True)
            last.then_inc(S["kn_done"], 1)

            pe.wait_ge(S["a_done"], 8)
            pe.wait_ge(S["kn_read"], 1)
            def pairs(i):
                for g in range(2):
                    b = 4 * g
                    pe.wait_ge(S[f"prep{g}"], i + 1)
                    wait_past(pe, S[f"ye{g}"], i * 2)
                    wait_past(pe, S[f"st{g}"], i * 2)
                    for q, lhs in enumerate((beta_bd, kappa_bd)):
                        for n in range(4):
                            for w, src in enumerate((24, 90)):
                                rhs = big[:, ds(i * 2 + (src + g), 1), n * 64:(n + 1) * 64].broadcast_to([P, 2, 64])
                                col = (n % 2) * 256 + w * P
                                last = pe.matmul(PS[:, b + 2 * q + n // 2, col:col + P], lhs[g][:, n, :], rhs, start=True, stop=True)
                    last.then_inc(S[f"s1{g}"], 1)
                for g in range(2):
                    b = 4 * g
                    pe.wait_ge(S[f"s1e{g}"], i * 4 + 4)
                    for w, src in enumerate((v_bd, alpha_bd, beta_bd, kappa_bd)):
                        for n in range(4):
                            last = pe.transpose(PS[:, b + w, n * P:(n + 1) * P], src[g][:, n, :], ident)
                    last.then_inc(S[f"s2{g}"], 1)
                for g in range(2):
                    b = 4 * g
                    pe.wait_ge(S[f"va{g}"], i * 2 + 2)
                    pe.wait_ge(S[f"xt1{g}"], i + 1)
                    for n in range(4):
                        last = pe.transpose(PS[:, b, n * P:(n + 1) * P], Xt[g][:, n, :], ident)
                    last.then_inc(S[f"xp{g}"], 1)
                for lv in range(5):
                    for g in range(2):
                        b = 4 * g
                        pe.wait_ge(S[f"lm{g}"], i * 5 + lv + 1)
                        if lv == 0:
                            pe.wait_ge(S[f"xc{g}"], i * 10 + 1)
                        else:
                            pe.wait_ge(S[f"xc{g}"], i * 10 + 2 * lv + 1)
                        for n in range(4):
                            last = pe.matmul(PS[:, b + 1, n * P:(n + 1) * P], Lm[g][:, n, :], X[g][:, n, :], start=True, stop=True)
                        last.then_inc(S[f"w{g}"], 1)
                    for g in range(2):
                        b = 4 * g
                        if lv == 0:
                            pe.wait_ge(S[f"bk{g}"], i * 2 + 2)
                        pe.wait_ge(S[f"wn{g}"], i * 5 + lv + 1)
                        if lv < 4:
                            for n in range(4):
                                pe.matmul(PS[:, b + 2, n * P:(n + 1) * P], Xt[g][:, n, :], Wn[g][:, n, :], start=True, stop=True)
                        for n in range(4):
                            last = pe.matmul(PS[:, b + 3, n * P:(n + 1) * P], Wn[g][:, n, :], Xt[g][:, n, :], start=True, stop=True)
                        last.then_inc(S[f"xx{g}"], 1)
                for g in range(2):
                    b = 4 * g
                    for n in range(4):
                        last = pe.matmul(PS[:, b, n * P:(n + 1) * P], B2[g][:, n, 0, :], Vn[g][:, n, :], start=True, stop=True)
                    last.then_inc(S[f"mv{g}"], 1)
                for g in range(2):
                    b = 4 * g
                    pe.wait_ge(S[f"xc{g}"], i * 10 + 10)
                    pe.wait_ge(S[f"mvc{g}"], i + 1)
                    for n in range(4):
                        last = pe.matmul(PS[:, b + 1 + n // 2, (n % 2) * 256:(n % 2 + 1) * 256], Xt[g][:, n, :],
                                         AM[g][:, n, :, :], start=True, stop=True)
                    last.then_inc(S[f"as{g}"], 1)
                for g in range(2):
                    b = 4 * g
                    pe.wait_ge(S[f"asc{g}"], i * 2 + 2)
                    for n in range(4):
                        cols = slice(n * P, (n + 1) * P)
                        pe.matmul(PS[:, b + 3, cols], AS[g][:, n, 0, :], bn_[g][:, n, :], start=True, stop=True)
                        pe.matmul(PS[:, b, cols], kn_[g][:, n, :], Vn[g][:, n, :], start=True, stop=False)
                        pe.matmul(PS[:, b, cols], bn_[g][:, n, :], AS[g][:, n, 1, :], start=False, stop=True)
                        last = pe.matmul(PS[:, b + 1, cols], AS[g][:, n, 0, :], B1[g][:, n, 1, :], start=True, stop=True)
                    last.then_inc(S[f"f{g}"], 1)

                def y_chunk(g, n, state):
                    out = PS[:, 4 * g + 2, n * P:(n + 1) * P]
                    if state is not None:
                        pe.matmul(out, state, B2[g][:, n, 0, :], start=True, stop=False)
                    pe.matmul(out, AS[g][:, n, 1, :], B1[g][:, n, 1, :], start=state is None, stop=False)
                    return pe.matmul(out, Vn[g][:, n, :], B2[g][:, n, 1, :], start=False, stop=True)
                for n in range(4):
                    for g in range(2):
                        state = [None, B1[g][:, 0, 0, :], St[g][:, 0, :], St[g][:, 1, :]][n]
                        if n == 0:
                            pe.wait_ge(S[f"fe{g}"], i * 4 + 4)
                        if n >= 2:
                            pe.wait_ge(S[f"st{g}"], i * 2 + n - 1)
                        if n in (1, 2):
                            pe.matmul(PS[:, 4 * g + 3, n * P:(n + 1) * P], Lm[g][:, n, :], state, start=True,
                                      stop=True).then_inc(S[f"ch{g}"], 1)
                        last = y_chunk(g, n, state)
                        if n == 3:
                            last.then_inc(S[f"y{g}"], 1)
            run_loop(pe, 0, 4, pairs)

            for g in range(2):
                pe.wait_ge(S[f"ye{g}"], 8)
                pe.wait_ge(S[f"st{g}"], 8)
            for q in range(4):
                last = pe.matmul(PS[:, q, :], ones_bd, flat(Z(114 + 2 * q, 116 + 2 * q)), start=True, stop=True)
            last.then_inc(S["ym_done"], 1)
            pe.wait_ge(S["ysq_done"], 1)
            for q in range(4):
                last = pe.matmul(PS[:, 4 + q, :], ones_bd, flat(Z(66 + 2 * q, 68 + 2 * q)), start=True, stop=True)
            last.then_inc(S["yv_done"], 1)
            pe.wait_ge(S["rk_done"], 1)
            pe.wait_ge(S["yc_done"], 1)
            for q in range(4):
                last = pe.matmul(PS[:, q, :], ones_bd, flat(Z(32 + 2 * q, 34 + 2 * q)), start=True, stop=True)
            last.then_inc(S["bonus"], 1)
            pe.wait_ge(S["gup_in"], 16)
            pe.wait_ge(S["yvar"], 1)
            gup = flat(Z(122, 126))
            for k in range(8):
                last = pe.matmul(half(4 + k // 2)[:, k % 2, :], gup[:, k * P:(k + 1) * P], big[:, 57, :], start=True, stop=True)
            last.then_inc(S["gate_up"], 1)
            pe.wait_ge(S["bonus_read"], 1)
            project("gates")
            pe.wait_ge(S["act_split"], 8)
            project("ret")
            project("rwkv")
            pe.wait_ge(S["act_split"], 12)
            project("out")
            pe.wait_ge(S["proj_evac"], 69)
            for gi in range(8):
                tt, cg = gi // 4, gi % 4
                for c in range(4):
                    last = pe.transpose(PS[:, gi, c * P:(c + 1) * P], big[:, 4 * cg + c, tt * P:(tt + 1) * P], ident)
                last.then_inc(S["dT_done"], 1)
            pe.wait_ge(S["normed"], 4)
            transpose_tokens(xn, "x2T_done", lambda: None)
            pe.wait_ge(S["keys_in"], 32)
            pe.wait_ge(S["h2T"], 8)
            for w in range(2):
                last = pe.transpose(PS[:, 7, w * P:(w + 1) * P], flat(Z(48, 49))[:, w * P:(w + 1) * P], ident)
            last.then_inc(S["kT_done"], 1)
            pe.wait_ge(S["act_split"], 16)
            project("wq")
            pe.wait_ge(S["proj_evac"], 77)
            pe.wait_ge(S["keysT"], 1)
            for tt in range(2):
                for q in range(4):
                    for c in range(4):
                        j = 4 * q + c
                        last = pe.matmul(PS[:, 4 * tt + q, c * P:(c + 1) * P], big[:, 32 + j, tt * P:(tt + 1) * P],
                                         keysT[:, (j % 2) * P:(j % 2 + 1) * P], start=True, stop=True)
                last.then_inc(S["s_done"], 1)
            pe.wait_ge(S["sc_copied"], 2)
            for w, src in enumerate((66, 68, 70)):
                for tt in range(2):
                    pe.wait_ge(S["picked"], tt + 1)
                    last = pe.transpose(PS[:, 0 if w < 2 else 1, (w % 2) * 256 + tt * P:(w % 2) * 256 + (tt + 1) * P],
                                        big[:, src + tt, 0:P], ident)
            last.then_inc(S["egT"], 1)
            pe.wait_ge(S["eg_done"], 2)

            def tokens(i):
                for s in range(2):
                    pe.wait_ge(S[f"hot{s}"], i + 1)
                    wait_past(pe, S[f"g_evac{s}"], i)
                    for t in range(4):
                        last = pe.matmul(PS[:, 4 + s, t * P:(t + 1) * P], hotB[s][:, t, :], hotA[:, 4 * s + t, :], start=True, stop=True)
                    last.then_inc(S[f"g_mm{s}"], 1)
            run_loop(pe, 0, 32, tokens)

            def ut(it, k):
                pe.wait_ge(S[f"raw_in{k}"], it * 16 + 16 * (U0 // 4 + 1))
                for hh in range(2):
                    pe.wait_ge(S["unit_split"], it * 8 + (2 * (U0 + k) - 3 + hh))
                    for c in range(4):
                        last = pe.transpose(PS[:, 2 * (k % 2) + hh, c * P:(c + 1) * P],
                                            raw[:, k, (4 * hh + c) * P:(4 * hh + c + 1) * P], ident)
                    last.then_inc(S["uT_bank"], 1)

            def um(it, k):
                for hh in range(2):
                    pe.wait_ge(S["unit_split"], it * 8 + (2 * (U0 + k) + hh + 1))
                    if k % 2 == 0 and hh == 0:
                        wait_past(pe, S[f"gelu{k // 2}"], it)
                    for c in range(4):
                        kc = (k % 2) * 8 + 4 * hh + c
                        cols = slice((4 * hh + c) * P, (4 * hh + c + 1) * P)
                        last = mm3(PS[:, 4 + k // 2, 0:TOK], w_hi[:, k % 2, cols], w_lo[:, k % 2, cols],
                                   act_hi[:, kc, :], act_lo[:, kc, :], kc == 0, kc == 15)
                last.then_inc(S["unit_used"], 1)

            for s in range(2):
                pe.wait_ge(S[f"g_evac{s}"], 32)
            ut(0, 0)

            def u_blocks(it):
                for k in range(4):
                    if k < 3:
                        ut(it, k + 1)
                    else:
                        ut(it + 1, 0)
                    um(it, k)
            run_loop(pe, 0, BLOCKS // 2 - 1, u_blocks)
            last_it = BLOCKS // 2 - 1
            for k in range(4):
                if k < 3:
                    ut(last_it, k + 1)
                um(last_it, k)

            pe.wait_ge(S["gelu0"], BLOCKS // 2)
            pe.wait_ge(S["gelu1"], BLOCKS // 2)

            def vm(it, k, start, stop):
                b = k // 2
                if k % 2 == 0:
                    pe.wait_ge(S["act2_split"], it * 2 + b + 1)
                for hh in range(2):
                    pe.wait_ge(S["unit_split"], it * 8 + (2 * (V0 + k) + hh + 1))
                    for tt in range(2):
                        out = PS[:, 4 * tt + 2 * (k % 2) + hh, :]
                        cols = slice(hh * 512, (hh + 1) * 512)
                        ah = act_hi[:, b, tt * P:(tt + 1) * P]
                        al = act_lo[:, b, tt * P:(tt + 1) * P]
                        pe.matmul(out, ah, w_hi[:, k % 2, cols], start=start and k < 2, stop=False)
                        pe.matmul(out, ah, w_lo[:, k % 2, cols], start=False, stop=False)
                        last = pe.matmul(out, al, w_hi[:, k % 2, cols], start=False, stop=stop and k >= 2)
                last.then_inc(S["unit_used"], 1)
            for k in range(4):
                vm(0, k, True, False)
            with pe.Fori(1, BLOCKS // 2 - 1) as it:
                for k in range(4):
                    vm(it, k, False, False)
            for k in range(4):
                vm(BLOCKS // 2 - 1, k, False, True)

        @block.scalar
        def _(act):
            ch = Chain(act, S["act_chain"])

            def hi(m, slot, hh, used):
                if hh == 0:
                    act.wait_ge(S[f"raw_in{slot}"], m * 16 + 16)
                    if used is not None:
                        act.wait_ge(S["unit_used"], used)
                act.activation(w_hi[:, slot % 2, hh * 512:(hh + 1) * 512], raw[:, slot, hh * 512:(hh + 1) * 512],
                               ACT.Copy).then_inc(S["unit_hi"], 1)

            def split_seg(name, evac=None):
                u0, g0, ng, ku, _ = SEG[name]

                def body(t, g, m, j):
                    for kq in range(ku):
                        slot = unit_slot(ku, j, kq)
                        first = name == "main" and isinstance(t, int) and t == 0 and j == 0 and kq < 2
                        for hh in range(2):
                            hi(m, slot, hh, None if first else m * 4 + slot - 1)
                        if kq == 1 and evac and not (isinstance(g, int) and g == 0):
                            act.wait_ge(S["unit_used"], m * 4 + (2 * j if ku == 2 else 0))
                            evac(g - 1, (g0 + j + 1) % 2)
                seg_loop(act, name, body)
                if evac:
                    act.wait_ge(S["unit_used"], u0 + ng * ku)
                    evac(ng - 1, (g0 + ng - 1) % 2)

            def split_act(src, n):
                for pc in range(4):
                    act.activation(act_hi[:, 4 * pc:4 * pc + 4, :], src[:, 4 * pc:4 * pc + 4, :], ACT.Copy).then_inc(S["act_hi"], 1)

            def norm_root(src, junk, nth):
                for tt in range(2):
                    act.activation(junk[tt], src[tt], ACT.Square, accum_out=ss[:, tt:tt + 1]).then_inc(S["norm_sum"], 1)
                act.wait_ge(S["norm_mean"], nth + 1)
                act.activation(rstd, ss, ACT.Sqrt).then_inc(S["norm_root"], 1)

            def norm(src, dst, nth):
                norm_root(src, dst, nth)
                act.wait_ge(S["norm_rstd"], nth + 1)
                for tt in range(2):
                    act.activation(dst[tt], src[tt], ACT.Copy, scale=rstd[:, tt:tt + 1]).then_inc(S["normed"], 1)

            xs = [flat(Z(90 + 8 * t, 98 + 8 * t)) for t in range(2)]
            xn = [flat(Z(106 + 8 * t, 114 + 8 * t)) for t in range(2)]
            act.wait_ge(S["x_in"], 16)
            norm(xs, xn, 0)
            act.wait_ge(S["hT"], 8)
            split_act(Z(58, 74), 0)

            def evac_copy(base):
                def evac(g, par):
                    act.activation(big[:, ds(g * 2 + base, 2), :] if not isinstance(g, int) else big[:, base + 2 * g:base + 2 * g + 2, :],
                                   PS[:, 2 * par:2 * par + 2, 0:TOK], ACT.Copy).then_inc(S["proj_evac"], 1)
                return evac

            def evac_sigmoid(base):
                def evac(g, par):
                    act.activation(big[:, ds(g * 2 + base, 2), :] if not isinstance(g, int) else big[:, base + 2 * g:base + 2 * g + 2, :],
                                   PS[:, 2 * par:2 * par + 2, 0:TOK], ACT.Sigmoid).then_inc(S["proj_evac"], 1)
                return evac
            split_seg("main", evac_copy(0))

            vtok = flat(Z(106, 114))
            for bank in range(4):
                act.wait_ge(S["vT_done"], bank + 1)
                act.activation(vtok[:, bank * 512:(bank + 1) * 512], PS[:, bank, :], ACT.Copy).then_inc(S["vtok"], 1)
            act.wait_ge(S["proj_evac"], 29)
            act.activation(Z(24, 32), Z(24, 32), ACT.Silu).then_inc(S["silu"], 1)
            act.wait_ge(S["on_var"], 1)
            act.activation(rs8, rs8, ACT.Sqrt).then_inc(S["on_sqrt"], 1)

            act.wait_ge(S["mixB"], 1)
            act.activation(big[0:64, 56, :], big[0:64, 56, :], ACT.Tanh).then_inc(S["lora_in"], 1)
            act.activation(Z(57, 58), Z(57, 58), ACT.Sigmoid).then_inc(S["xg_done"], 1)
            for k in range(8):
                if k % 2 == 0:
                    act.wait_ge(S["lora_w"], k // 2 + 1)
                act.activation(big[:, 90 + k, :], half(k // 2)[:, k % 2, :], ACT.Sigmoid, bias=v1("rwkv_w0", k)).then_inc(S["sg_done"], 1)
            for k in range(8):
                if k % 2 == 0:
                    act.wait_ge(S["lora_a"], k // 2 + 1)
                act.activation(big[:, 8 + k, :], half(4 + k // 2)[:, k % 2, :], ACT.Sigmoid, bias=v1("rwkv_a0", k)).then_inc(S["a_done"], 1)
            act.wait_ge(S["sg_done"], 8)
            act.activation(Z(90, 98), Z(90, 98), ACT.Exp, scale=-float(np.exp(-0.5))).then_inc(S["dec_done"], 1)
            act.wait_ge(S["kn_done"], 1)
            act.activation(flat(Z(16, 24)).rearrange("p (q n) -> p q n", q=4), PS[:, 0:4, :], ACT.Sqrt).then_inc(S["kn_read"], 1)
            act.wait_ge(S["scan_done"], 1)
            pc = Z(98, 106).rearrange("p c (n t) -> p (c n) t", t=64)
            pp = Z(114, 122).rearrange("p c (n t) -> p (c n) t", t=64)
            act.activation(pp[:, :, 1:64], pc[:, :, 0:63], ACT.Copy).then_inc(S["pprev"], 1)
            with act.Fori(0, 4) as i:
                for g in range(2):
                    act.wait_ge(S[f"s2{g}"], i + 1)
                    for w, dst in enumerate((bn_, kn_)):
                        act.activation(dst[g], PS[:, 4 * g + 2 + w, :].rearrange("p (n c) -> p n c", n=4), ACT.Copy).then_inc(S[f"bk{g}"], 1)
                for g in range(2):
                    act.wait_ge(S[f"xp{g}"], i + 1)
                    act.activation(X[g], PS[:, 4 * g, :].rearrange("p (n c) -> p n c", n=4), ACT.Copy).then_inc(S[f"xc{g}"], 1)
                for lv in range(5):
                    for g in range(2):
                        act.wait_ge(S[f"xx{g}"], i * 5 + lv + 1)
                        if lv < 4:
                            act.activation(X[g], PS[:, 4 * g + 2, :].rearrange("p (n c) -> p n c", n=4), ACT.Copy).then_inc(S[f"xc{g}"], 1)
                        act.activation(Xt[g], PS[:, 4 * g + 3, :].rearrange("p (n c) -> p n c", n=4), ACT.Copy).then_inc(S[f"xc{g}"], 1)
                for g in range(2):
                    act.wait_ge(S[f"mv{g}"], i + 1)
                    act.activation(AM[g][:, :, 1, :], PS[:, 4 * g, :].rearrange("p (n c) -> p n c", n=4), ACT.Copy).then_inc(S[f"mvc{g}"], 1)
                for g in range(2):
                    act.wait_ge(S[f"as{g}"], i + 1)
                    for q in range(2):
                        act.activation(AS[g][:, 2 * q:2 * q + 2, :, :],
                                       PS[:, 4 * g + 1 + q, :].rearrange("p (n w c) -> p n w c", n=2, w=2), ACT.Copy,
                                       scale=-1.0).then_inc(S[f"asc{g}"], 1)
                for g in range(2):
                    act.wait_ge(S[f"y{g}"], i + 1)
                    for h in range(2):
                        rows = slice(64 * h, 64 * h + 64)
                        act.activation(big[rows, ds(i * 2 + (114 + g), 1), :].rearrange("p a (n t) -> p (a n) t", n=4),
                                       PS[rows, 4 * g + 2, :].rearrange("p (n w t) -> p n w t", n=4, w=2)[:, :, h, :],
                                       ACT.Copy).then_inc(S[f"ye{g}"], 1)
            act.wait_ge(S["yc_done"], 1)
            act.activation(Z(66, 74), Z(58, 66), ACT.Square).then_inc(S["ysq_done"], 1)
            act.wait_ge(S["yvar"], 1)
            act.activation(Z(74, 82), Z(74, 82), ACT.Sqrt).then_inc(S["ystd"], 1)
            act.wait_ge(S["orwkv"], 1)
            split_seg("gates", evac_sigmoid(58))
            act.wait_ge(S["orwkv"], 1)
            split_act(Z(0, 16), 1)
            split_seg("ret")
            split_seg("rwkv")
            act.wait_ge(S["unit_used"], SEG["out"][0])
            act.wait_ge(S["merged"], 1)
            split_act(Z(58, 74), 2)
            split_seg("out", evac_copy(0))
            act.wait_ge(S["x1_done"], 8)
            norm(xs, xn, 1)
            act.wait_ge(S["h2T"], 8)
            split_act(Z(16, 32), 3)
            act.wait_ge(S["kT_done"], 1)
            act.activation(keysT, PS[:, 7, 0:256], ACT.Copy).then_inc(S["keysT"], 1)
            split_seg("wq", evac_copy(32))
            for tt in range(2):
                act.wait_ge(S["s_done"], tt + 1)
                act.activation(flat(Z(50 + 8 * tt, 58 + 8 * tt)).rearrange("p (q n) -> p q n", q=4), PS[:, 4 * tt:4 * tt + 4, :],
                               ACT.Copy).then_inc(S["sc_copied"], 1)
            for tt in range(2):
                act.wait_ge(S["topm"], tt + 1)
                act.activation(big[:, 70 + tt, 0:P], big[:, 70 + tt, 0:P], ACT.Exp).then_inc(S["gexp"], 1)
            G = big[:, :, :]
            with act.Fori(0, 32) as i:
                for s in range(2):
                    act.wait_ge(S[f"g_mm{s}"], i + 1)
                    act.activation(G[:, :, ds(i * 8 + 4 * s, 4)],
                                   PS[:, 4 + s, :].rearrange("p (t e) -> p e t", t=4), ACT.Copy).then_inc(S[f"g_evac{s}"], 1)

            def u_hi(it, k):
                for hh in range(2):
                    act.wait_ge(S["uT_bank"], it * 8 + (2 * k + hh + 1))
                    if hh == 0:
                        act.wait_ge(S["unit_used"], it * 4 + (U0 + k - 1))
                    act.activation(w_hi[:, k % 2, hh * 512:(hh + 1) * 512], PS[:, 2 * (k % 2) + hh, :], ACT.Copy).then_inc(S["unit_hi"], 1)

            for k in range(4):
                u_hi(0, k)
                if k == 2:
                    act.wait_ge(S["unit_used"], U0 + 2)
                    act.activation(gelu_t[:, 0, :], PS[:, 4, 0:TOK], ACT.Gelu).then_inc(S["gelu0"], 1)
            with act.Fori(1, BLOCKS // 2) as it:
                for k in range(4):
                    u_hi(it, k)
                    if k == 0:
                        act.wait_ge(S["unit_used"], it * 4 + U0)
                        act.wait_ge(S["gated0"], it)
                        act.activation(gelu_t[:, 1, :], PS[:, 5, 0:TOK], ACT.Gelu).then_inc(S["gelu1"], 1)
                    if k == 2:
                        act.wait_ge(S["unit_used"], it * 4 + (U0 + 2))
                        act.wait_ge(S["gated0"], it)
                        act.activation(gelu_t[:, 0, :], PS[:, 4, 0:TOK], ACT.Gelu).then_inc(S["gelu0"], 1)
            act.wait_ge(S["unit_used"], V0)
            act.wait_ge(S["gated1"], BLOCKS // 2 - 1)
            act.activation(gelu_t[:, 1, :], PS[:, 5, 0:TOK], ACT.Gelu).then_inc(S["gelu1"], 1)
            act.wait_ge(S["gated0"], BLOCKS // 2)
            act.wait_ge(S["gated1"], BLOCKS // 2)

            def v_hi(it, k):
                if k % 2 == 0:
                    b = k // 2
                    act.wait_ge(S["unit_used"], it * 4 + (V0 + k - 2))
                    act.activation(act_hi[:, b, :], big[:, ds(it * 2 + b, 1), :].rearrange("p a n -> p (a n)")
                                   if not isinstance(it, int) else big[:, 2 * it + b, :], ACT.Copy).then_inc(S["act2_hi"], 1)
                for hh in range(2):
                    hi(it + V0 // 4, k, hh, it * 4 + (V0 + k - 1))
            for k in range(4):
                v_hi(0, k)
            with act.Fori(1, BLOCKS // 2) as it:
                for k in range(4):
                    v_hi(it, k)
            act.wait_ge(S["res_done"], 2)
            norm_root([flat(Z(8 * tt, 8 * tt + 8)) for tt in range(2)], [flat(Z(40, 48)), flat(Z(48, 56))], 2)

        @block.gpsimd
        def _(pool):
            ch = Chain(pool, S["pool_chain"])
            QK = Z(0, 16).rearrange("p (a w) n -> p a w n", w=2)
            sinb = bc(cst[:, SIN:SIN + TOK], 8)
            pool.wait_ge(S["proj_evac"], 29)
            pool.wait_ge(S["const_in"], 16)
            pool.tensor_tensor(Z(66, 74), QK[:, :, 1, :], sinb, ALU.mult).then_inc(S["rot_sin"], 1)
            pool.tensor_tensor(Z(90, 98), QK[:, :, 0, :], sinb, ALU.mult).then_inc(S["rot_sin"], 1)
            pool.wait_ge(S["rot_cos"], 2)
            pool.wait_ge(S["rot_sin"], 2)
            pool.tensor_tensor(QK[:, :, 1, :], Z(74, 82), Z(90, 98), ALU.add).then_inc(S["rot_done"], 1)
            for h in range(2):
                pool.wait_ge(S["oret_pre"], 4 * h + 4)
                pool.wait_ge(S["silu"], 1)
                pool.wait_ge(S["sc_done"], 4)
                last = pool.tensor_tensor(Z(4 * h, 4 * h + 4), Z(66 + 4 * h, 70 + 4 * h), Z(24 + 4 * h, 28 + 4 * h), ALU.mult)
                last.then_inc(S["oret"], 1)

            z, d = Z(48, 58), Z(74, 84)
            pool.tensor_tensor(d[:, :, 1:TOK], z[:, :, 0:TOK - 1], z[:, :, 1:TOK], ALU.subtract)
            ch.link(pool.tensor_scalar(d[:, :, 0:1], z[:, :, 0:1], -1.0, None, ALU.mult))
            ch.link(pool.tensor_tensor(d, d, per_token("rwkv_mix", 16, 10), ALU.mult))
            pool.tensor_tensor(z, z, d, ALU.add).then_inc(S["mixB"], 1)
            pool.memset(Z(106, 114), 0.0).then_inc(S["d1_zero"], 1)
            pp = Z(114, 122).rearrange("p c (n t) -> p (c n) t", t=64)
            pool.memset(pp[:, :, 0:1], 1.0).then_inc(S["pprev1"], 1)
            pool.wait_ge(S["a_done"], 8)
            pool.wait_ge(S["mixA"], 1)
            for k in range(8):
                last = pool.tensor_scalar(big[:, 58 + k, :], big[:, 8 + k, :], 1.0, v1("rwkv_k_a", k), ALU.subtract, ALU.mult)
            last.then_inc(S["ka"], 1)
            pool.wait_ge(S["pre_done"], 1)
            eye = bc(ident, 4)

            def level(lv):
                return bc(cst[:, LEVEL + (lv - 1) * P:LEVEL + lv * P], 4)
            n0 = ch.n

            def pairs(i):
                ch.n, ch.offset = n0, i * 2
                for g in range(2):
                    wait_past(pool, S[f"y{g}"], i)
                    for src, dst in ((8, beta_bd), (98, kappa_bd), (48, v_bd), (24, alpha_bd)):
                        rows = big[:, ds(i * 2 + (src + g), 1), :].rearrange("p a (n t) -> p (a n) t", n=4)
                        last = pool.tensor_tensor(dst[g].rearrange("p n (h t) -> p n h t", h=2), bc(rows, 2, 2),
                                                  bc(bdmask.rearrange("p (h t) -> p h t", h=2), 4), ALU.mult)
                    last.then_inc(S[f"prep{g}"], 1)
                for g in range(2):
                    pool.wait_ge(S[f"s1e{g}"], i * 4 + 2)
                    ch.link(pool.tensor_tensor(Lm[g], B1[g][:, :, 0, :], level(1), ALU.mult))
                    pool.wait_ge(S[f"s2{g}"], i + 1)
                    pool.tensor_tensor(Xt[g], eye, Lm[g], ALU.subtract).then_inc(S[f"xt1{g}"], 1)
                for lv in range(2, 7):
                    for g in range(2):
                        if lv == 2:
                            pool.wait_ge(S[f"xt1{g}"], i + 1)
                        else:
                            pool.wait_ge(S[f"w{g}"], i * 5 + lv - 2)
                        pool.tensor_tensor(Lm[g], B1[g][:, :, 0, :], level(lv), ALU.mult).then_inc(S[f"lm{g}"], 1)
                assert ch.n == n0 + 2
            run_loop(pool, 0, 4, pairs)
            ch.offset, ch.n = 0, n0 + 8
            ch.link(pool.tensor_tensor(Z(32, 40), Z(32, 40), Z(40, 48), ALU.mult))
            pool.tensor_tensor(Z(32, 40), Z(32, 40), per_token("rwkv_r_k"), ALU.mult).then_inc(S["rk_done"], 1)

        @block.vector
        def _(dve):
            ch = Chain(dve, S["dve_chain"])
            link = ch.link

            def lo(m, slot, hh):
                dve.wait_ge(S["unit_hi"], m * 8 + 2 * slot + hh + 1)
                cols = slice(hh * 512, (hh + 1) * 512)
                dve.tensor_tensor(w_lo[:, slot % 2, cols], raw[:, slot, cols], w_hi[:, slot % 2, cols].bitcast(f32),
                                  ALU.subtract).then_inc(S["unit_split"], 1)

            def split_seg(name, evac=None):
                u0, g0, ng, ku, _ = SEG[name]

                def body(t, g, m, j):
                    for kq in range(ku):
                        slot = unit_slot(ku, j, kq)
                        for hh in range(2):
                            lo(m, slot, hh)
                        if kq == 1 and evac and not (isinstance(g, int) and g == 0):
                            dve.wait_ge(S["unit_used"], m * 4 + (2 * j if ku == 2 else 0))
                            evac(g - 1, (g0 + j + 1) % 2)
                seg_loop(dve, name, body)
                if evac:
                    dve.wait_ge(S["unit_used"], u0 + ng * ku)
                    evac(ng - 1, (g0 + ng - 1) % 2)

            def split_act(src, n):
                for pc in range(4):
                    dve.wait_ge(S["act_hi"], 4 * n + pc + 1)
                    dve.tensor_tensor(act_lo[:, 4 * pc:4 * pc + 4, :], src[:, 4 * pc:4 * pc + 4, :],
                                      act_hi[:, 4 * pc:4 * pc + 4, :].bitcast(f32), ALU.subtract).then_inc(S["act_split"], 1)

            def norm(nth):
                dve.wait_ge(S["norm_sum"], 2 * nth + 2)
                dve.tensor_scalar(ss, ss, 1.0 / DM, NORM_EPS, ALU.mult, ALU.add).then_inc(S["norm_mean"], 1)
                dve.wait_ge(S["norm_root"], nth + 1)
                dve.reciprocal(rstd, rstd).then_inc(S["norm_rstd"], 1)

            dve.wait_ge(S["vecT"], 1)
            dve.tensor_copy(vec[:, :], PS[:, 7, 0:NVEC]).then_inc(S["vec_done"], 1)
            dve.wait_ge(S["vec_done"], 1)
            norm(0)

            def to_channels(base, done, out_sem, weight):
                for gi in range(8):
                    tt, cg = gi // 4, gi % 4
                    dve.wait_ge(S[done], gi + 1)
                    w = vec[:, VEC[weight][0] + 4 * cg:VEC[weight][0] + 4 * cg + 4].unsqueeze(2).broadcast_to([P, 4, P])
                    dve.tensor_tensor(big[:, base + 4 * cg:base + 4 * cg + 4, tt * P:(tt + 1) * P],
                                      PS[:, gi, :].rearrange("p (c n) -> p c n", c=4), w, ALU.mult).then_inc(S[out_sem], 1)
            to_channels(58, "xT_done", "hT", "norm1_w")
            split_act(Z(58, 74), 0)
            split_seg("main")

            QK = Z(0, 16).rearrange("p (a w) n -> p a w n", w=2)
            cosb = bc(cst[:, COS:COS + TOK], 8)
            dve.wait_ge(S["proj_evac"], 29)
            dve.tensor_tensor(Z(58, 66), QK[:, :, 0, :], cosb, ALU.mult).then_inc(S["rot_cos"], 1)
            dve.tensor_tensor(Z(74, 82), QK[:, :, 1, :], cosb, ALU.mult).then_inc(S["rot_cos"], 1)
            dve.wait_ge(S["rot_cos"], 2)
            dve.wait_ge(S["rot_sin"], 2)
            dve.tensor_tensor(QK[:, :, 0, :], Z(58, 66), Z(66, 74), ALU.subtract).then_inc(S["rot_done"], 1)
            dve.wait_ge(S["decay_in"], 16)
            for h in range(HEADS):
                dve.wait_ge(S["sc_done"], h + 1)
                dve.tensor_tensor(Z(98 + 2 * h, 100 + 2 * h), half(4 + h), Z(82 + 2 * h, 84 + 2 * h), ALU.mult).then_inc(S["st_done"], 1)
            for h in range(HEADS):
                dve.wait_ge(S["o_done"], h + 1)
                for nt in range(2):
                    link(dve.bn_stats(bnst, half(h)[:, nt, :]))
                    link(dve.bn_aggr(mv[:, 2 * h + nt, :], bnst))
            dve.tensor_scalar(rs8, mv[:, :, 1], NORM_EPS, None, ALU.add).then_inc(S["on_var"], 1)
            dve.wait_ge(S["on_sqrt"], 1)
            link(dve.reciprocal(rs8, rs8))
            for k in range(8):
                dve.tensor_scalar(big[:, 58 + k, :], half(k // 2)[:, k % 2, :], mv[:, k, 0:1], rs8[:, k:k + 1], ALU.subtract,
                                  ALU.mult).then_inc(S["on_done"], 1)
            for k in range(8):
                dve.wait_ge(S["oT_done"], k // 2 + 1)
                dve.tensor_scalar(big[:, 66 + k, :], half(4 + k // 2)[:, k % 2, :], v1("ret_gn_w", k), v1("ret_gn_b", k),
                                  ALU.mult, ALU.add).then_inc(S["oret_pre"], 1)

            dve.wait_ge(S["oret"], 2)
            z, d = Z(32, 48), Z(58, 74)
            dve.tensor_tensor(d[:, :, 1:TOK], z[:, :, 0:TOK - 1], z[:, :, 1:TOK], ALU.subtract)
            link(dve.tensor_scalar(d[:, :, 0:1], z[:, :, 0:1], -1.0, None, ALU.mult))
            link(dve.tensor_tensor(d, d, per_token("rwkv_mix", 0, 16), ALU.mult))
            dve.tensor_tensor(z, z, d, ALU.add).then_inc(S["mixA"], 1)
            dve.wait_ge(S["mixA"], 1)
            kk, k_, a_ = Z(24, 32), Z(40, 48), Z(8, 16)
            link(dve.tensor_tensor(kk, k_, per_token("rwkv_k_k"), ALU.mult))
            dve.tensor_tensor(Z(16, 24), kk, kk, ALU.mult).then_inc(S["sq_done"], 1)
            dec = Z(90, 98).rearrange("p c (n t) -> p (c n) t", t=64)
            d1 = Z(106, 114).rearrange("p c (n t) -> p (c n) t", t=64)
            prod = Z(98, 106).rearrange("p c (n t) -> p (c n) t", t=64)
            dve.wait_ge(S["dec_done"], 1)
            dve.wait_ge(S["d1_zero"], 1)
            link(dve.tensor_copy(d1[:, :, 0:1], dec[:, :, 0:1]))
            link(dve.memset(dec[:, :, 0:1], 0.0))
            dve.tensor_tensor_scan(flat(Z(98, 106)), flat(Z(90, 98)), flat(Z(106, 114)), 0.0, ALU.mult, ALU.add).then_inc(S["scan_done"], 1)
            dve.wait_ge(S["scan_done"], 1)
            dve.tensor_copy(pend, prod[:, :, 63])
            dve.tensor_tensor(Z(90, 98), Z(98, 106), Z(32, 40), ALU.mult)
            link(dve.reciprocal(Z(106, 114), Z(98, 106)))
            dve.wait_ge(S["kn_read"], 1)
            link(dve.tensor_scalar(Z(16, 24), Z(16, 24), 1e-12, None, ALU.max))
            link(dve.reciprocal(Z(16, 24), Z(16, 24)))
            link(dve.tensor_tensor(kk, kk, Z(16, 24), ALU.mult))
            dve.wait_ge(S["ka"], 1)
            link(dve.scalar_tensor_tensor(flat(k_), flat(Z(58, 66)), 1.0, flat(k_), ALU.add, ALU.mult))
            link(dve.tensor_tensor(a_, a_, kk, ALU.mult))
            dve.tensor_tensor(a_, a_, Z(106, 114), ALU.mult)
            dve.wait_ge(S["pprev"], 1)
            dve.wait_ge(S["pprev1"], 1)
            dve.tensor_tensor(kk, kk, Z(114, 122), ALU.mult)
            dve.tensor_tensor(Z(98, 106), k_, Z(106, 114), ALU.mult).then_inc(S["pre_done"], 1)

            s1mask = bc(cst[:, S1MASK:S1MASK + 256], 2)
            eye4 = bc(ident, 4)
            dve.wait_ge(S["pre_done"], 1)
            with dve.Fori(0, 4) as i:
                for g in range(2):
                    dve.wait_ge(S[f"s1{g}"], i + 1)
                    for q, dst in enumerate((B1, B2)):
                        for n2 in range(2):
                            dve.tensor_tensor(dst[g][:, 2 * n2:2 * n2 + 2, :, :].rearrange("p n w c -> p n (w c)"),
                                              half(4 * g + 2 * q + n2), s1mask, ALU.mult).then_inc(S[f"s1e{g}"], 1)
                for g in range(2):
                    dve.wait_ge(S[f"s2{g}"], i + 1)
                    for w, dst in enumerate((Vn[g], AM[g][:, :, 0, :])):
                        dve.tensor_copy(dst, one(PS[:, 4 * g + w, :])).then_inc(S[f"va{g}"], 1)
                for lv in range(5):
                    for g in range(2):
                        dve.wait_ge(S[f"w{g}"], i * 5 + lv + 1)
                        dve.tensor_tensor(Wn[g], eye4, one(PS[:, 4 * g + 1, :]), ALU.subtract).then_inc(S[f"wn{g}"], 1)
                for g in range(2):
                    dve.wait_ge(S[f"f{g}"], i + 1)
                    dve.tensor_tensor(Lm[g], one(PS[:, 4 * g + 3, :]), eye4, ALU.add).then_inc(S[f"fe{g}"], 1)
                    pe4 = pend[:, ds(i * 8 + 4 * g, 4)].unsqueeze(2).broadcast_to([P, 4, P])
                    dve.tensor_tensor(B1[g][:, :, 0, :], one(PS[:, 4 * g, :]), pe4, ALU.mult).then_inc(S[f"fe{g}"], 1)
                    for h in range(2):
                        rows = slice(64 * h, 64 * h + 64)
                        dve.tensor_tensor(B2[g][rows, :, 0, 64 * h:64 * h + 64], one(PS[rows, 4 * g + 1, :])[:, :, 64 * h:64 * h + 64],
                                          big[rows, ds(i * 2 + (90 + g), 1), :].rearrange("p a (n t) -> p (a n) t", n=4),
                                          ALU.add).then_inc(S[f"fe{g}"], 1)
                for n in (1, 2):
                    for g in range(2):
                        dve.wait_ge(S[f"ch{g}"], i * 2 + n)
                        if n == 1:
                            dve.wait_ge(S[f"fe{g}"], i * 4 + 4)
                        dve.scalar_tensor_tensor(St[g][:, n - 1, :], PS[:, 4 * g + 3, n * P:(n + 1) * P],
                                                 pend[:, ds(i * 8 + (4 * g + n), 1)], B1[g][:, n, 0, :], ALU.mult,
                                                 ALU.add).then_inc(S[f"st{g}"], 1)
            y = flat(Z(114, 122)).rearrange("p (q n) -> p q n", q=4)
            q4 = lambda lo_: flat(Z(lo_, lo_ + 8)).rearrange("p (q n) -> p q n", q=4)
            dve.wait_ge(S["ym_done"], 1)
            dve.scalar_tensor_tensor(q4(58), PS[:, 0:4, :], -1.0 / 64, y, ALU.mult, ALU.add).then_inc(S["yc_done"], 1)
            dve.wait_ge(S["yv_done"], 1)
            dve.tensor_scalar(q4(74), PS[:, 4:8, :], 1.0 / 64, GN_EPS, ALU.mult, ALU.add).then_inc(S["yvar"], 1)
            dve.wait_ge(S["yvar"], 1)
            dve.wait_ge(S["ystd"], 1)
            link(dve.reciprocal(Z(74, 82), Z(74, 82)))
            link(dve.tensor_tensor(Z(58, 66), Z(58, 66), Z(74, 82), ALU.mult))
            for k in range(8):
                last = dve.tensor_scalar(big[:, 58 + k, :], big[:, 58 + k, :], v1("rwkv_ln_w", k), v1("rwkv_ln_b", k), ALU.mult, ALU.add)
            link(last)
            dve.wait_ge(S["bonus"], 1)
            dve.tensor_tensor(q4(66), PS[:, 0:4, :], q4(48), ALU.mult).then_inc(S["bonus_read"], 1)
            dve.wait_ge(S["bonus_read"], 1)
            link(dve.tensor_tensor(Z(58, 66), Z(58, 66), Z(66, 74), ALU.add))
            dve.wait_ge(S["gate_up"], 1)
            dve.tensor_tensor(q4(8), q4(58), PS[:, 4:8, :], ALU.mult).then_inc(S["orwkv"], 1)
            split_seg("gates")
            split_act(Z(0, 16), 1)

            def chunks2(g, base):
                return big[:, base + 2 * g:base + 2 * g + 2, :] if isinstance(g, int) else big[:, ds(g * 2 + base, 2), :]

            def evac_ret(g, par):
                dve.tensor_tensor(chunks2(g, 58), PS[:, 2 * par:2 * par + 2, 0:TOK], chunks2(g, 58), ALU.mult).then_inc(S["proj_evac"], 1)

            def evac_rwkv(g, par):
                dve.tensor_tensor(chunks2(g, 74), PS[:, 2 * par:2 * par + 2, 0:TOK], chunks2(g, 74), ALU.mult).then_inc(S["proj_evac"], 1)
            dve.wait_ge(S["proj_evac"], 45)
            split_seg("ret", evac_ret)
            split_seg("rwkv", evac_rwkv)
            dve.wait_ge(S["proj_evac"], 61)
            dve.tensor_tensor(Z(58, 74), Z(58, 74), Z(74, 90), ALU.add).then_inc(S["merged"], 1)
            split_act(Z(58, 74), 2)
            split_seg("out")
            dve.wait_ge(S["x_again"], 16)
            for gi in range(8):
                dve.wait_ge(S["dT_done"], gi + 1)
                cols = slice(gi * 512, (gi + 1) * 512)
                dve.tensor_tensor(flat(Z(90, 106))[:, cols], flat(Z(90, 106))[:, cols], PS[:, gi, :], ALU.add).then_inc(S["x1_done"], 1)
            norm(1)
            to_channels(16, "x2T_done", "h2T", "norm2_w")
            split_act(Z(16, 32), 3)
            split_seg("wq")

            NEG = -3.0e38
            dve.wait_ge(S["x1_out"], 16)
            for tt in range(2):
                v16 = flat(Z(72 + tt, 73 + tt)).rearrange("p (j k) -> p j k", k=16)
                i16 = flat(Z(74 + tt, 75 + tt)).bitcast(u32).rearrange("p (j k) -> p j k", k=16)
                i16f = flat(Z(76 + tt, 77 + tt)).rearrange("p (j k) -> p j k", k=16)
                top = big[:, 70 + tt, 0:P].rearrange("p (h k) -> p h k", k=16)
                tix = big[:, 78 + tt, 0:P].bitcast(u32).rearrange("p (h k) -> p h k", k=16)
                tmp_i = [big[:, 80 + tt, w * P:(w + 1) * P].bitcast(u32) for w in range(2)]
                tmp_f = [big[:, 82 + tt, w * P:(w + 1) * P] for w in range(2)]
                dve.wait_ge(S["sc_copied"], tt + 1)
                sc = SC[tt]

                def top16(src, n, vout, iout):
                    for r in range(2):
                        for j in range(n):
                            last = dve.max(vout[:, j, 8 * r:8 * r + 8], src[:, j, :])
                        link(last)
                        for j in range(n):
                            last = dve.max_index(iout[:, j, 8 * r:8 * r + 8], vout[:, j, 8 * r:8 * r + 8], src[:, j, :])
                        if r == 0:
                            for j in range(n):
                                last = dve.match_replace(src[:, j, :], vout[:, j, 0:8], src[:, j, :], NEG)
                        link(last)
                top16(sc, 16, v16, i16)
                link(dve.tensor_copy(i16f, i16))
                cand = flat(Z(84, 92)).rearrange("p (h i j) -> p h i j", h=8, i=16)
                vv = v16.rearrange("p (h w) k -> p h w k", w=2)
                link(dve.tensor_tensor(cand, vv[:, :, 0, :].unsqueeze(3).broadcast_to([P, 8, 16, 16]),
                                       vv[:, :, 1, :].unsqueeze(2).broadcast_to([P, 8, 16, 16]), ALU.add))
                top16(cand.rearrange("p h i j -> p h (i j)"), 8, top, tix)
                tflat = tix.rearrange("p h k -> p (h k)")
                dve.tensor_scalar(tmp_i[0], tflat, 4, None, ALU.logical_shift_right)
                link(dve.tensor_scalar(tmp_i[1], tflat, 15, None, ALU.bitwise_and))
                dve.tensor_copy(tmp_f[0], tmp_i[0])
                link(dve.tensor_copy(tmp_f[1], tmp_i[1]))
                ii = i16f.rearrange("p (h w) k -> p h w k", w=2)
                oh = flat(Z(92, 100)).rearrange("p (h k i) -> p h k i", h=8, k=16)
                for w in range(2):
                    link(dve.tensor_tensor(oh, tmp_f[w].rearrange("p (h k) -> p h k", h=8).unsqueeze(3).broadcast_to([P, 8, 16, 16]),
                                           iota[:, 0:16].unsqueeze(1).unsqueeze(1).broadcast_to([P, 8, 16, 16]), ALU.is_equal))
                    link(dve.tensor_tensor(oh, oh, ii[:, :, w, :].unsqueeze(2).broadcast_to([P, 8, 16, 16]), ALU.mult))
                    link(dve.tensor_reduce(big[:, 66 + 2 * w + tt, 0:P].rearrange("p (h k) -> p h k", h=8), oh, AX.X, ALU.add))
                link(dve.tensor_copy(sums[:, 0:8], top[:, :, 0]))
                dve.tensor_tensor(top, top, sums[:, 0:8].unsqueeze(2).broadcast_to([P, 8, 16]), ALU.subtract).then_inc(S["topm"], 1)
                dve.wait_ge(S["gexp"], tt + 1)
                link(dve.tensor_reduce(sums[:, 0:8], top, AX.X, ALU.add))
                link(dve.reciprocal(sums[:, 0:8], sums[:, 0:8]))
                dve.tensor_tensor(top, top, sums[:, 0:8].unsqueeze(2).broadcast_to([P, 8, 16]), ALU.mult).then_inc(S["picked"], 1)
            dve.wait_ge(S["egT"], 1)
            dve.tensor_copy(eg[:, 0:2, :], half(0)).then_inc(S["eg_done"], 1)
            dve.tensor_copy(eg[:, 2, :], PS[:, 1, 0:256]).then_inc(S["eg_done"], 1)
            dve.wait_ge(S["eg_done"], 2)
            def tokens(i):
                for s in range(2):
                    wait_past(dve, S[f"g_mm{s}"], i)
                    dve.tensor_tensor(hotB[s], bc(iota, 4), bc(eg[:, 1, ds(i * 8 + 4 * s, 4)], P, 2), ALU.is_equal)
                    for t in range(4):
                        last = dve.tensor_scalar(hotA[:, 4 * s + t, :], iota, eg[:, 0, ds(i * 8 + (4 * s + t), 1)],
                                                 eg[:, 2, ds(i * 8 + (4 * s + t), 1)], ALU.is_equal, ALU.mult)
                    last.then_inc(S[f"hot{s}"], 1)
            run_loop(dve, 0, 32, tokens)

            def u_lo(it, k):
                for hh in range(2):
                    dve.wait_ge(S["unit_hi"], it * 8 + (2 * (U0 + k) + hh + 1))
                    cols = slice(hh * 512, (hh + 1) * 512)
                    dve.tensor_tensor(w_lo[:, k % 2, cols], PS[:, 2 * (k % 2) + hh, :], w_hi[:, k % 2, cols].bitcast(f32),
                                      ALU.subtract).then_inc(S["unit_split"], 1)

            def gate(it, b):
                dve.wait_ge(S[f"gelu{b}"], it + 1)
                g = big[:, 2 * it + b, :] if isinstance(it, int) else big[:, ds(it * 2 + b, 1), :].rearrange("p a n -> p (a n)")
                dve.tensor_tensor(g, g, gelu_t[:, b, :], ALU.mult).then_inc(S[f"gated{b}"], 1)
            for k in range(4):
                u_lo(0, k)
                if k == 2:
                    gate(0, 0)
            with dve.Fori(1, BLOCKS // 2) as it:
                for k in range(4):
                    u_lo(it, k)
                    if k == 0:
                        gate(it - 1, 1)
                    if k == 2:
                        gate(it, 0)
            gate(BLOCKS // 2 - 1, 1)

            def v_lo(it, k):
                if k % 2 == 0:
                    b = k // 2
                    g = big[:, 2 * it + b, :] if isinstance(it, int) else big[:, ds(it * 2 + b, 1), :].rearrange("p a n -> p (a n)")
                    dve.wait_ge(S["act2_hi"], it * 2 + b + 1)
                    dve.tensor_tensor(act_lo[:, b, :], g, act_hi[:, b, :].bitcast(f32), ALU.subtract).then_inc(S["act2_split"], 1)
                for hh in range(2):
                    lo(it + V0 // 4, k, hh)
            for k in range(4):
                v_lo(0, k)
            with dve.Fori(1, BLOCKS // 2) as it:
                for k in range(4):
                    v_lo(it, k)
            dve.wait_ge(S["x1_in"], 16)
            dve.wait_ge(S["unit_used"], V0 + 2 * BLOCKS)
            for tt in range(2):
                x1 = flat(Z(8 * tt, 8 * tt + 8)).rearrange("p (q n) -> p q n", q=4)
                dve.tensor_tensor(x1, x1, PS[:, 4 * tt:4 * tt + 4, :], ALU.add).then_inc(S["res_done"], 1)
            norm(2)
            dve.wait_ge(S["norm_rstd"], 3)
            dve.wait_ge(S["fw_in"], 16)
            for tt in range(2):
                dve.scalar_tensor_tensor(flat(Z(24 + 8 * tt, 32 + 8 * tt)), flat(Z(8 * tt, 8 * tt + 8)), rstd[:, tt:tt + 1],
                                         flat(Z(16, 24)), ALU.mult, ALU.mult).then_inc(S["y_ready"], 1)


def shape_constants():
    c = np.zeros((P, NCONST), np.float32)
    i = np.arange(P)
    c[:, IDENT:IDENT + P] = np.eye(P)
    c[:, IOTA:IOTA + P] = i[None, :]
    head, s = i // 64, i % 64
    same = head[:, None] == head[None, :]
    before = s[:, None] < s[None, :]
    c[:, S1MASK:S1MASK + P] = same & before
    c[:, S1MASK + P:S1MASK + 2 * P] = same & (before | (s[:, None] == s[None, :]))
    c[:, BDMASK:BDMASK + P] = same
    for lv in range(1, 7):
        whole = (s[:, None] >> lv) == (s[None, :] >> lv)
        parts = (s[:, None] >> (lv - 1)) != (s[None, :] >> (lv - 1))
        c[:, LEVEL + (lv - 1) * P:LEVEL + lv * P] = same & before & whole & parts
    c[:, ONES:ONES + P] = same
    t = np.arange(TOK)
    inv_freq = np.float32(10000.0) ** (-np.arange(P, dtype=np.float32) * np.float32(2.0) / np.float32(256))
    ang = t.astype(np.float32)[None, :] * inv_freq[:, None].astype(np.float32)
    c[:, COS:COS + TOK] = np.cos(ang)
    c[:, SIN:SIN + TOK] = np.sin(ang)
    m, n = t[:, None], t[None, :]
    decay = np.zeros((P, HEADS, 2, TOK), np.float32)
    for h in range(HEADS):
        log_g = np.log(1.0 - 2.0 ** (-5.0 - h))
        w = np.where((m // 64 == n // 64) | (m < n), np.exp(log_g * np.abs(n - m)), 0.0) / 16.0
        decay[:, h] = w.reshape(2, P, TOK).transpose(1, 0, 2)
    return c, decay.reshape(P, -1)


_INS = ["x", "norm1_w", "w_in", "ret_gn_w", "ret_gn_b", "rwkv_mix", "rwkv_w0", "rwkv_w_up", "rwkv_a0", "rwkv_a_up",
        "rwkv_g_up", "rwkv_k_k", "rwkv_k_a", "rwkv_r_k", "rwkv_ln_w", "rwkv_ln_b", "w_ret_branch", "w_rwkv_branch",
        "w_out", "norm2_w", "peer_w_q", "peer_keys_1", "peer_keys_2", "peer_u", "peer_v", "final_norm_w"]


def kernel(**inputs):
    import numpy as _np
    import concourse.bacc as _bacc
    from concourse import mybir as _mybir
    from concourse.bass_utils import run_bass_kernel_spmd as _run

    nc = _bacc.Bacc("TRN2", target_bir_lowering=False, num_devices=1)
    arrays, args = {}, {}
    for name in _INS:
        arrays[f"in_{name}"] = _np.ascontiguousarray(inputs[name])
    arrays["in_consts"], arrays["in_ret_decay"] = shape_constants()
    for key, v in arrays.items():
        args[key[3:]] = nc.dram_tensor(key, v.shape, _mybir.dt.from_np(v.dtype), kind="ExternalInput").ap()
    args["out"] = nc.dram_tensor("out_0", (1, TOK, DM), _mybir.dt.float32, kind="ExternalOutput").ap()
    hybrid_block_kernel(nc, args)
    r = _run(nc, [arrays], core_ids=[0])
    return r.results[0]["out_0"]
```

```python
import numpy as np
import concourse.bass as bass
from concourse import mybir
from contextlib import ExitStack

P = 128
TOK = 256
DM = 2048
KC = DM // P
HEADS = 4
NE = 16384
BLOCKS = NE // P
TOPK = 16
NORM_EPS = 1e-6
GN_EPS = 64e-5

IDENT, IOTA, S1MASK, BDMASK, LEVEL, ONES, COS, SIN = 0, 128, 256, 512, 640, 1408, 1536, 1792
NCONST = 2048

VEC_ROWS = [("norm1_w", 16), ("rwkv_mix", 26), ("ret_gn_w", 8), ("ret_gn_b", 8), ("rwkv_w0", 8), ("rwkv_a0", 8),
            ("rwkv_k_k", 8), ("rwkv_k_a", 8), ("rwkv_r_k", 8), ("rwkv_ln_w", 8), ("rwkv_ln_b", 8)]
VEC = {}
_at = 0
for _name, _rows in VEC_ROWS:
    VEC[_name] = (_at, _rows)
    _at += _rows
VROWS = _at
VEC["norm2_w"] = (VROWS, 16)
NVEC = VROWS + 16

SEG = {"main_rwkv": (0, 0, 13, 4, 0), "main_ret": (52, 13, 16, 4, 0), "gates": (116, 29, 16, 4, 0), "ret": (180, 45, 8, 2, 0), "rwkv": (196, 53, 8, 2, 8),
       "out": (212, 61, 8, 4, 0), "wq": (244, 69, 8, 4, 0)}
U0, V0 = 276, 532
PREP_MIX, PREP_LORA_IN, PREP_LORA_W, PREP_DECAY, PREP_EXP, PREP_LORA_A, PREP_A = 3, 12, 14, 16, 20, 21, 23
PREP_SCAN, PREP_KN, PREP_SHIFT, PREP_ROOT = 23, 28, 29, 31
EXP_AT, PICKED_AT, GATE_AT = 13, 16, 48
GATE_PARTS = ((0, 96), (96, 128))
GATE_BASE = (0, 32)
GATE_STEPS = (4, 8)
V_TURN = 3


class Chain:

    def __init__(self, eng, sem):
        self.eng, self.sem, self.n, self.offset = eng, sem, 0, 0

    def link(self, ins):
        self.n += 1
        ins.then_inc(self.sem, 1)
        self.eng.wait_ge(self.sem, self.offset + self.n)


def run_loop(eng, first, count, body, unrolled=False):
    if unrolled:
        for i in range(first, count):
            body(i)
        return
    body(first)
    with eng.Fori(first + 1, count) as i:
        body(i)


def wait_past(eng, sem, value):
    if not (isinstance(value, int) and value <= 0):
        eng.wait_ge(sem, value)


def hybrid_block_kernel(nc, a):
    f32, f32r, u32 = mybir.dt.float32, mybir.dt.float32r, mybir.dt.uint32
    ALU, ACT, AX = mybir.AluOpType, mybir.ActivationFunctionType, mybir.AxisListType
    ds = bass.ds
    ctx = ExitStack()
    with ctx:
        def sb(name, shape, dt=f32):
            return ctx.enter_context(nc.sbuf_tensor(name, shape, dt))

        class Sems(dict):
            def __missing__(self, name):
                self[name] = ctx.enter_context(nc.semaphore("s_" + name))
                return self[name]

        S = Sems()

        big = sb("big", [P, P, TOK])
        act_hi = sb("act_hi", [P, KC, TOK], f32r)
        act_lo = sb("act_lo", [P, KC, TOK], f32r)
        raw = sb("raw", [P, 4, 1024])
        w_hi = sb("w_hi", [P, 2, 1024], f32r)
        w_lo = sb("w_lo", [P, 2, 1024], f32r)
        cst = sb("cst", [P, NCONST])
        vec = sb("vec", [P, NVEC])
        extra = sb("extra", [P, 1024])
        onehot2 = sb("onehot2", [P, 512])
        small = sb("small", [P, 96])
        PS = ctx.enter_context(nc.psum_tensor("PS", [P, 8, 512], f32))
        x1_dram = nc.dram_tensor("x1_scratch", [TOK, DM], f32, kind="Internal").ap()

        ident = cst[:, IDENT:IDENT + P]
        iota = cst[:, IOTA:IOTA + P]
        bdmask = cst[:, BDMASK:BDMASK + P]
        ones_bd = cst[:, ONES:ONES + P]

        def Z(lo, hi):
            return big[:, lo:hi, :]

        def flat(ap):
            return ap.rearrange("p c n -> p (c n)")

        def half(k):
            return PS[:, k, :].rearrange("p (j n) -> p j n", j=2)

        def per_token(name, lo=0, n=None):
            at, rows = VEC[name]
            n = rows if n is None else n
            return vec[:, at + lo:at + lo + n].unsqueeze(2).broadcast_to([P, n, TOK])

        def v1(name, k):
            return vec[:, VEC[name][0] + k:VEC[name][0] + k + 1]

        def bc(ap, n, axis=1):
            b = ap.unsqueeze(axis)
            shape = list(b.shape)
            shape[axis] = n
            return b.broadcast_to(shape)

        ss, rstd = small[:, 0:2], small[:, 2:4]
        bnst = small[:, 4:10]
        mv = small[:, 10:26].rearrange("p (k c) -> p k c", c=2)
        rs8 = small[:, 26:34]
        pend = small[:, 34:66]
        sums = small[:, 66:82]

        r1 = flat(Z(58, 90))
        r2 = flat(Z(16, 24))
        r3 = flat(Z(24, 32))
        r4 = flat(Z(126, 128))
        place = [
            dict(B1=r1[:, 0:1024], B2=r1[:, 1024:2048], AM=r1[:, 2048:3072], XW=r1[:, 3072:4096], V=r1[:, 4096:4608],
                 Xt=r1[:, 4608:5120], bn=r1[:, 5120:5632], kn=r1[:, 5632:6144], Lm=r1[:, 6144:6656], S=extra[:, 512:768]),
            dict(B1=r1[:, 6656:7680], V=r1[:, 7680:8192], B2=r2[:, 0:1024], AM=r2[:, 1024:2048], XW=r3[:, 0:1024],
                 Xt=r3[:, 1024:1536], bn=r3[:, 1536:2048], kn=r4, Lm=extra[:, 0:512], S=extra[:, 768:1024]),
        ]

        def two(ap):
            return ap.rearrange("p (n w c) -> p n w c", n=4, w=2)

        def one(ap):
            return ap.rearrange("p (n c) -> p n c", n=4)

        B1 = [two(d["B1"]) for d in place]
        B2 = [two(d["B2"]) for d in place]
        AM = [two(d["AM"]) for d in place]
        AS = [two(d["XW"]) for d in place]
        X = [one(d["XW"][:, 0:512]) for d in place]
        Wn = [one(d["XW"][:, 512:1024]) for d in place]
        beta_bd, kappa_bd = X, Wn
        Vn = [one(d["V"]) for d in place]
        Xt = [one(d["Xt"]) for d in place]
        v_bd = Xt
        alpha_bd = [AM[g][:, :, 1, :] for g in range(2)]
        bn_ = [one(d["bn"]) for d in place]
        kn_ = [one(d["kn"]) for d in place]
        Lm = [one(d["Lm"]) for d in place]
        St = [d["S"].rearrange("p (n c) -> p n c", n=2) for d in place]

        keysT = flat(Z(49, 50))
        SC = [flat(Z(50 + 8 * t, 58 + 8 * t)).rearrange("p (j k) -> p j k", k=P) for t in range(2)]
        eg = extra[:, 0:768].rearrange("p (w n) -> p w n", w=3)
        hotA = cst[:, S1MASK:S1MASK + 1024].rearrange("p (n e) -> p n e", n=8)
        hotB = [cst[:, S1MASK + 1024:S1MASK + 1536].rearrange("p (n e) -> p n e", n=4),
                onehot2[:, :].rearrange("p (n e) -> p n e", n=4)]

        block = ctx.enter_context(nc.Block())

        def seg_loop(eng, name, body, unrolled=False):
            u0, g0, ng, ku, _ = SEG[name]

            def pair(t, count=2):
                for j in range(count):
                    body(t, t * 2 + j, t * (ku // 2) + u0 // 4 + (j if ku == 4 else 0), j)
            run_loop(eng, 0, ng // 2, pair, unrolled)
            if ng % 2:
                pair(ng // 2, 1)

        def unit_slot(ku, j, kq):
            return kq if ku == 4 else 2 * j + kq

        @block.sync
        def _(sp):
            sp.dma_start(flat(Z(90, 106)).rearrange("p (a n) -> p a n", a=2),
                         a["x"][0].rearrange("(a p) n -> p a n", p=P)).then_inc(S["x_in"], 16)
            at = 0
            for name, rows in VEC_ROWS:
                src = a[name].rearrange("l h w -> (l h w)") if name == "rwkv_r_k" else a[name].rearrange("l n -> (l n)")
                sp.dma_start(flat(Z(122, 123))[at:at + rows, 0:P], src.rearrange("(r c) -> r c", c=P)).then_inc(S["rows_in"], 16)
                at += rows
            sp.dma_start(flat(Z(122, 123))[0:16, P:2 * P],
                         a["norm2_w"].rearrange("l n -> (l n)").rearrange("(r c) -> r c", c=P)).then_inc(S["rows_in"], 16)
            sp.dma_start(cst[:, :], a["consts"]).then_inc(S["const_in"], 16)

            def load_seg(name, weight, col0):
                _, g0, _, ku, _ = SEG[name]
                w = weight.rearrange("(c p) n -> p c n", p=P)

                def body(t, g, m, j):
                    for kq in range(ku):
                        slot = unit_slot(ku, j, kq)
                        if not (name == "main_rwkv" and isinstance(t, int) and t == 0 and j == 0):
                            sp.wait_ge(S["unit_split"], m * 8 + 2 * slot - 6)
                        sp.dma_start(raw[:, slot, :].rearrange("p (c n) -> p c n", c=4),
                                     w[:, 4 * kq:4 * kq + 4, ds(g * 256 + col0, 256)]).then_inc(S[f"raw_in{slot}"], 16)
                seg_loop(sp, name, body)

            w_in = a["w_in"][0]
            load_seg("main_rwkv", w_in, 32 * P)
            sp.wait_ge(S["vecT"], 1)
            sp.dma_start(flat(Z(122, 126))[0:64, :], a["rwkv_w_up"][0]).then_inc(S["up_in"], 16)
            sp.dma_start(flat(Z(122, 126))[64:128, :], a["rwkv_a_up"][0]).then_inc(S["up_in"], 16)
            load_seg("main_ret", w_in, 0)
            sp.wait_ge(S["lora_a"], 4)
            sp.dma_start(flat(Z(122, 126)), a["rwkv_g_up"][0]).then_inc(S["gup_in"], 16)
            sp.wait_ge(S["rot_done"], 2)
            sp.dma_start(flat(Z(82, 90)), a["ret_decay"]).then_inc(S["decay_in"], 16)
            load_seg("gates", w_in, 58 * P)
            load_seg("ret", a["w_ret_branch"][0], 0)
            load_seg("rwkv", a["w_rwkv_branch"][0], 0)
            load_seg("out", a["w_out"][0], 0)
            sp.wait_ge(S["merged"], 1)
            sp.dma_start(flat(Z(90, 106)).rearrange("p (a n) -> p a n", a=2),
                         a["x"][0].rearrange("(a p) n -> p a n", p=P)).then_inc(S["x_again"], 16)
            sp.dma_start(flat(Z(48, 49))[:, 0:P], a["peer_keys_1"][0]).then_inc(S["keys_in"], 16)
            sp.dma_start(flat(Z(48, 49))[:, P:2 * P], a["peer_keys_2"][0]).then_inc(S["keys_in"], 16)
            load_seg("wq", a["peer_w_q"][0], 0)
            sp.wait_ge(S["x1_done"], 8)                
            sp.dma_start(x1_dram.rearrange("(a p) n -> p a n", p=P),
                         flat(Z(90, 106)).rearrange("p (a n) -> p a n", a=2)).then_inc(S["x1_out"], 16)
            u_rows = a["peer_u"][0].rearrange("(b e) n -> b e n", e=P)
            v_rows = a["peer_v"][0].rearrange("(b e) n -> b e n", e=P)

            def load_experts(rows, it, sem, value):
                for k in range(4):
                    sp.wait_ge(S[sem], value(k))
                    sp.dma_start(raw[:, k, :], rows[ds(it * 2 + k // 2, 1), :, (k % 2) * 1024:(k % 2 + 1) * 1024]
                                 .rearrange("a e n -> e (a n)")).then_inc(S[f"raw_in{k}"], 16)
            load_experts(u_rows, 0, "unit_split", lambda k: 2 * (U0 + k) - 6)
            with sp.Fori(1, BLOCKS // 2) as it:
                load_experts(u_rows, it, "uT_bank", lambda k: it * 8 + 2 * k - 6)
            for h in range(2):
                def load_v(it):
                    for k in range(4):
                        if h == 0 and isinstance(it, int):
                            sp.wait_ge(S["uT_bank"], 4 * BLOCKS + 2 * k - 6)
                        else:
                            sp.wait_ge(S["unit_split"], it * 8 + (2 * (V0 + h * BLOCKS + k) - 6))
                        sp.dma_start(raw[:, k, :], v_rows[ds(it * 4 + k, 1), :, h * 1024:(h + 1) * 1024]
                                     .rearrange("a e n -> e (a n)")).then_inc(S[f"raw_in{k}"], 16)
                run_loop(sp, 0, BLOCKS // 4, load_v)
            sp.wait_ge(S["half_used"], 2 * (V0 + BLOCKS + 60))
            sp.dma_start(flat(Z(0, 16)).rearrange("p (a n) -> p a n", a=2),
                         x1_dram.rearrange("(a p) n -> p a n", p=P)).then_inc(S["x1_in"], 16)
            sp.dma_start(flat(Z(16, 24)), a["final_norm_w"].partition_broadcast(P)).then_inc(S["fw_in"], 16)
            for tt in range(2):
                sp.wait_ge(S["y_ready"], tt + 1)
                sp.dma_start(a["out"][0, tt * P:(tt + 1) * P, :], flat(Z(24 + 8 * tt, 32 + 8 * tt))).then_inc(S["stored"], 16)
            sp.wait_ge(S["stored"], 32)

        @block.tensor
        def _(pe):
            def mm3(out, wh, wl, xh, xl, start, stop):
                pe.matmul(out, wh, xh, start=start, stop=False)
                pe.matmul(out, wh, xl, start=False, stop=False)
                return pe.matmul(out, wl, xh, start=False, stop=stop)

            def project(name, between=None):
                u0, g0, ng, ku, koff = SEG[name]

                def body(t, g, m, j):
                    par = (g0 + j) % 2
                    if not (name == "main_rwkv" and isinstance(t, int) and t == 0):
                        pe.wait_ge(S["proj_evac"], g + g0 - 1)
                    for kq in range(ku):
                        slot = unit_slot(ku, j, kq)
                        for hh in range(2):
                            pe.wait_ge(S["unit_split"], m * 8 + 2 * slot + hh + 1)
                            for c in (2 * hh, 2 * hh + 1):
                                kc = koff + 4 * kq + c
                                for jj in range(2):
                                    cols = slice(c * 256 + jj * P, c * 256 + (jj + 1) * P)
                                    last = mm3(PS[:, 2 * par + jj, 0:TOK], w_hi[:, slot % 2, cols], w_lo[:, slot % 2, cols],
                                               act_hi[:, kc, :], act_lo[:, kc, :],
                                               kq == 0 and c == 0, kq == ku - 1 and c == 3)
                            last.then_inc(S["half_used"], 1)
                        if between:
                            between(4 * g + kq)
                seg_loop(pe, name, body, between is not None)

            pe.wait_ge(S["const_in"], 16)
            pe.wait_ge(S["rows_in"], 16 * 12)
            pe.transpose(PS[:, 7, 0:VROWS], flat(Z(122, 123))[0:VROWS, 0:P], ident[0:VROWS, 0:VROWS])
            pe.transpose(PS[:, 7, VROWS:NVEC], flat(Z(122, 123))[0:16, P:2 * P], ident[0:16, 0:16]).then_inc(S["vecT"], 1)
            xn = [flat(Z(106 + 8 * t, 114 + 8 * t)) for t in range(2)]

            def transpose_tokens(src, done, bank7_free):
                for gi in range(8):
                    tt, cg = gi // 4, gi % 4
                    if gi == 7:
                        bank7_free()
                    for c in range(4):
                        col = (4 * cg + c) * P
                        last = pe.transpose(PS[:, gi, c * P:(c + 1) * P], src[tt][:, col:col + P], ident)
                    last.then_inc(S[done], 1)
            pe.wait_ge(S["normed"], 2)
            transpose_tokens(xn, "xT_done", lambda: pe.wait_ge(S["vec_done"], 1))

            pe.wait_ge(S["act_split"], 4)
            project("main_rwkv")

            up = flat(Z(122, 126))

            def rwkv_between(unit):
                if unit == PREP_LORA_W:
                    pe.wait_ge(S["up_in"], 32)
                    pe.wait_ge(S["lora_in"], 1)
                    for k in range(8):
                        last = pe.matmul(half(4 + k // 2)[:, k % 2, :], up[0:64, k * P:(k + 1) * P], big[0:64, 56, :],
                                         start=True, stop=True)
                        if k % 2:
                            last.then_inc(S["lora_w"], 1)
                if unit == PREP_LORA_A:
                    pe.wait_ge(S["sg_done"], 8)
                    for k in range(8):
                        last = pe.matmul(half(4 + k // 2)[:, k % 2, :], up[64:128, k * P:(k + 1) * P], big[64:128, 56, :],
                                         start=True, stop=True)
                        if k % 2:
                            last.then_inc(S["lora_a"], 1)
                if unit == PREP_KN:
                    pe.wait_ge(S["sq_done"], 2)
                    pe.wait_ge(S["a_done"], 8)
                    for q in range(4):
                        last = pe.matmul(PS[:, 4 + q, :], ones_bd, flat(Z(82 + 2 * q, 84 + 2 * q)), start=True, stop=True)
                    last.then_inc(S["kn_done"], 1)
            project("main_ret", rwkv_between)

            pe.wait_ge(S["proj_evac"], 29)
            for bank in range(4):
                tt, q = bank // 2, bank % 2
                for c in range(4):
                    last = pe.transpose(PS[:, bank, c * P:(c + 1) * P], big[:, 16 + 4 * q + c, tt * P:(tt + 1) * P], ident)
                last.then_inc(S["vT_done"], 1)
            pe.wait_ge(S["rot_done"], 2)
            pe.wait_ge(S["kn_read"], 2)
            for h in range(HEADS):
                for mt in range(2):
                    for kc in range(2):
                        last = pe.matmul(half(4 + h)[:, mt, :], big[:, 8 + 2 * h + kc, mt * P:(mt + 1) * P],
                                         big[:, 2 * h + kc, :], start=kc == 0, stop=kc == 1)
                last.then_inc(S["sc_done"], 1)
            sT = Z(66, 74).rearrange("p (h m) n -> p h m n", m=2)
            vtok = Z(74, 82).rearrange("p (m h) n -> p m h n", m=2)
            pe.wait_ge(S["vtok"], 4)
            for h in range(HEADS):
                pe.wait_ge(S["st_done"], h + 1)
                for nt in range(2):
                    for mt in range(2):
                        last = pe.matmul(half(h)[:, nt, :], sT[:, h, mt, nt * P:(nt + 1) * P], vtok[:, mt, h, :],
                                         start=mt == 0, stop=mt == 1)
                last.then_inc(S["o_done"], 1)
            pe.wait_ge(S["on_done"], 8)
            for h in range(HEADS):
                for ec in range(2):
                    for nt in range(2):
                        last = pe.transpose(PS[:, 4 + h, ec * 256 + nt * P:ec * 256 + (nt + 1) * P],
                                            big[:, 58 + 2 * h + nt, ec * P:(ec + 1) * P], ident)
                last.then_inc(S["oT_done"], 1)

            def pairs(i):
                for g in range(2):
                    b = 4 * g
                    pe.wait_ge(S[f"prep{g}"], i + 1)
                    wait_past(pe, S[f"ye{g}"], i * 2)
                    wait_past(pe, S[f"st{g}"], i * 2)
                    for q, lhs in enumerate((beta_bd, kappa_bd)):
                        for n in range(4):
                            for w, src in enumerate((114, 90)):
                                rhs = big[:, ds(i * 2 + (src + g), 1), n * 64:(n + 1) * 64].broadcast_to([P, 2, 64])
                                col = (n % 2) * 256 + w * P
                                last = pe.matmul(PS[:, b + 2 * q + n // 2, col:col + P], lhs[g][:, n, :], rhs, start=True, stop=True)
                    last.then_inc(S[f"s1{g}"], 1)
                for g in range(2):
                    b = 4 * g
                    pe.wait_ge(S[f"s1e{g}"], i * 4 + 4)
                    for w, src in enumerate((v_bd, alpha_bd, beta_bd, kappa_bd)):
                        for n in range(4):
                            last = pe.transpose(PS[:, b + w, n * P:(n + 1) * P], src[g][:, n, :], ident)
                    last.then_inc(S[f"s2{g}"], 1)
                for g in range(2):
                    b = 4 * g
                    pe.wait_ge(S[f"va{g}"], i * 2 + 2)
                    pe.wait_ge(S[f"xt1{g}"], i + 1)
                    for n in range(4):
                        last = pe.transpose(PS[:, b, n * P:(n + 1) * P], Xt[g][:, n, :], ident)
                    last.then_inc(S[f"xp{g}"], 1)
                for lv in range(5):
                    for g in range(2):
                        b = 4 * g
                        pe.wait_ge(S[f"lm{g}"], i * 5 + lv + 1)
                        if lv == 0:
                            pe.wait_ge(S[f"xc{g}"], i * 10 + 1)
                        else:
                            pe.wait_ge(S[f"xc{g}"], i * 10 + 2 * lv + 1)
                        for n in range(4):
                            last = pe.matmul(PS[:, b + 1, n * P:(n + 1) * P], Lm[g][:, n, :], X[g][:, n, :], start=True, stop=True)
                        last.then_inc(S[f"w{g}"], 1)
                    for g in range(2):
                        b = 4 * g
                        if lv == 0:
                            pe.wait_ge(S[f"bk{g}"], i * 2 + 2)
                        pe.wait_ge(S[f"wn{g}"], i * 5 + lv + 1)
                        if lv < 4:
                            for n in range(4):
                                pe.matmul(PS[:, b + 2, n * P:(n + 1) * P], Xt[g][:, n, :], Wn[g][:, n, :], start=True, stop=True)
                        for n in range(4):
                            last = pe.matmul(PS[:, b + 3, n * P:(n + 1) * P], Wn[g][:, n, :], Xt[g][:, n, :], start=True, stop=True)
                        last.then_inc(S[f"xx{g}"], 1)
                for g in range(2):
                    b = 4 * g
                    for n in range(4):
                        last = pe.matmul(PS[:, b, n * P:(n + 1) * P], B2[g][:, n, 0, :], Vn[g][:, n, :], start=True, stop=True)
                    last.then_inc(S[f"mv{g}"], 1)
                for g in range(2):
                    b = 4 * g
                    pe.wait_ge(S[f"xc{g}"], i * 10 + 10)
                    pe.wait_ge(S[f"mvc{g}"], i + 1)
                    for n in range(4):
                        last = pe.matmul(PS[:, b + 1 + n // 2, (n % 2) * 256:(n % 2 + 1) * 256], Xt[g][:, n, :],
                                         AM[g][:, n, :, :], start=True, stop=True)
                    last.then_inc(S[f"as{g}"], 1)
                for g in range(2):
                    b = 4 * g
                    pe.wait_ge(S[f"asc{g}"], i * 2 + 2)
                    for n in range(4):
                        cols = slice(n * P, (n + 1) * P)
                        pe.matmul(PS[:, b + 3, cols], AS[g][:, n, 0, :], bn_[g][:, n, :], start=True, stop=True)
                        pe.matmul(PS[:, b, cols], kn_[g][:, n, :], Vn[g][:, n, :], start=True, stop=False)
                        pe.matmul(PS[:, b, cols], bn_[g][:, n, :], AS[g][:, n, 1, :], start=False, stop=True)
                        last = pe.matmul(PS[:, b + 1, cols], AS[g][:, n, 0, :], B1[g][:, n, 1, :], start=True, stop=True)
                    last.then_inc(S[f"f{g}"], 1)

                def y_chunk(g, n, state):
                    out = PS[:, 4 * g + 2, n * P:(n + 1) * P]
                    if state is not None:
                        pe.matmul(out, state, B2[g][:, n, 0, :], start=True, stop=False)
                    pe.matmul(out, AS[g][:, n, 1, :], B1[g][:, n, 1, :], start=state is None, stop=False)
                    return pe.matmul(out, Vn[g][:, n, :], B2[g][:, n, 1, :], start=False, stop=True)
                for n in range(4):
                    for g in range(2):
                        state = [None, B1[g][:, 0, 0, :], St[g][:, 0, :], St[g][:, 1, :]][n]
                        if n == 0:
                            pe.wait_ge(S[f"fe{g}"], i * 4 + 4)
                        if n >= 2:
                            pe.wait_ge(S[f"st{g}"], i * 2 + n - 1)
                        if n in (1, 2):
                            pe.matmul(PS[:, 4 * g + 3, n * P:(n + 1) * P], Lm[g][:, n, :], state, start=True,
                                      stop=True).then_inc(S[f"ch{g}"], 1)
                        last = y_chunk(g, n, state)
                        if n == 3:
                            last.then_inc(S[f"y{g}"], 1)
            run_loop(pe, 0, 4, pairs)

            for g in range(2):
                pe.wait_ge(S[f"ye{g}"], 8)
                pe.wait_ge(S[f"st{g}"], 8)
            for q in range(4):
                last = pe.matmul(PS[:, q, :], ones_bd, flat(Z(114 + 2 * q, 116 + 2 * q)), start=True, stop=True)
            last.then_inc(S["ym_done"], 1)
            pe.wait_ge(S["ysq_done"], 1)
            for q in range(4):
                last = pe.matmul(PS[:, 4 + q, :], ones_bd, flat(Z(66 + 2 * q, 68 + 2 * q)), start=True, stop=True)
            last.then_inc(S["yv_done"], 1)
            pe.wait_ge(S["rk_done"], 1)
            pe.wait_ge(S["yc_done"], 1)
            for q in range(4):
                last = pe.matmul(PS[:, q, :], ones_bd, flat(Z(32 + 2 * q, 34 + 2 * q)), start=True, stop=True)
            last.then_inc(S["bonus"], 1)
            pe.wait_ge(S["gup_in"], 16)
            pe.wait_ge(S["yvar"], 1)
            gup = flat(Z(122, 126))
            for k in range(8):
                last = pe.matmul(half(4 + k // 2)[:, k % 2, :], gup[:, k * P:(k + 1) * P], big[:, 57, :], start=True, stop=True)
            last.then_inc(S["gate_up"], 1)
            pe.wait_ge(S["bonus_read"], 1)
            project("gates")
            pe.wait_ge(S["act_split"], 8)
            project("ret")
            project("rwkv")
            pe.wait_ge(S["act_split"], 12)
            project("out")
            pe.wait_ge(S["proj_evac"], 69)
            for gi in range(8):
                tt, cg = gi // 4, gi % 4
                for c in range(4):
                    last = pe.transpose(PS[:, gi, c * P:(c + 1) * P], big[:, 4 * cg + c, tt * P:(tt + 1) * P], ident)
                last.then_inc(S["dT_done"], 1)
            pe.wait_ge(S["normed"], 4)
            transpose_tokens(xn, "x2T_done", lambda: None)
            pe.wait_ge(S["keys_in"], 32)
            pe.wait_ge(S["h2T"], 8)
            for w in range(2):
                last = pe.transpose(PS[:, 7, w * P:(w + 1) * P], flat(Z(48, 49))[:, w * P:(w + 1) * P], ident)
            last.then_inc(S["kT_done"], 1)
            pe.wait_ge(S["act_split"], 16)
            project("wq")
            pe.wait_ge(S["proj_evac"], 77)
            pe.wait_ge(S["keysT"], 1)
            for tt in range(2):
                for q in range(4):
                    for c in range(4):
                        j = 4 * q + c
                        last = pe.matmul(PS[:, 4 * tt + q, c * P:(c + 1) * P], big[:, 32 + j, tt * P:(tt + 1) * P],
                                         keysT[:, (j % 2) * P:(j % 2 + 1) * P], start=True, stop=True)
                last.then_inc(S["s_done"], 1)

            def ut(it, k):
                pe.wait_ge(S[f"raw_in{k}"], it * 16 + 16 * (U0 // 4 + 1))
                for hh in range(2):
                    pe.wait_ge(S["unit_split"], it * 8 + (2 * (U0 + k) - 3 + hh))
                    for c in range(4):
                        last = pe.transpose(PS[:, 2 * (k % 2) + hh, c * P:(c + 1) * P],
                                            raw[:, k, (4 * hh + c) * P:(4 * hh + c + 1) * P], ident)
                    last.then_inc(S["uT_bank"], 1)

            def um(it, k):
                for hh in range(2):
                    pe.wait_ge(S["unit_split"], it * 8 + (2 * (U0 + k) + hh + 1))
                    if k % 2 == 0 and hh == 0:
                        wait_past(pe, S[f"gelu{k // 2}"], it)
                    for c in range(4):
                        kc = (k % 2) * 8 + 4 * hh + c
                        cols = slice((4 * hh + c) * P, (4 * hh + c + 1) * P)
                        last = mm3(PS[:, 4 + k // 2, 0:TOK], w_hi[:, k % 2, cols], w_lo[:, k % 2, cols],
                                   act_hi[:, kc, :], act_lo[:, kc, :], kc == 0, kc == 15)
                    last.then_inc(S["half_used"], 1)

            def gates_mm(i, k, part):
                par, seen = k % 2, i * (GATE_STEPS[part] // 2) + (GATE_BASE[part] + k // 2)
                lo_, hi_ = GATE_PARTS[part]
                pe.wait_ge(S[f"hot{par}"], seen + 1)
                wait_past(pe, S[f"gated{par}"], seen)
                for t in range(4):
                    last = pe.matmul(PS[:, 6 + par, t * P:t * P + hi_ - lo_], hotB[par][:, t, :], hotA[:, 4 * par + t, 0:hi_ - lo_],
                                     start=True, stop=True)
                last.then_inc(S[f"g_mm{par}"], 1)

            def u_blocks(it, gating=None, final=False):
                for k in range(4):
                    if k < 3:
                        ut(it, k + 1)
                    elif not final:
                        ut(it + 1, 0)
                    um(it, k)
                    if gating is not None:
                        gates_mm(gating, k, 0)
            pe.wait_ge(S["sc_copied"], 1)
            ut(0, 0)
            pe.wait_ge(S["sc_copied"], 2)
            run_loop(pe, 0, PICKED_AT, u_blocks)
            pe.wait_ge(S["picked"], 2)
            for w, src in enumerate((66, 68, 70)):
                for tt in range(2):
                    last = pe.transpose(PS[:, 6 + w // 2, (w % 2) * 256 + tt * P:(w % 2) * 256 + (tt + 1) * P],
                                        big[:, src + tt, 0:P], ident)
            last.then_inc(S["egT"], 1)
            with pe.Fori(PICKED_AT, GATE_AT) as it:
                u_blocks(it)
            pe.wait_ge(S["eg_done"], 2)
            u_blocks(GATE_AT, 0)
            with pe.Fori(1, 15) as i:
                u_blocks(i + GATE_AT, i)
            u_blocks(BLOCKS // 2 - 1, 15, True)

            pe.wait_ge(S["gelu0"], BLOCKS // 2)
            pe.wait_ge(S["gelu1"], BLOCKS // 2)

            def vm(h, it, k, start=False, stop=False):
                u = it * 8 + 2 * (V0 + h * BLOCKS + k)
                pe.wait_ge(S["act2_split"], it * 4 + (h * BLOCKS + k + 1))
                for hh in range(2):
                    pe.wait_ge(S["unit_split"], u + hh + 1)
                    for tt in range(2):
                        out = PS[:, 4 * h + 2 * tt + hh, :]
                        cols = slice(hh * 512, (hh + 1) * 512)
                        ah = act_hi[:, k % 2, tt * P:(tt + 1) * P]
                        al = act_lo[:, k % 2, tt * P:(tt + 1) * P]
                        pe.matmul(out, ah, w_hi[:, k % 2, cols], start=start, stop=False)
                        pe.matmul(out, ah, w_lo[:, k % 2, cols], start=False, stop=False)
                        last = pe.matmul(out, al, w_hi[:, k % 2, cols], start=False, stop=stop)
                    last.then_inc(S["half_used"], 1)
            for h in range(2):
                def v_blocks(it, first=False, final=False):
                    for k in range(4):
                        vm(h, it, k, first and k == 0, final and k == 3)

                def v_gating(i):
                    for u in range(4 * V_TURN):
                        vm(h, i * V_TURN + u // 4, u % 4, isinstance(i, int) and u == 0)
                        if u % 3 < 2:
                            gates_mm(i, u - u // 3, 1)
                if h == 0:
                    run_loop(pe, 0, 8, v_gating)
                else:
                    pe.wait_ge(S["gated0"], 64)
                    pe.wait_ge(S["gated1"], 64)
                    v_blocks(0, first=True)
                with pe.Fori(8 * V_TURN if h == 0 else 1, BLOCKS // 4 - 1) as it:
                    v_blocks(it)
                v_blocks(BLOCKS // 4 - 1, final=True)

        @block.scalar
        def _(act):
            ch = Chain(act, S["act_chain"])

            def hi(m, slot, hh, first=False):
                if hh == 0:
                    act.wait_ge(S[f"raw_in{slot}"], m * 16 + 16)
                if not first:
                    act.wait_ge(S["half_used"], m * 8 + (2 * slot - 3 + hh))
                act.activation(w_hi[:, slot % 2, hh * 512:(hh + 1) * 512], raw[:, slot, hh * 512:(hh + 1) * 512],
                               ACT.Copy).then_inc(S["unit_hi"], 1)

            def split_seg(name, evac=None, between=None):
                u0, g0, ng, ku, _ = SEG[name]

                def body(t, g, m, j):
                    for kq in range(ku):
                        slot = unit_slot(ku, j, kq)
                        first = name == "main_rwkv" and isinstance(t, int) and t == 0 and j == 0 and kq < 2
                        for hh in range(2):
                            hi(m, slot, hh, first)
                        if kq == 1 and evac and not (isinstance(g, int) and g == 0):
                            act.wait_ge(S["half_used"], m * 8 + (4 * j if ku == 2 else 0))
                            evac(g - 1, (g0 + j + 1) % 2)
                        if between:
                            between(4 * g + kq)
                seg_loop(act, name, body, between is not None)
                if evac and name != "main_rwkv":
                    act.wait_ge(S["half_used"], 2 * (u0 + ng * ku))
                    evac(ng - 1, (g0 + ng - 1) % 2)

            def split_act(src, n):
                for pc in range(4):
                    act.activation(act_hi[:, 4 * pc:4 * pc + 4, :], src[:, 4 * pc:4 * pc + 4, :], ACT.Copy).then_inc(S["act_hi"], 1)

            def norm_root(src, junk, nth):
                for tt in range(2):
                    act.activation(junk[tt], src[tt], ACT.Square, accum_out=ss[:, tt:tt + 1]).then_inc(S["norm_sum"], 1)
                act.wait_ge(S["norm_mean"], nth + 1)
                act.activation(rstd, ss, ACT.Sqrt).then_inc(S["norm_root"], 1)

            def norm(src, dst, nth):
                norm_root(src, dst, nth)
                act.wait_ge(S["norm_rstd"], nth + 1)
                for tt in range(2):
                    act.activation(dst[tt], src[tt], ACT.Copy, scale=rstd[:, tt:tt + 1]).then_inc(S["normed"], 1)

            xs = [flat(Z(90 + 8 * t, 98 + 8 * t)) for t in range(2)]
            xn = [flat(Z(106 + 8 * t, 114 + 8 * t)) for t in range(2)]
            act.wait_ge(S["x_in"], 16)
            norm(xs, xn, 0)
            act.wait_ge(S["hT"], 8)
            split_act(Z(58, 74), 0)

            def evac_copy(base):
                def evac(g, par):
                    act.activation(big[:, ds(g * 2 + base, 2), :] if not isinstance(g, int) else big[:, base + 2 * g:base + 2 * g + 2, :],
                                   PS[:, 2 * par:2 * par + 2, 0:TOK], ACT.Copy).then_inc(S["proj_evac"], 1)
                return evac

            def evac_sigmoid(base):
                def evac(g, par):
                    act.activation(big[:, ds(g * 2 + base, 2), :] if not isinstance(g, int) else big[:, base + 2 * g:base + 2 * g + 2, :],
                                   PS[:, 2 * par:2 * par + 2, 0:TOK], ACT.Sigmoid).then_inc(S["proj_evac"], 1)
                return evac
            split_seg("main_rwkv", evac_copy(32))

            pc = Z(98, 106).rearrange("p c (n t) -> p (c n) t", t=64)
            pp = Z(66, 74).rearrange("p c (n t) -> p (c n) t", t=64)

            def rwkv_between(unit):
                if unit == 1:
                    act.wait_ge(S["half_used"], 2 * SEG["main_ret"][0])
                    evac_copy(32)(SEG["main_rwkv"][2] - 1, 0)
                if unit == PREP_LORA_IN:
                    act.wait_ge(S["mixB"], 1)
                    act.activation(big[0:64, 56, :], big[0:64, 56, :], ACT.Tanh).then_inc(S["lora_in"], 1)
                    act.activation(Z(57, 58), Z(57, 58), ACT.Sigmoid).then_inc(S["xg_done"], 1)
                for start, name, done, dst, bias in ((PREP_DECAY, "lora_w", "sg_done", 90, "rwkv_w0"),
                                                     (PREP_A, "lora_a", "a_done", 74, "rwkv_a0")):
                    q = unit - start
                    if 0 <= q < 4:
                        act.wait_ge(S[name], q + 1)
                        for k in (2 * q, 2 * q + 1):
                            act.activation(big[:, dst + k, :], half(4 + q)[:, k % 2, :], ACT.Sigmoid, bias=v1(bias, k)).then_inc(S[done], 1)
                if unit == PREP_EXP:
                    act.wait_ge(S["sg_done"], 8)
                q = unit - PREP_EXP
                if 0 <= q < 2:
                    rows = Z(90 + 4 * q, 94 + 4 * q)
                    act.activation(rows, rows, ACT.Exp, scale=-float(np.exp(-0.5))).then_inc(S["dec_done"], 1)
                q = unit - PREP_SHIFT
                if 0 <= q < 2:
                    act.wait_ge(S["scan_done"], q + 1)
                    act.wait_ge(S["mixA"], 4)
                    act.activation(pp[:, 16 * q:16 * q + 16, 1:64], pc[:, 16 * q:16 * q + 16, 0:63], ACT.Copy).then_inc(S["pprev"], 1)
                q = unit - PREP_ROOT
                if 0 <= q < 2:
                    act.wait_ge(S["kn_done"], 1)
                    act.activation(flat(Z(82 + 4 * q, 86 + 4 * q)).rearrange("p (q n) -> p q n", q=2), PS[:, 4 + 2 * q:6 + 2 * q, :],
                                   ACT.Sqrt).then_inc(S["kn_read"], 1)
            split_seg("main_ret", evac_copy(0), rwkv_between)

            vtok = flat(Z(74, 82))
            act.wait_ge(S["rot_done"], 2)
            for bank in range(4):
                act.wait_ge(S["vT_done"], bank + 1)
                act.activation(vtok[:, bank * 512:(bank + 1) * 512], PS[:, bank, :], ACT.Copy).then_inc(S["vtok"], 1)
            act.wait_ge(S["proj_evac"], 29)
            act.activation(Z(24, 32), Z(24, 32), ACT.Silu).then_inc(S["silu"], 1)
            act.wait_ge(S["on_var"], 1)
            act.activation(rs8, rs8, ACT.Sqrt).then_inc(S["on_sqrt"], 1)

            with act.Fori(0, 4) as i:
                for g in range(2):
                    act.wait_ge(S[f"s2{g}"], i + 1)
                    for w, dst in enumerate((bn_, kn_)):
                        act.activation(dst[g], PS[:, 4 * g + 2 + w, :].rearrange("p (n c) -> p n c", n=4), ACT.Copy).then_inc(S[f"bk{g}"], 1)
                for g in range(2):
                    act.wait_ge(S[f"xp{g}"], i + 1)
                    act.activation(X[g], PS[:, 4 * g, :].rearrange("p (n c) -> p n c", n=4), ACT.Copy).then_inc(S[f"xc{g}"], 1)
                for lv in range(5):
                    for g in range(2):
                        act.wait_ge(S[f"xx{g}"], i * 5 + lv + 1)
                        if lv < 4:
                            act.activation(X[g], PS[:, 4 * g + 2, :].rearrange("p (n c) -> p n c", n=4), ACT.Copy).then_inc(S[f"xc{g}"], 1)
                        act.activation(Xt[g], PS[:, 4 * g + 3, :].rearrange("p (n c) -> p n c", n=4), ACT.Copy).then_inc(S[f"xc{g}"], 1)
                for g in range(2):
                    act.wait_ge(S[f"mv{g}"], i + 1)
                    act.activation(AM[g][:, :, 1, :], PS[:, 4 * g, :].rearrange("p (n c) -> p n c", n=4), ACT.Copy).then_inc(S[f"mvc{g}"], 1)
                for g in range(2):
                    act.wait_ge(S[f"as{g}"], i + 1)
                    for q in range(2):
                        act.activation(AS[g][:, 2 * q:2 * q + 2, :, :],
                                       PS[:, 4 * g + 1 + q, :].rearrange("p (n w c) -> p n w c", n=2, w=2), ACT.Copy,
                                       scale=-1.0).then_inc(S[f"asc{g}"], 1)
                for g in range(2):
                    act.wait_ge(S[f"y{g}"], i + 1)
                    for h in range(2):
                        rows = slice(64 * h, 64 * h + 64)
                        act.activation(big[rows, ds(i * 2 + (114 + g), 1), :].rearrange("p a (n t) -> p (a n) t", n=4),
                                       PS[rows, 4 * g + 2, :].rearrange("p (n w t) -> p n w t", n=4, w=2)[:, :, h, :],
                                       ACT.Copy).then_inc(S[f"ye{g}"], 1)
            act.wait_ge(S["yc_done"], 1)
            act.activation(Z(66, 74), Z(58, 66), ACT.Square).then_inc(S["ysq_done"], 1)
            act.wait_ge(S["yvar"], 1)
            act.activation(Z(74, 82), Z(74, 82), ACT.Sqrt).then_inc(S["ystd"], 1)
            act.wait_ge(S["orwkv"], 1)
            split_seg("gates", evac_sigmoid(58))
            act.wait_ge(S["orwkv"], 1)
            split_act(Z(0, 16), 1)
            split_seg("ret")
            split_seg("rwkv")
            act.wait_ge(S["half_used"], 2 * SEG["out"][0])
            act.wait_ge(S["merged"], 1)
            split_act(Z(58, 74), 2)
            split_seg("out", evac_copy(0))
            act.wait_ge(S["x1_done"], 8)
            norm(xs, xn, 1)
            act.wait_ge(S["h2T"], 8)
            split_act(Z(16, 32), 3)
            act.wait_ge(S["kT_done"], 1)
            act.activation(keysT, PS[:, 7, 0:256], ACT.Copy).then_inc(S["keysT"], 1)
            split_seg("wq", evac_copy(32))
            for tt in range(2):
                act.wait_ge(S["s_done"], tt + 1)
                act.activation(flat(Z(50 + 8 * tt, 58 + 8 * tt)).rearrange("p (q n) -> p q n", q=4), PS[:, 4 * tt:4 * tt + 4, :],
                               ACT.Copy).then_inc(S["sc_copied"], 1)

            def u_hi(it, k):
                for hh in range(2):
                    act.wait_ge(S["uT_bank"], it * 8 + (2 * k + hh + 1))
                    act.wait_ge(S["half_used"], it * 8 + (2 * (U0 + k) - 3 + hh))
                    act.activation(w_hi[:, k % 2, hh * 512:(hh + 1) * 512], PS[:, 2 * (k % 2) + hh, :], ACT.Copy).then_inc(S["unit_hi"], 1)

            def gelu(it, b):
                act.wait_ge(S["half_used"], it * 8 + (2 * U0 + 4 * b + 4))
                dst = big[:, 2 * it + b, :] if isinstance(it, int) else big[:, ds(it * 2 + b, 1), :].rearrange("p a n -> p (a n)")
                act.activation(dst, PS[:, 4 + b, 0:TOK], ACT.Gelu).then_inc(S[f"gelu{b}"], 1)

            def u_blocks(it):
                for k in range(4):
                    u_hi(it, k)
                    if k == 0 and not (isinstance(it, int) and it == 0):
                        gelu(it - 1, 1)
                    if k == 2:
                        gelu(it, 0)
            run_loop(act, 0, EXP_AT, u_blocks)
            for tt in range(2):
                act.wait_ge(S["topm"], tt + 1)
                act.activation(big[:, 70 + tt, 0:P], big[:, 70 + tt, 0:P], ACT.Exp).then_inc(S["gexp"], 1)
            with act.Fori(EXP_AT, PICKED_AT + 4) as it:
                u_blocks(it)
            act.wait_ge(S["eg_done"], 2)
            with act.Fori(PICKED_AT + 4, BLOCKS // 2) as it:
                u_blocks(it)
            gelu(BLOCKS // 2 - 1, 1)
            for h in range(2):
                def v_hi(it):
                    for k in range(4):
                        u = it * 4 + (V0 + h * BLOCKS + k)
                        act.wait_ge(S["half_used"], u * 2 - 2)
                        act.activation(act_hi[:, k % 2, :], big[:, 4 * it + k, :] if isinstance(it, int) else
                                       big[:, ds(it * 4 + k, 1), :].rearrange("p a n -> p (a n)"), ACT.Copy).then_inc(S["act2_hi"], 1)
                        for hh in range(2):
                            hi(it + (V0 + h * BLOCKS) // 4, k, hh)
                if h == 0:
                    act.wait_ge(S["gated0"], 32)
                    act.wait_ge(S["gated1"], 32)
                    run_loop(act, 0, GATE_PARTS[1][0] // 4, v_hi)
                    act.wait_ge(S["gated0"], 64)
                    act.wait_ge(S["gated1"], 64)
                    with act.Fori(GATE_PARTS[1][0] // 4, BLOCKS // 4) as it:
                        v_hi(it)
                else:
                    run_loop(act, 0, BLOCKS // 4, v_hi)
            act.wait_ge(S["res_done"], 4)
            norm_root([flat(Z(8 * tt, 8 * tt + 8)) for tt in range(2)], [flat(Z(40, 48)), flat(Z(48, 56))], 2)

        @block.gpsimd
        def _(pool):
            ch = Chain(pool, S["pool_chain"])
            z, d = Z(48, 58), Z(74, 84)
            pool.wait_ge(S["proj_evac"], 13)
            pool.tensor_tensor(d[:, :, 1:TOK], z[:, :, 0:TOK - 1], z[:, :, 1:TOK], ALU.subtract)
            ch.link(pool.tensor_scalar(d[:, :, 0:1], z[:, :, 0:1], -1.0, None, ALU.mult))
            ch.link(pool.tensor_tensor(d, d, per_token("rwkv_mix", 16, 10), ALU.mult))
            pool.tensor_tensor(z, z, d, ALU.add).then_inc(S["mixB"], 1)
            pool.memset(Z(106, 114), 0.0).then_inc(S["d1_zero"], 1)
            pool.wait_ge(S["mixA"], 4)
            pp = Z(66, 74).rearrange("p c (n t) -> p (c n) t", t=64)
            pool.memset(pp[:, :, 0:1], 1.0).then_inc(S["pprev1"], 1)
            pool.wait_ge(S["a_done"], 8)
            for k in range(8):
                last = pool.tensor_scalar(big[:, 58 + k, :], big[:, 74 + k, :], 1.0, v1("rwkv_k_a", k), ALU.subtract, ALU.mult)
            last.then_inc(S["ka"], 1)

            pool.wait_ge(S["pre_done"], 1)
            QK = Z(0, 16).rearrange("p (a w) n -> p a w n", w=2)
            sinb = bc(cst[:, SIN:SIN + TOK], 8)
            pool.wait_ge(S["proj_evac"], 29)
            pool.wait_ge(S["const_in"], 16)
            pool.tensor_tensor(Z(66, 74), QK[:, :, 1, :], sinb, ALU.mult).then_inc(S["rot_sin"], 1)
            pool.tensor_tensor(Z(82, 90), QK[:, :, 0, :], sinb, ALU.mult).then_inc(S["rot_sin"], 1)
            pool.wait_ge(S["rot_cos"], 2)
            pool.wait_ge(S["rot_sin"], 2)
            pool.tensor_tensor(QK[:, :, 1, :], Z(74, 82), Z(82, 90), ALU.add).then_inc(S["rot_done"], 1)
            for h in range(2):
                pool.wait_ge(S["oret_pre"], 4 * h + 4)
                pool.wait_ge(S["silu"], 1)
                pool.wait_ge(S["sc_done"], 4)
                last = pool.tensor_tensor(Z(4 * h, 4 * h + 4), Z(66 + 4 * h, 70 + 4 * h), Z(24 + 4 * h, 28 + 4 * h), ALU.mult)
                last.then_inc(S["oret"], 1)

            pool.wait_ge(S["oret"], 2)
            eye = bc(ident, 4)

            def level(lv):
                return bc(cst[:, LEVEL + (lv - 1) * P:LEVEL + lv * P], 4)
            n0 = ch.n

            def pairs(i):
                ch.n, ch.offset = n0, i * 2
                for g in range(2):
                    wait_past(pool, S[f"y{g}"], i)
                    for src, dst in ((106, beta_bd), (98, kappa_bd), (48, v_bd), (114, alpha_bd)):
                        rows = big[:, ds(i * 2 + (src + g), 1), :].rearrange("p a (n t) -> p (a n) t", n=4)
                        last = pool.tensor_tensor(dst[g].rearrange("p n (h t) -> p n h t", h=2), bc(rows, 2, 2),
                                                  bc(bdmask.rearrange("p (h t) -> p h t", h=2), 4), ALU.mult)
                    last.then_inc(S[f"prep{g}"], 1)
                for g in range(2):
                    pool.wait_ge(S[f"s1e{g}"], i * 4 + 2)
                    ch.link(pool.tensor_tensor(Lm[g], B1[g][:, :, 0, :], level(1), ALU.mult))
                    pool.wait_ge(S[f"s2{g}"], i + 1)
                    pool.tensor_tensor(Xt[g], eye, Lm[g], ALU.subtract).then_inc(S[f"xt1{g}"], 1)
                for lv in range(2, 7):
                    for g in range(2):
                        if lv == 2:
                            pool.wait_ge(S[f"xt1{g}"], i + 1)
                        else:
                            pool.wait_ge(S[f"w{g}"], i * 5 + lv - 2)
                        pool.tensor_tensor(Lm[g], B1[g][:, :, 0, :], level(lv), ALU.mult).then_inc(S[f"lm{g}"], 1)
                assert ch.n == n0 + 2
            run_loop(pool, 0, 4, pairs)
            ch.offset, ch.n = 0, n0 + 8
            ch.link(pool.tensor_tensor(Z(32, 40), Z(32, 40), Z(40, 48), ALU.mult))
            pool.tensor_tensor(Z(32, 40), Z(32, 40), per_token("rwkv_r_k"), ALU.mult).then_inc(S["rk_done"], 1)

        @block.vector
        def _(dve):
            ch = Chain(dve, S["dve_chain"])
            link = ch.link

            def lo(m, slot, hh):
                dve.wait_ge(S["unit_hi"], m * 8 + 2 * slot + hh + 1)
                cols = slice(hh * 512, (hh + 1) * 512)
                dve.tensor_tensor(w_lo[:, slot % 2, cols], raw[:, slot, cols], w_hi[:, slot % 2, cols].bitcast(f32),
                                  ALU.subtract).then_inc(S["unit_split"], 1)

            def split_seg(name, evac=None, between=None):
                u0, g0, ng, ku, _ = SEG[name]

                def body(t, g, m, j):
                    for kq in range(ku):
                        slot = unit_slot(ku, j, kq)
                        for hh in range(2):
                            lo(m, slot, hh)
                        if kq == 1 and evac and not (isinstance(g, int) and g == 0):
                            dve.wait_ge(S["half_used"], m * 8 + (4 * j if ku == 2 else 0))
                            evac(g - 1, (g0 + j + 1) % 2)
                        if between:
                            between(4 * g + kq)
                seg_loop(dve, name, body, between is not None)
                if evac:
                    dve.wait_ge(S["half_used"], 2 * (u0 + ng * ku))
                    evac(ng - 1, (g0 + ng - 1) % 2)

            def split_act(src, n):
                for pc in range(4):
                    dve.wait_ge(S["act_hi"], 4 * n + pc + 1)
                    dve.tensor_tensor(act_lo[:, 4 * pc:4 * pc + 4, :], src[:, 4 * pc:4 * pc + 4, :],
                                      act_hi[:, 4 * pc:4 * pc + 4, :].bitcast(f32), ALU.subtract).then_inc(S["act_split"], 1)

            def norm(nth):
                dve.wait_ge(S["norm_sum"], 2 * nth + 2)
                dve.tensor_scalar(ss, ss, 1.0 / DM, NORM_EPS, ALU.mult, ALU.add).then_inc(S["norm_mean"], 1)
                dve.wait_ge(S["norm_root"], nth + 1)
                dve.reciprocal(rstd, rstd).then_inc(S["norm_rstd"], 1)

            dve.wait_ge(S["vecT"], 1)
            dve.tensor_copy(vec[:, :], PS[:, 7, 0:NVEC]).then_inc(S["vec_done"], 1)
            dve.wait_ge(S["vec_done"], 1)
            norm(0)

            def to_channels(base, done, out_sem, weight):
                for gi in range(8):
                    tt, cg = gi // 4, gi % 4
                    dve.wait_ge(S[done], gi + 1)
                    w = vec[:, VEC[weight][0] + 4 * cg:VEC[weight][0] + 4 * cg + 4].unsqueeze(2).broadcast_to([P, 4, P])
                    dve.tensor_tensor(big[:, base + 4 * cg:base + 4 * cg + 4, tt * P:(tt + 1) * P],
                                      PS[:, gi, :].rearrange("p (c n) -> p c n", c=4), w, ALU.mult).then_inc(S[out_sem], 1)
            to_channels(58, "xT_done", "hT", "norm1_w")
            split_act(Z(58, 74), 0)
            split_seg("main_rwkv")

            def cut(lo_, n=4):
                return [Z(lo_ + q, lo_ + q + n) for q in range(0, 8, n)]

            def shift_steps():
                dve.wait_ge(S["proj_evac"], 13)
                for q in range(0, 16, 4):
                    z, d = Z(32 + q, 36 + q), Z(58 + q, 62 + q)
                    dve.tensor_tensor(d[:, :, 1:TOK], z[:, :, 0:TOK - 1], z[:, :, 1:TOK], ALU.subtract)
                    link(dve.tensor_scalar(d[:, :, 0:1], z[:, :, 0:1], -1.0, None, ALU.mult))
                    yield
                    link(dve.tensor_tensor(d, d, per_token("rwkv_mix", q, 4), ALU.mult))
                    yield
                    dve.tensor_tensor(z, z, d, ALU.add).then_inc(S["mixA"], 1)
                    yield
                dve.wait_ge(S["mixA"], 4)
                for q in range(2):
                    link(dve.tensor_tensor(cut(114)[q], cut(40)[q], per_token("rwkv_k_k", 4 * q, 4), ALU.mult))
                    yield
                dve.wait_ge(S["mixB"], 1)
                for q in range(2):
                    dve.tensor_tensor(cut(82)[q], cut(114)[q], cut(114)[q], ALU.mult).then_inc(S["sq_done"], 1)
                    yield

            def decay_steps():
                dec = Z(90, 98).rearrange("p c (n t) -> p (c n) t", t=64)
                d1 = Z(106, 114).rearrange("p c (n t) -> p (c n) t", t=64)
                prod = Z(98, 106).rearrange("p c (n t) -> p (c n) t", t=64)
                dve.wait_ge(S["dec_done"], 2)
                dve.wait_ge(S["d1_zero"], 1)
                link(dve.tensor_copy(d1[:, :, 0:1], dec[:, :, 0:1]))
                link(dve.memset(dec[:, :, 0:1], 0.0))
                for q in range(2):
                    dve.tensor_tensor_scan(flat(cut(98)[q]), flat(cut(90)[q]), flat(cut(106)[q]), 0.0, ALU.mult,
                                           ALU.add).then_inc(S["scan_done"], 1)
                    yield
                dve.wait_ge(S["scan_done"], 2)
                dve.tensor_copy(pend, prod[:, :, 63])
                for q in range(2):
                    dve.tensor_tensor(cut(90)[q], cut(98)[q], cut(32)[q], ALU.mult)
                    yield
                for q in range(8):
                    link(dve.reciprocal(cut(106, 1)[q], cut(98, 1)[q]))
                    yield
                dve.wait_ge(S["kn_read"], 2)
                for q in range(2):
                    link(dve.tensor_scalar(cut(82)[q], cut(82)[q], 1e-12, None, ALU.max))
                    yield
                for q in range(8):
                    link(dve.reciprocal(cut(82, 1)[q], cut(82, 1)[q]))
                    yield
                for q in range(2):
                    link(dve.tensor_tensor(cut(114)[q], cut(114)[q], cut(82)[q], ALU.mult))
                    yield
                dve.wait_ge(S["ka"], 1)
                for q in range(2):
                    link(dve.scalar_tensor_tensor(flat(cut(40)[q]), flat(cut(58)[q]), 1.0, flat(cut(40)[q]), ALU.add, ALU.mult))
                    yield
                for q in range(2):
                    link(dve.tensor_tensor(cut(74)[q], cut(74)[q], cut(114)[q], ALU.mult))
                    yield
                dve.wait_ge(S["pprev"], 2)
                dve.wait_ge(S["pprev1"], 1)
                for q in range(2):
                    link(dve.tensor_tensor(cut(98)[q], cut(40)[q], cut(106)[q], ALU.mult))
                    yield
                for q in range(2):
                    dve.tensor_tensor(cut(106)[q], cut(74)[q], cut(106)[q], ALU.mult)
                    yield
                for q in range(2):
                    last = dve.tensor_tensor(cut(114)[q], cut(114)[q], cut(66)[q], ALU.mult)
                    yield
                last.then_inc(S["pre_done"], 1)
            shift, decay = shift_steps(), decay_steps()

            def rwkv_between(unit):
                if unit >= PREP_MIX:
                    next(shift, None)
                if unit >= PREP_SCAN:
                    next(decay, None)
            split_seg("main_ret", None, rwkv_between)
            assert next(decay, "ended") == "ended" and next(shift, "ended") == "ended"

            QK = Z(0, 16).rearrange("p (a w) n -> p a w n", w=2)
            cosb = bc(cst[:, COS:COS + TOK], 8)
            dve.wait_ge(S["proj_evac"], 29)
            dve.tensor_tensor(Z(58, 66), QK[:, :, 0, :], cosb, ALU.mult).then_inc(S["rot_cos"], 1)
            dve.tensor_tensor(Z(74, 82), QK[:, :, 1, :], cosb, ALU.mult).then_inc(S["rot_cos"], 1)
            dve.wait_ge(S["rot_cos"], 2)
            dve.wait_ge(S["rot_sin"], 2)
            dve.tensor_tensor(QK[:, :, 0, :], Z(58, 66), Z(66, 74), ALU.subtract).then_inc(S["rot_done"], 1)
            dve.wait_ge(S["decay_in"], 16)
            for h in range(HEADS):
                dve.wait_ge(S["sc_done"], h + 1)
                dve.tensor_tensor(Z(66 + 2 * h, 68 + 2 * h), half(4 + h), Z(82 + 2 * h, 84 + 2 * h), ALU.mult).then_inc(S["st_done"], 1)
            for h in range(HEADS):
                dve.wait_ge(S["o_done"], h + 1)
                for nt in range(2):
                    link(dve.bn_stats(bnst, half(h)[:, nt, :]))
                    link(dve.bn_aggr(mv[:, 2 * h + nt, :], bnst))
            dve.tensor_scalar(rs8, mv[:, :, 1], NORM_EPS, None, ALU.add).then_inc(S["on_var"], 1)
            dve.wait_ge(S["on_sqrt"], 1)
            link(dve.reciprocal(rs8, rs8))
            for k in range(8):
                dve.tensor_scalar(big[:, 58 + k, :], half(k // 2)[:, k % 2, :], mv[:, k, 0:1], rs8[:, k:k + 1], ALU.subtract,
                                  ALU.mult).then_inc(S["on_done"], 1)
            for k in range(8):
                dve.wait_ge(S["oT_done"], k // 2 + 1)
                dve.tensor_scalar(big[:, 66 + k, :], half(4 + k // 2)[:, k % 2, :], v1("ret_gn_w", k), v1("ret_gn_b", k),
                                  ALU.mult, ALU.add).then_inc(S["oret_pre"], 1)

            s1mask = bc(cst[:, S1MASK:S1MASK + 256], 2)
            eye4 = bc(ident, 4)
            with dve.Fori(0, 4) as i:
                for g in range(2):
                    dve.wait_ge(S[f"s1{g}"], i + 1)
                    for q, dst in enumerate((B1, B2)):
                        for n2 in range(2):
                            dve.tensor_tensor(dst[g][:, 2 * n2:2 * n2 + 2, :, :].rearrange("p n w c -> p n (w c)"),
                                              half(4 * g + 2 * q + n2), s1mask, ALU.mult).then_inc(S[f"s1e{g}"], 1)
                for g in range(2):
                    dve.wait_ge(S[f"s2{g}"], i + 1)
                    for w, dst in enumerate((Vn[g], AM[g][:, :, 0, :])):
                        dve.tensor_copy(dst, one(PS[:, 4 * g + w, :])).then_inc(S[f"va{g}"], 1)
                for lv in range(5):
                    for g in range(2):
                        dve.wait_ge(S[f"w{g}"], i * 5 + lv + 1)
                        dve.tensor_tensor(Wn[g], eye4, one(PS[:, 4 * g + 1, :]), ALU.subtract).then_inc(S[f"wn{g}"], 1)
                for g in range(2):
                    dve.wait_ge(S[f"f{g}"], i + 1)
                    dve.tensor_tensor(Lm[g], one(PS[:, 4 * g + 3, :]), eye4, ALU.add).then_inc(S[f"fe{g}"], 1)
                    pe4 = pend[:, ds(i * 8 + 4 * g, 4)].unsqueeze(2).broadcast_to([P, 4, P])
                    dve.tensor_tensor(B1[g][:, :, 0, :], one(PS[:, 4 * g, :]), pe4, ALU.mult).then_inc(S[f"fe{g}"], 1)
                    for h in range(2):
                        rows = slice(64 * h, 64 * h + 64)
                        dve.tensor_tensor(B2[g][rows, :, 0, 64 * h:64 * h + 64], one(PS[rows, 4 * g + 1, :])[:, :, 64 * h:64 * h + 64],
                                          big[rows, ds(i * 2 + (90 + g), 1), :].rearrange("p a (n t) -> p (a n) t", n=4),
                                          ALU.add).then_inc(S[f"fe{g}"], 1)
                for n in (1, 2):
                    for g in range(2):
                        dve.wait_ge(S[f"ch{g}"], i * 2 + n)
                        if n == 1:
                            dve.wait_ge(S[f"fe{g}"], i * 4 + 4)
                        dve.scalar_tensor_tensor(St[g][:, n - 1, :], PS[:, 4 * g + 3, n * P:(n + 1) * P],
                                                 pend[:, ds(i * 8 + (4 * g + n), 1)], B1[g][:, n, 0, :], ALU.mult,
                                                 ALU.add).then_inc(S[f"st{g}"], 1)
            y = flat(Z(114, 122)).rearrange("p (q n) -> p q n", q=4)
            q4 = lambda lo_: flat(Z(lo_, lo_ + 8)).rearrange("p (q n) -> p q n", q=4)
            dve.wait_ge(S["ym_done"], 1)
            dve.scalar_tensor_tensor(q4(58), PS[:, 0:4, :], -1.0 / 64, y, ALU.mult, ALU.add).then_inc(S["yc_done"], 1)
            dve.wait_ge(S["yv_done"], 1)
            dve.tensor_scalar(q4(74), PS[:, 4:8, :], 1.0 / 64, GN_EPS, ALU.mult, ALU.add).then_inc(S["yvar"], 1)
            dve.wait_ge(S["yvar"], 1)
            dve.wait_ge(S["ystd"], 1)
            link(dve.reciprocal(Z(74, 82), Z(74, 82)))
            link(dve.tensor_tensor(Z(58, 66), Z(58, 66), Z(74, 82), ALU.mult))
            for k in range(8):
                last = dve.tensor_scalar(big[:, 58 + k, :], big[:, 58 + k, :], v1("rwkv_ln_w", k), v1("rwkv_ln_b", k), ALU.mult, ALU.add)
            link(last)
            dve.wait_ge(S["bonus"], 1)
            dve.tensor_tensor(q4(66), PS[:, 0:4, :], q4(48), ALU.mult).then_inc(S["bonus_read"], 1)
            dve.wait_ge(S["bonus_read"], 1)
            link(dve.tensor_tensor(Z(58, 66), Z(58, 66), Z(66, 74), ALU.add))
            dve.wait_ge(S["gate_up"], 1)
            dve.tensor_tensor(q4(8), q4(58), PS[:, 4:8, :], ALU.mult).then_inc(S["orwkv"], 1)
            split_seg("gates")
            split_act(Z(0, 16), 1)

            def chunks2(g, base):
                return big[:, base + 2 * g:base + 2 * g + 2, :] if isinstance(g, int) else big[:, ds(g * 2 + base, 2), :]

            def evac_ret(g, par):
                dve.tensor_tensor(chunks2(g, 58), PS[:, 2 * par:2 * par + 2, 0:TOK], chunks2(g, 58), ALU.mult).then_inc(S["proj_evac"], 1)

            def evac_rwkv(g, par):
                dve.tensor_tensor(chunks2(g, 74), PS[:, 2 * par:2 * par + 2, 0:TOK], chunks2(g, 74), ALU.mult).then_inc(S["proj_evac"], 1)
            dve.wait_ge(S["proj_evac"], 45)
            split_seg("ret", evac_ret)
            split_seg("rwkv", evac_rwkv)
            dve.wait_ge(S["proj_evac"], 61)
            dve.tensor_tensor(Z(58, 74), Z(58, 74), Z(74, 90), ALU.add).then_inc(S["merged"], 1)
            split_act(Z(58, 74), 2)
            split_seg("out")
            dve.wait_ge(S["x_again"], 16)
            for gi in range(8):
                dve.wait_ge(S["dT_done"], gi + 1)
                cols = slice(gi * 512, (gi + 1) * 512)
                dve.tensor_tensor(flat(Z(90, 106))[:, cols], flat(Z(90, 106))[:, cols], PS[:, gi, :], ALU.add).then_inc(S["x1_done"], 1)
            norm(1)
            to_channels(16, "x2T_done", "h2T", "norm2_w")
            split_act(Z(16, 32), 3)
            split_seg("wq")

            def places(tt):
                v16 = flat(Z(72 + tt, 73 + tt)).rearrange("p (j k) -> p j k", k=16)
                i16 = flat(Z(74 + tt, 75 + tt)).bitcast(u32).rearrange("p (j k) -> p j k", k=16)
                i16f = flat(Z(76 + tt, 77 + tt)).rearrange("p (j k) -> p j k", k=16)
                top = big[:, 70 + tt, 0:P].rearrange("p (h k) -> p h k", k=16)
                tix = big[:, 78 + tt, 0:P].bitcast(u32).rearrange("p (h k) -> p h k", k=16)
                return v16, i16, i16f, top, tix

            def top16(src, n, vout, iout):
                for r in range(2):
                    for j in range(n):
                        last = dve.max(vout[:, j, 8 * r:8 * r + 8], src[:, j, :])
                        if j % 8 == 7:
                            link(last)
                            yield
                    for j in range(n):
                        last = dve.max_index(iout[:, j, 8 * r:8 * r + 8], vout[:, j, 8 * r:8 * r + 8], src[:, j, :])
                        if j % 8 == 7:
                            link(last)
                            yield
                    for j in range(n if r == 0 else 0):
                        last = dve.match_replace(src[:, j, :], vout[:, j, 0:8], src[:, j, :], -3.0e38)
                        if j % 8 == 7:
                            link(last)
                            yield

            def pick_steps():
                dve.wait_ge(S["x1_out"], 16)
                for tt in range(2):
                    v16, i16, i16f, top, tix = places(tt)
                    tmp_i = [big[:, 80 + tt, w * P:(w + 1) * P].bitcast(u32) for w in range(2)]
                    tmp_f = [big[:, 82 + tt, w * P:(w + 1) * P] for w in range(2)]
                    dve.wait_ge(S["sc_copied"], tt + 1)
                    yield from top16(SC[tt], 16, v16, i16)
                    link(dve.tensor_copy(i16f, i16))
                    cand = flat(Z(84, 92)).rearrange("p (h i j) -> p h i j", h=8, i=16)
                    vv = v16.rearrange("p (h w) k -> p h w k", w=2)
                    link(dve.tensor_tensor(cand, vv[:, :, 0, :].unsqueeze(3).broadcast_to([P, 8, 16, 16]),
                                           vv[:, :, 1, :].unsqueeze(2).broadcast_to([P, 8, 16, 16]), ALU.add))
                    yield
                    yield from top16(cand.rearrange("p h i j -> p h (i j)"), 8, top, tix)
                    tflat = tix.rearrange("p h k -> p (h k)")
                    dve.tensor_scalar(tmp_i[0], tflat, 4, None, ALU.logical_shift_right)
                    link(dve.tensor_scalar(tmp_i[1], tflat, 15, None, ALU.bitwise_and))
                    dve.tensor_copy(tmp_f[0], tmp_i[0])
                    link(dve.tensor_copy(tmp_f[1], tmp_i[1]))
                    ii = i16f.rearrange("p (h w) k -> p h w k", w=2)
                    oh = flat(Z(92, 100)).rearrange("p (h k i) -> p h k i", h=8, k=16)
                    for w in range(2):
                        link(dve.tensor_tensor(oh, tmp_f[w].rearrange("p (h k) -> p h k", h=8).unsqueeze(3).broadcast_to([P, 8, 16, 16]),
                                               iota[:, 0:16].unsqueeze(1).unsqueeze(1).broadcast_to([P, 8, 16, 16]), ALU.is_equal))
                        yield
                        link(dve.tensor_tensor(oh, oh, ii[:, :, w, :].unsqueeze(2).broadcast_to([P, 8, 16, 16]), ALU.mult))
                        yield
                        link(dve.tensor_reduce(big[:, 66 + 2 * w + tt, 0:P].rearrange("p (h k) -> p h k", h=8), oh, AX.X, ALU.add))
                        yield
                    link(dve.tensor_copy(sums[:, 8 * tt:8 * tt + 8], top[:, :, 0]))
                    dve.tensor_tensor(top, top, sums[:, 8 * tt:8 * tt + 8].unsqueeze(2).broadcast_to([P, 8, 16]),
                                      ALU.subtract).then_inc(S["topm"], 1)

            def softmax_rest(tt):
                top = places(tt)[3]
                total = sums[:, 8 * tt:8 * tt + 8]
                dve.wait_ge(S["gexp"], tt + 1)
                link(dve.tensor_reduce(total, top, AX.X, ALU.add))
                link(dve.reciprocal(total, total))
                dve.tensor_tensor(top, top, total.unsqueeze(2).broadcast_to([P, 8, 16]), ALU.mult).then_inc(S["picked"], 1)

            def u_lo(it, k, between=iter(())):
                for hh in range(2):
                    dve.wait_ge(S["unit_hi"], it * 8 + (2 * (U0 + k) + hh + 1))
                    cols = slice(hh * 512, (hh + 1) * 512)
                    dve.tensor_tensor(w_lo[:, k % 2, cols], PS[:, 2 * (k % 2) + hh, :], w_hi[:, k % 2, cols].bitcast(f32),
                                      ALU.subtract).then_inc(S["unit_split"], 1)
                    next(between, None)

            def gate_in(i, k, part):
                par, seen = k % 2, i * (GATE_STEPS[part] // 2) + (GATE_BASE[part] + k // 2)
                lo_, hi_ = GATE_PARTS[part]
                n0 = i * (4 * GATE_STEPS[part]) + 4 * k
                g = big[:, lo_:hi_, n0:n0 + 4] if isinstance(n0, int) else big[:, lo_:hi_, ds(n0, 4)]
                dve.wait_ge(S[f"g_mm{par}"], seen + 1)
                dve.tensor_tensor(g, PS[:, 6 + par, :].rearrange("p (t e) -> p e t", t=4)[:, 0:hi_ - lo_, :], g,
                                  ALU.mult).then_inc(S[f"gated{par}"], 1)

            def gate_step(i, k, part):
                par, seen = k % 2, i * (GATE_STEPS[part] // 2) + (GATE_BASE[part] + k // 2)
                lo_, hi_ = GATE_PARTS[part]
                wait_past(dve, S[f"g_mm{par}"], seen)
                dve.tensor_tensor(hotB[par], bc(iota, 4), bc(eg[:, 1, ds(i * (4 * GATE_STEPS[part]) + 4 * k, 4)], P, 2), ALU.is_equal)
                yield
                for t in range(4):
                    last = dve.tensor_scalar(hotA[:, 4 * par + t, 0:hi_ - lo_], iota[:, lo_:hi_], eg[:, 0, ds(i * (4 * GATE_STEPS[part]) + (4 * k + t), 1)],
                                             eg[:, 2, ds(i * (4 * GATE_STEPS[part]) + (4 * k + t), 1)], ALU.is_equal, ALU.mult)
                last.then_inc(S[f"hot{par}"], 1)
                if k > 0:
                    gate_in(i, k - 1, part)
                elif not (isinstance(i, int) and i == 0):
                    gate_in(i - 1, GATE_STEPS[part] - 1, part)

            def gate_turn(it, i):
                for k in range(4):
                    if isinstance(i, int) and i == 0 and k == 1:
                        dve.wait_ge(S["gelu0"], GATE_AT)
                        dve.wait_ge(S["gelu1"], GATE_AT)
                    u_lo(it, k, gate_step(i, k, 0))
            picks = pick_steps()
            for unit in range(4 * PICKED_AT + 4):
                u_lo(unit // 4, unit % 4)
                if unit < 4 * EXP_AT:
                    next(picks, None)
                if unit == 4 * EXP_AT - 1:
                    assert next(picks, "ended") == "ended"
                if unit == 4 * EXP_AT + 6:
                    softmax_rest(0)
                    softmax_rest(1)
            dve.wait_ge(S["egT"], 1)
            dve.tensor_copy(eg[:, 0:2, :], half(6)).then_inc(S["eg_done"], 1)
            dve.tensor_copy(eg[:, 2, :], PS[:, 7, 0:256]).then_inc(S["eg_done"], 1)
            dve.wait_ge(S["eg_done"], 2)
            with dve.Fori(PICKED_AT + 1, GATE_AT) as it:
                for k in range(4):
                    u_lo(it, k)
            gate_turn(GATE_AT, 0)
            with dve.Fori(1, 16) as i:
                gate_turn(i + GATE_AT, i)
            gate_in(15, 3, 0)
            for h in range(2):
                def v_lo(it, gating=None, first_unit=0):
                    for k in range(4):
                        g = big[:, 4 * it + k, :] if isinstance(it, int) else big[:, ds(it * 4 + k, 1), :].rearrange("p a n -> p (a n)")
                        dve.wait_ge(S["act2_hi"], it * 4 + (h * BLOCKS + k + 1))
                        dve.tensor_tensor(act_lo[:, k % 2, :], g, act_hi[:, k % 2, :].bitcast(f32), ALU.subtract).then_inc(S["act2_split"], 1)
                        u = first_unit + k
                        step = gate_step(gating, u - u // 3, 1) if gating is not None and u % 3 < 2 else iter(())
                        for hh in range(2):
                            lo(it + (V0 + h * BLOCKS) // 4, k, hh)
                            next(step, None)

                def v_gating(i):
                    for j in range(V_TURN):
                        v_lo(i * V_TURN + j, i, 4 * j)
                if h == 0:
                    run_loop(dve, 0, 8, v_gating)
                    gate_in(7, GATE_STEPS[1] - 1, 1)
                    with dve.Fori(8 * V_TURN, BLOCKS // 4) as it:
                        v_lo(it)
                else:
                    run_loop(dve, 0, BLOCKS // 4, v_lo)
            dve.wait_ge(S["x1_in"], 16)
            dve.wait_ge(S["half_used"], 2 * (V0 + 2 * BLOCKS))
            for tt in range(2):
                x1 = flat(Z(8 * tt, 8 * tt + 8)).rearrange("p (h q n) -> p h q n", h=2, q=2)
                for h in range(2):
                    dve.tensor_tensor(x1[:, h], x1[:, h], PS[:, 4 * h + 2 * tt:4 * h + 2 * tt + 2, :], ALU.add).then_inc(S["res_done"], 1)
            norm(2)
            dve.wait_ge(S["norm_rstd"], 3)
            dve.wait_ge(S["fw_in"], 16)
            for tt in range(2):
                dve.scalar_tensor_tensor(flat(Z(24 + 8 * tt, 32 + 8 * tt)), flat(Z(8 * tt, 8 * tt + 8)), rstd[:, tt:tt + 1],
                                         flat(Z(16, 24)), ALU.mult, ALU.mult).then_inc(S["y_ready"], 1)


def shape_constants():
    c = np.zeros((P, NCONST), np.float32)
    i = np.arange(P)
    c[:, IDENT:IDENT + P] = np.eye(P)
    c[:, IOTA:IOTA + P] = i[None, :]
    head, s = i // 64, i % 64
    same = head[:, None] == head[None, :]
    before = s[:, None] < s[None, :]
    c[:, S1MASK:S1MASK + P] = same & before
    c[:, S1MASK + P:S1MASK + 2 * P] = same & (before | (s[:, None] == s[None, :]))
    c[:, BDMASK:BDMASK + P] = same
    for lv in range(1, 7):
        whole = (s[:, None] >> lv) == (s[None, :] >> lv)
        parts = (s[:, None] >> (lv - 1)) != (s[None, :] >> (lv - 1))
        c[:, LEVEL + (lv - 1) * P:LEVEL + lv * P] = same & before & whole & parts
    c[:, ONES:ONES + P] = same
    t = np.arange(TOK)
    inv_freq = np.float32(10000.0) ** (-np.arange(P, dtype=np.float32) * np.float32(2.0) / np.float32(256))
    ang = t.astype(np.float32)[None, :] * inv_freq[:, None].astype(np.float32)
    c[:, COS:COS + TOK] = np.cos(ang)
    c[:, SIN:SIN + TOK] = np.sin(ang)
    m, n = t[:, None], t[None, :]
    decay = np.zeros((P, HEADS, 2, TOK), np.float32)
    for h in range(HEADS):
        log_g = np.log(1.0 - 2.0 ** (-5.0 - h))
        w = np.where((m // 64 == n // 64) | (m < n), np.exp(log_g * np.abs(n - m)), 0.0) / 16.0
        decay[:, h] = w.reshape(2, P, TOK).transpose(1, 0, 2)
    return c, decay.reshape(P, -1)


_INS = ["x", "norm1_w", "w_in", "ret_gn_w", "ret_gn_b", "rwkv_mix", "rwkv_w0", "rwkv_w_up", "rwkv_a0", "rwkv_a_up",
        "rwkv_g_up", "rwkv_k_k", "rwkv_k_a", "rwkv_r_k", "rwkv_ln_w", "rwkv_ln_b", "w_ret_branch", "w_rwkv_branch",
        "w_out", "norm2_w", "peer_w_q", "peer_keys_1", "peer_keys_2", "peer_u", "peer_v", "final_norm_w"]


def kernel(**inputs):
    import numpy as _np
    import concourse.bacc as _bacc
    from concourse import mybir as _mybir
    from concourse.bass_utils import run_bass_kernel_spmd as _run

    nc = _bacc.Bacc("TRN2", target_bir_lowering=False, num_devices=1)
    arrays, args = {}, {}
    for name in _INS:
        arrays[f"in_{name}"] = _np.ascontiguousarray(inputs[name])
    arrays["in_consts"], arrays["in_ret_decay"] = shape_constants()
    for key, v in arrays.items():
        args[key[3:]] = nc.dram_tensor(key, v.shape, _mybir.dt.from_np(v.dtype), kind="ExternalInput").ap()
    args["out"] = nc.dram_tensor("out_0", (1, TOK, DM), _mybir.dt.float32, kind="ExternalOutput").ap()
    hybrid_block_kernel(nc, args)
    r = _run(nc, [arrays], core_ids=[0])
    return r.results[0]["out_0"]
```

```python
import numpy as np
import concourse.bass as bass
from concourse import mybir
from contextlib import ExitStack

P = 128
TOK = 256
DM = 2048
KC = DM // P
HEADS = 4
NE = 16384
BLOCKS = NE // P
TOPK = 16
NORM_EPS = 1e-6
GN_EPS = 64e-5

IDENT, IOTA, S1MASK, BDMASK, LEVEL, ONES, COS, SIN = 0, 128, 256, 512, 640, 1408, 1536, 1792
NCONST = 2048

VEC_ROWS = [("norm1_w", 16), ("rwkv_mix", 26), ("ret_gn_w", 8), ("ret_gn_b", 8), ("rwkv_w0", 8), ("rwkv_a0", 8),
            ("rwkv_k_k", 8), ("rwkv_k_a", 8), ("rwkv_r_k", 8), ("rwkv_ln_w", 8), ("rwkv_ln_b", 8)]
VEC = {}
_at = 0
for _name, _rows in VEC_ROWS:
    VEC[_name] = (_at, _rows)
    _at += _rows
VROWS = _at
VEC["norm2_w"] = (VROWS, 16)
NVEC = VROWS + 16

SEG = {"main_rwkv": (0, 0, 13, 4, 0), "main_ret": (52, 13, 16, 4, 0), "gates": (116, 29, 16, 4, 0), "ret": (180, 45, 8, 2, 0), "rwkv": (196, 53, 8, 2, 8),
       "out": (212, 61, 8, 4, 0), "wq": (244, 69, 8, 4, 0)}
U0, V0 = 276, 532
PEEL = {"main_ret": 8, "gates": 4}
PREP_MIX, PREP_LORA_IN, PREP_LORA_W, PREP_DECAY, PREP_EXP, PREP_LORA_A, PREP_A = 3, 12, 14, 16, 20, 21, 23
PREP_SCAN, PREP_KN, PREP_SHIFT, PREP_ROOT = 23, 28, 29, 31
HEAD_SQUARE, HEAD_VAR_MM, HEAD_VAR, HEAD_BONUS_MM, HEAD_ROOT, HEAD_BONUS, HEAD_REST, HEAD_GATE_MM = 2, 4, 6, 9, 9, 11, 13, 15
EXP_AT, PICKED_AT, GATE_AT = 13, 16, 48
GATE_PARTS = ((0, 96), (96, 128))
GATE_BASE = (0, 32)
GATE_STEPS = (4, 8)
V_TURN = 3


class Chain:

    def __init__(self, eng, sem):
        self.eng, self.sem, self.n, self.offset = eng, sem, 0, 0

    def link(self, ins):
        self.n += 1
        ins.then_inc(self.sem, 1)
        self.eng.wait_ge(self.sem, self.offset + self.n)


def run_loop(eng, first, count, body, peel=1):
    for i in range(first, first + peel):
        body(i)
    if first + peel < count:
        with eng.Fori(first + peel, count) as i:
            body(i)


def wait_past(eng, sem, value):
    if not (isinstance(value, int) and value <= 0):
        eng.wait_ge(sem, value)


def hybrid_block_kernel(nc, a):
    f32, f32r, u32 = mybir.dt.float32, mybir.dt.float32r, mybir.dt.uint32
    ALU, ACT, AX = mybir.AluOpType, mybir.ActivationFunctionType, mybir.AxisListType
    ds = bass.ds
    ctx = ExitStack()
    with ctx:
        def sb(name, shape, dt=f32):
            return ctx.enter_context(nc.sbuf_tensor(name, shape, dt))

        class Sems(dict):
            def __missing__(self, name):
                self[name] = ctx.enter_context(nc.semaphore("s_" + name))
                return self[name]

        S = Sems()

        big = sb("big", [P, P, TOK])
        act_hi = sb("act_hi", [P, KC, TOK], f32r)
        act_lo = sb("act_lo", [P, KC, TOK], f32r)
        raw = sb("raw", [P, 4, 1024])
        w_hi = sb("w_hi", [P, 2, 1024], f32r)
        w_lo = sb("w_lo", [P, 2, 1024], f32r)
        cst = sb("cst", [P, NCONST])
        vec = sb("vec", [P, NVEC])
        extra = sb("extra", [P, 1024])
        onehot2 = sb("onehot2", [P, 512])
        small = sb("small", [P, 96])
        PS = ctx.enter_context(nc.psum_tensor("PS", [P, 8, 512], f32))
        x1_dram = nc.dram_tensor("x1_scratch", [TOK, DM], f32, kind="Internal").ap()

        ident = cst[:, IDENT:IDENT + P]
        iota = cst[:, IOTA:IOTA + P]
        bdmask = cst[:, BDMASK:BDMASK + P]
        ones_bd = cst[:, ONES:ONES + P]

        def Z(lo, hi):
            return big[:, lo:hi, :]

        def flat(ap):
            return ap.rearrange("p c n -> p (c n)")

        def half(k):
            return PS[:, k, :].rearrange("p (j n) -> p j n", j=2)

        def per_token(name, lo=0, n=None):
            at, rows = VEC[name]
            n = rows if n is None else n
            return vec[:, at + lo:at + lo + n].unsqueeze(2).broadcast_to([P, n, TOK])

        def v1(name, k):
            return vec[:, VEC[name][0] + k:VEC[name][0] + k + 1]

        def bc(ap, n, axis=1):
            b = ap.unsqueeze(axis)
            shape = list(b.shape)
            shape[axis] = n
            return b.broadcast_to(shape)

        ss, rstd = small[:, 0:2], small[:, 2:4]
        bnst = small[:, 4:10]
        mv = small[:, 10:26].rearrange("p (k c) -> p k c", c=2)
        rs8 = small[:, 26:34]
        pend = small[:, 34:66]
        sums = small[:, 66:82]

        r1 = flat(Z(58, 90))
        r2 = flat(Z(16, 24))
        r3 = flat(Z(24, 32))
        r4 = flat(Z(126, 128))
        place = [
            dict(B1=r1[:, 0:1024], B2=r1[:, 1024:2048], V=r1[:, 2048:2560], bn=r1[:, 2560:3072], kn=r1[:, 3072:3584],
                 Lm=r1[:, 3584:4096], XW=r1[:, 4096:5120], Xt=r1[:, 5120:5632], AM=r1[:, 5632:6656], S=extra[:, 512:768]),
            dict(AM=r1[:, 6656:7680], V=r1[:, 7680:8192], XW=r2[:, 0:1024], Xt=r2[:, 1024:1536], bn=r2[:, 1536:2048],
                 B1=r3[:, 0:1024], B2=r3[:, 1024:2048], kn=r4, Lm=extra[:, 0:512], S=extra[:, 768:1024]),
        ]

        def two(ap):
            return ap.rearrange("p (n w c) -> p n w c", n=4, w=2)

        def one(ap):
            return ap.rearrange("p (n c) -> p n c", n=4)

        B1 = [two(d["B1"]) for d in place]
        B2 = [two(d["B2"]) for d in place]
        AM = [two(d["AM"]) for d in place]
        AS = [two(d["XW"]) for d in place]
        X = [one(d["XW"][:, 0:512]) for d in place]
        Wn = [one(d["XW"][:, 512:1024]) for d in place]
        beta_bd, kappa_bd = X, Wn
        Vn = [one(d["V"]) for d in place]
        Xt = [one(d["Xt"]) for d in place]
        v_bd = Xt
        alpha_bd = [AM[g][:, :, 1, :] for g in range(2)]
        bn_ = [one(d["bn"]) for d in place]
        kn_ = [one(d["kn"]) for d in place]
        Lm = [one(d["Lm"]) for d in place]
        St = [d["S"].rearrange("p (n c) -> p n c", n=2) for d in place]

        keysT = flat(Z(49, 50))
        SC = [flat(Z(50 + 8 * t, 58 + 8 * t)).rearrange("p (j k) -> p j k", k=P) for t in range(2)]
        eg = extra[:, 0:768].rearrange("p (w n) -> p w n", w=3)
        hotA = cst[:, S1MASK:S1MASK + 1024].rearrange("p (n e) -> p n e", n=8)
        hotB = [cst[:, S1MASK + 1024:S1MASK + 1536].rearrange("p (n e) -> p n e", n=4),
                onehot2[:, :].rearrange("p (n e) -> p n e", n=4)]

        def by_head(eng, i, g, src, dst):
            rows = big[:, ds(i * 2 + (src + g), 1), :].rearrange("p a (n t) -> p (a n) t", n=4)
            return eng.tensor_tensor(dst[g].rearrange("p n (h t) -> p n h t", h=2), bc(rows, 2, 2),
                                     bc(bdmask.rearrange("p (h t) -> p h t", h=2), 4), ALU.mult)

        block = ctx.enter_context(nc.Block())

        def seg_loop(eng, name, body, peel=1):
            u0, g0, ng, ku, _ = SEG[name]

            def pair(t, count=2):
                for j in range(count):
                    body(t, t * 2 + j, t * (ku // 2) + u0 // 4 + (j if ku == 4 else 0), j)
            run_loop(eng, 0, ng // 2, pair, peel)
            if ng % 2:
                pair(ng // 2, 1)

        operand = {"main_rwkv": Z(58, 74), "ret": Z(0, 16), "rwkv": Z(0, 16), "out": Z(58, 74), "wq": Z(16, 32)}
        nth_operand = {"main_rwkv": 0, "main_ret": 0, "gates": 0, "ret": 1, "rwkv": 1, "out": 2, "wq": 3}

        QK = Z(0, 16).rearrange("p (t a w) n -> p t a w n", t=2, w=2)

        def rot_part(lo_, hp):
            return Z(lo_ + 4 * hp, lo_ + 4 * hp + 4).rearrange("p (t a) n -> p t a n", t=2)

        def rot_half(hp, w):
            return QK[:, :, 2 * hp:2 * hp + 2, w, :]

        def rot_table(col):
            return cst[:, col:col + TOK].unsqueeze(1).unsqueeze(1).broadcast_to([P, 2, 2, TOK])

        def unit_slot(ku, j, kq):
            return kq if ku == 4 else 2 * j + kq

        @block.sync
        def _(sp):
            for tt in range(2):
                sp.dma_start(flat(Z(90 + 8 * tt, 98 + 8 * tt)), a["x"][0, tt * P:(tt + 1) * P, :]).then_inc(S[f"x_in{tt}"], 16)
            at = 0
            for name, rows in VEC_ROWS:
                src = a[name].rearrange("l h w -> (l h w)") if name == "rwkv_r_k" else a[name].rearrange("l n -> (l n)")
                sp.dma_start(flat(Z(122, 123))[at:at + rows, 0:P], src.rearrange("(r c) -> r c", c=P)).then_inc(S["rows_in"], 16)
                at += rows
            sp.dma_start(flat(Z(122, 123))[0:16, P:2 * P],
                         a["norm2_w"].rearrange("l n -> (l n)").rearrange("(r c) -> r c", c=P)).then_inc(S["rows_in"], 16)
            sp.dma_start(cst[:, :], a["consts"]).then_inc(S["const_in"], 16)

            def load_seg(name, weight, col0):
                _, g0, _, ku, _ = SEG[name]
                w = weight.rearrange("(c p) n -> p c n", p=P)

                def body(t, g, m, j):
                    for kq in range(ku):
                        slot = unit_slot(ku, j, kq)
                        if not (name == "main_rwkv" and isinstance(t, int) and t == 0 and j == 0):
                            sp.wait_ge(S["unit_split"], m * 8 + 2 * slot - 6)
                        sp.dma_start(raw[:, slot, :].rearrange("p (c n) -> p c n", c=4),
                                     w[:, 4 * kq:4 * kq + 4, ds(g * 256 + col0, 256)]).then_inc(S[f"raw_in{slot}"], 16)
                seg_loop(sp, name, body)

            w_in = a["w_in"][0]
            load_seg("main_rwkv", w_in, 32 * P)
            sp.wait_ge(S["vecT"], 1)
            sp.dma_start(flat(Z(122, 126))[0:64, :], a["rwkv_w_up"][0]).then_inc(S["up_in"], 16)
            sp.dma_start(flat(Z(122, 126))[64:128, :], a["rwkv_a_up"][0]).then_inc(S["up_in"], 16)
            load_seg("main_ret", w_in, 0)
            sp.wait_ge(S["lora_a"], 4)
            sp.dma_start(flat(Z(122, 126)), a["rwkv_g_up"][0]).then_inc(S["gup_in"], 16)
            sp.wait_ge(S["rot_done"], 4)
            sp.dma_start(flat(Z(82, 90)), a["ret_decay"]).then_inc(S["decay_in"], 16)
            load_seg("gates", w_in, 58 * P)
            load_seg("ret", a["w_ret_branch"][0], 0)
            load_seg("rwkv", a["w_rwkv_branch"][0], 0)
            load_seg("out", a["w_out"][0], 0)
            sp.wait_ge(S["merged"], 8)
            sp.dma_start(flat(Z(90, 106)).rearrange("p (a n) -> p a n", a=2),
                         a["x"][0].rearrange("(a p) n -> p a n", p=P)).then_inc(S["x_again"], 16)
            sp.dma_start(flat(Z(48, 49))[:, 0:P], a["peer_keys_1"][0]).then_inc(S["keys_in"], 16)
            sp.dma_start(flat(Z(48, 49))[:, P:2 * P], a["peer_keys_2"][0]).then_inc(S["keys_in"], 16)
            load_seg("wq", a["peer_w_q"][0], 0)
            sp.wait_ge(S["x1_done"], 8)                
            sp.dma_start(x1_dram.rearrange("(a p) n -> p a n", p=P),
                         flat(Z(90, 106)).rearrange("p (a n) -> p a n", a=2)).then_inc(S["x1_out"], 16)
            u_rows = a["peer_u"][0].rearrange("(b e) n -> b e n", e=P)
            v_rows = a["peer_v"][0].rearrange("(b e) n -> b e n", e=P)

            def load_experts(rows, it, sem, value):
                for k in range(4):
                    sp.wait_ge(S[sem], value(k))
                    sp.dma_start(raw[:, k, :], rows[ds(it * 2 + k // 2, 1), :, (k % 2) * 1024:(k % 2 + 1) * 1024]
                                 .rearrange("a e n -> e (a n)")).then_inc(S[f"raw_in{k}"], 16)
            load_experts(u_rows, 0, "unit_split", lambda k: 2 * (U0 + k) - 6)
            with sp.Fori(1, BLOCKS // 2) as it:
                load_experts(u_rows, it, "uT_bank", lambda k: it * 8 + 2 * k - 6)
            for h in range(2):
                def load_v(it):
                    for k in range(4):
                        if h == 0 and isinstance(it, int):
                            sp.wait_ge(S["uT_bank"], 4 * BLOCKS + 2 * k - 6)
                        else:
                            sp.wait_ge(S["unit_split"], it * 8 + (2 * (V0 + h * BLOCKS + k) - 6))
                        sp.dma_start(raw[:, k, :], v_rows[ds(it * 4 + k, 1), :, h * 1024:(h + 1) * 1024]
                                     .rearrange("a e n -> e (a n)")).then_inc(S[f"raw_in{k}"], 16)
                run_loop(sp, 0, BLOCKS // 4, load_v)
            sp.wait_ge(S["half_used"], 2 * (V0 + BLOCKS + 60))
            sp.dma_start(flat(Z(0, 16)).rearrange("p (a n) -> p a n", a=2),
                         x1_dram.rearrange("(a p) n -> p a n", p=P)).then_inc(S["x1_in"], 16)
            sp.dma_start(flat(Z(16, 24)), a["final_norm_w"].partition_broadcast(P)).then_inc(S["fw_in"], 16)
            for tt in range(2):
                sp.wait_ge(S["y_ready"], tt + 1)
                sp.dma_start(a["out"][0, tt * P:(tt + 1) * P, :], flat(Z(24 + 8 * tt, 32 + 8 * tt))).then_inc(S["stored"], 16)
            sp.wait_ge(S["stored"], 32)

        @block.tensor
        def _(pe):
            def mm3(out, wh, wl, xh, xl, start, stop):
                pe.matmul(out, wh, xh, start=start, stop=False)
                pe.matmul(out, wh, xl, start=False, stop=False)
                return pe.matmul(out, wl, xh, start=False, stop=stop)

            def project(name, between=None):
                u0, g0, ng, ku, koff = SEG[name]

                def body(t, g, m, j):
                    par = (g0 + j) % 2
                    if not (name == "main_rwkv" and isinstance(t, int) and t == 0):
                        pe.wait_ge(S["proj_evac"], g + g0 - 1)
                    for kq in range(ku):
                        slot = unit_slot(ku, j, kq)
                        if isinstance(g, int) and g == 0:
                            pe.wait_ge(S["act_split"], 4 * nth_operand[name] + koff // 4 + kq + 1)
                        for hh in range(2):
                            pe.wait_ge(S["unit_split"], m * 8 + 2 * slot + hh + 1)
                            for c in (2 * hh, 2 * hh + 1):
                                kc = koff + 4 * kq + c
                                for jj in range(2):
                                    cols = slice(c * 256 + jj * P, c * 256 + (jj + 1) * P)
                                    last = mm3(PS[:, 2 * par + jj, 0:TOK], w_hi[:, slot % 2, cols], w_lo[:, slot % 2, cols],
                                               act_hi[:, kc, :], act_lo[:, kc, :],
                                               kq == 0 and c == 0, kq == ku - 1 and c == 3)
                            last.then_inc(S["half_used"], 1)
                        if between and isinstance(g, int):
                            between(4 * g + kq)
                seg_loop(pe, name, body, PEEL[name] if between else 1)

            pe.wait_ge(S["const_in"], 16)
            pe.wait_ge(S["rows_in"], 16 * 12)
            pe.transpose(PS[:, 7, 0:VROWS], flat(Z(122, 123))[0:VROWS, 0:P], ident[0:VROWS, 0:VROWS])
            pe.transpose(PS[:, 7, VROWS:NVEC], flat(Z(122, 123))[0:16, P:2 * P], ident[0:16, 0:16]).then_inc(S["vecT"], 1)
            xn = [flat(Z(106 + 8 * t, 114 + 8 * t)) for t in range(2)]

            def transpose_tokens(src, done, bank7_free):
                for gi in range(8):
                    tt, cg = gi // 4, gi % 4
                    if gi == 7:
                        bank7_free()
                    for c in range(4):
                        col = (4 * cg + c) * P
                        last = pe.transpose(PS[:, gi, c * P:(c + 1) * P], src[tt][:, col:col + P], ident)
                    last.then_inc(S[done], 1)
            pe.wait_ge(S["normed"], 2)
            transpose_tokens(xn, "xT_done", lambda: pe.wait_ge(S["vec_done"], 1))

            project("main_rwkv")

            up = flat(Z(122, 126))

            def rwkv_between(unit):
                if unit == PREP_LORA_W:
                    pe.wait_ge(S["up_in"], 32)
                    pe.wait_ge(S["lora_in"], 1)
                    for k in range(8):
                        last = pe.matmul(half(4 + k // 2)[:, k % 2, :], up[0:64, k * P:(k + 1) * P], big[0:64, 56, :],
                                         start=True, stop=True)
                        if k % 2:
                            last.then_inc(S["lora_w"], 1)
                if unit == PREP_LORA_A:
                    pe.wait_ge(S["sg_done"], 8)
                    for k in range(8):
                        last = pe.matmul(half(4 + k // 2)[:, k % 2, :], up[64:128, k * P:(k + 1) * P], big[64:128, 56, :],
                                         start=True, stop=True)
                        if k % 2:
                            last.then_inc(S["lora_a"], 1)
                if unit == PREP_KN:
                    pe.wait_ge(S["sq_done"], 2)
                    pe.wait_ge(S["a_done"], 8)
                    for q in range(4):
                        last = pe.matmul(PS[:, 4 + q, :], ones_bd, flat(Z(82 + 2 * q, 84 + 2 * q)), start=True, stop=True)
                    last.then_inc(S["kn_done"], 1)
            project("main_ret", rwkv_between)

            pe.wait_ge(S["proj_evac"], 29)
            for bank in range(4):
                tt, q = bank // 2, bank % 2
                for c in range(4):
                    last = pe.transpose(PS[:, bank, c * P:(c + 1) * P], big[:, 16 + 4 * q + c, tt * P:(tt + 1) * P], ident)
                last.then_inc(S["vT_done"], 1)
            pe.wait_ge(S["kn_read"], 2)
            for h in range(HEADS):
                pe.wait_ge(S["rot_done"], 2 * (h // 2) + 2)
                for mt in range(2):
                    for kc in range(2):
                        last = pe.matmul(half(4 + h)[:, mt, :], big[:, 8 + 2 * h + kc, mt * P:(mt + 1) * P],
                                         big[:, 2 * h + kc, :], start=kc == 0, stop=kc == 1)
                last.then_inc(S["sc_done"], 1)
            sT = Z(66, 74).rearrange("p (h m) n -> p h m n", m=2)
            vtok = Z(74, 82).rearrange("p (m h) n -> p m h n", m=2)
            pe.wait_ge(S["vtok"], 4)
            for h in range(HEADS):
                pe.wait_ge(S["st_done"], h + 1)
                for nt in range(2):
                    for mt in range(2):
                        last = pe.matmul(half(h)[:, nt, :], sT[:, h, mt, nt * P:(nt + 1) * P], vtok[:, mt, h, :],
                                         start=mt == 0, stop=mt == 1)
                last.then_inc(S["o_done"], 1)
            pe.wait_ge(S["on_done"], 8)
            for h in range(HEADS):
                for ec in range(2):
                    for nt in range(2):
                        last = pe.transpose(PS[:, 4 + h, ec * 256 + nt * P:ec * 256 + (nt + 1) * P],
                                            big[:, 58 + 2 * h + nt, ec * P:(ec + 1) * P], ident)
                last.then_inc(S["oT_done"], 1)

            pe.wait_ge(S["oret_pre"], 8)

            def pairs(i):
                for g in range(2):
                    b = 4 * g
                    pe.wait_ge(S[f"prep{g}"], i + 1)
                    wait_past(pe, S[f"prep_bk{g}"], i)
                    wait_past(pe, S[f"ye{g}"], i * 2)
                    wait_past(pe, S[f"st{g}"], i * 2)
                    for q, lhs in enumerate((beta_bd, kappa_bd)):
                        for n in range(4):
                            for w, src in enumerate((114, 90)):
                                rhs = big[:, ds(i * 2 + (src + g), 1), n * 64:(n + 1) * 64].broadcast_to([P, 2, 64])
                                col = (n % 2) * 256 + w * P
                                last = pe.matmul(PS[:, b + 2 * q + n // 2, col:col + P], lhs[g][:, n, :], rhs, start=True, stop=True)
                    last.then_inc(S[f"s1{g}"], 1)
                for g in range(2):
                    b = 4 * g
                    pe.wait_ge(S[f"s1e{g}"], i * 4 + 4)
                    for w, src in enumerate((v_bd, alpha_bd, beta_bd, kappa_bd)):
                        for n in range(4):
                            last = pe.transpose(PS[:, b + w, n * P:(n + 1) * P], src[g][:, n, :], ident)
                    last.then_inc(S[f"s2{g}"], 1)
                for g in range(2):
                    b = 4 * g
                    pe.wait_ge(S[f"va{g}"], i * 2 + 2)
                    pe.wait_ge(S[f"xt1{g}"], i + 1)
                    for n in range(4):
                        last = pe.transpose(PS[:, b, n * P:(n + 1) * P], Xt[g][:, n, :], ident)
                    last.then_inc(S[f"xp{g}"], 1)
                for lv in range(5):
                    for g in range(2):
                        b = 4 * g
                        pe.wait_ge(S[f"lm{g}"], i * 5 + lv + 1)
                        if lv == 0:
                            pe.wait_ge(S[f"xc{g}"], i * 10 + 1)
                        else:
                            pe.wait_ge(S[f"xc{g}"], i * 10 + 2 * lv + 1)
                        for n in range(4):
                            last = pe.matmul(PS[:, b + 1, n * P:(n + 1) * P], Lm[g][:, n, :], X[g][:, n, :], start=True, stop=True)
                        last.then_inc(S[f"w{g}"], 1)
                    for g in range(2):
                        b = 4 * g
                        if lv == 0:
                            pe.wait_ge(S[f"bk{g}"], i * 2 + 2)
                        pe.wait_ge(S[f"wn{g}"], i * 5 + lv + 1)
                        if lv < 4:
                            for n in range(4):
                                pe.matmul(PS[:, b + 2, n * P:(n + 1) * P], Xt[g][:, n, :], Wn[g][:, n, :], start=True, stop=True)
                        for n in range(4):
                            last = pe.matmul(PS[:, b + 3, n * P:(n + 1) * P], Wn[g][:, n, :], Xt[g][:, n, :], start=True, stop=True)
                        last.then_inc(S[f"xx{g}"], 1)
                for g in range(2):
                    b = 4 * g
                    for n in range(4):
                        last = pe.matmul(PS[:, b, n * P:(n + 1) * P], B2[g][:, n, 0, :], Vn[g][:, n, :], start=True, stop=True)
                    last.then_inc(S[f"mv{g}"], 1)
                for g in range(2):
                    b = 4 * g
                    pe.wait_ge(S[f"xc{g}"], i * 10 + 10)
                    pe.wait_ge(S[f"mvc{g}"], i + 1)
                    for n in range(4):
                        last = pe.matmul(PS[:, b + 1 + n // 2, (n % 2) * 256:(n % 2 + 1) * 256], Xt[g][:, n, :],
                                         AM[g][:, n, :, :], start=True, stop=True)
                    last.then_inc(S[f"as{g}"], 1)
                for g in range(2):
                    b = 4 * g
                    pe.wait_ge(S[f"asc{g}"], i * 2 + 2)
                    for n in range(4):
                        cols = slice(n * P, (n + 1) * P)
                        pe.matmul(PS[:, b + 3, cols], AS[g][:, n, 0, :], bn_[g][:, n, :], start=True, stop=True)
                        pe.matmul(PS[:, b, cols], kn_[g][:, n, :], Vn[g][:, n, :], start=True, stop=False)
                        pe.matmul(PS[:, b, cols], bn_[g][:, n, :], AS[g][:, n, 1, :], start=False, stop=True)
                        last = pe.matmul(PS[:, b + 1, cols], AS[g][:, n, 0, :], B1[g][:, n, 1, :], start=True, stop=True)
                    last.then_inc(S[f"f{g}"], 1)

                def y_chunk(g, n, state):
                    out = PS[:, 4 * g + 2, n * P:(n + 1) * P]
                    if state is not None:
                        pe.matmul(out, state, B2[g][:, n, 0, :], start=True, stop=False)
                    pe.matmul(out, AS[g][:, n, 1, :], B1[g][:, n, 1, :], start=state is None, stop=False)
                    return pe.matmul(out, Vn[g][:, n, :], B2[g][:, n, 1, :], start=False, stop=True)
                for n in range(4):
                    for g in range(2):
                        state = [None, B1[g][:, 0, 0, :], St[g][:, 0, :], St[g][:, 1, :]][n]
                        if n == 0:
                            pe.wait_ge(S[f"fe{g}"], i * 4 + 4)
                        if n >= 2:
                            pe.wait_ge(S[f"st{g}"], i * 2 + n - 1)
                        if n in (1, 2):
                            pe.matmul(PS[:, 4 * g + 3, n * P:(n + 1) * P], Lm[g][:, n, :], state, start=True,
                                      stop=True).then_inc(S[f"ch{g}"], 1)
                        last = y_chunk(g, n, state)
                        if n == 3:
                            last.then_inc(S[f"y{g}"], 1)
            run_loop(pe, 0, 4, pairs)

            for g in range(2):
                pe.wait_ge(S[f"ye{g}"], 8)
                pe.wait_ge(S[f"st{g}"], 8)
            for q in range(4):
                last = pe.matmul(PS[:, 4 + q, :], ones_bd, flat(Z(114 + 2 * q, 116 + 2 * q)), start=True, stop=True)
            last.then_inc(S["ym_done"], 1)

            def head_between(unit):
                if unit == HEAD_VAR_MM:
                    pe.wait_ge(S["ysq_done"], 2)
                    for q in range(4):
                        last = pe.matmul(PS[:, 4 + q, :], ones_bd, flat(Z(66 + 2 * q, 68 + 2 * q)), start=True, stop=True)
                    last.then_inc(S["yv_done"], 1)
                if unit == HEAD_BONUS_MM:
                    pe.wait_ge(S["rk_done"], 1)
                    pe.wait_ge(S["yvar"], 2)
                    for q in range(4):
                        last = pe.matmul(PS[:, 4 + q, :], ones_bd, flat(Z(32 + 2 * q, 34 + 2 * q)), start=True, stop=True)
                    last.then_inc(S["bonus"], 1)
                if unit == HEAD_GATE_MM:
                    pe.wait_ge(S["gup_in"], 16)
                    pe.wait_ge(S["bonus_read"], 2)
                    gup = flat(Z(122, 126))
                    for k in range(8):
                        last = pe.matmul(half(4 + k // 2)[:, k % 2, :], gup[:, k * P:(k + 1) * P], big[:, 57, :],
                                         start=True, stop=True)
                    last.then_inc(S["gate_up"], 1)
            project("gates", head_between)
            project("ret")
            project("rwkv")
            project("out")
            pe.wait_ge(S["proj_evac"], 69)
            for gi in range(8):
                tt, cg = gi // 4, gi % 4
                for c in range(4):
                    last = pe.transpose(PS[:, gi, c * P:(c + 1) * P], big[:, 4 * cg + c, tt * P:(tt + 1) * P], ident)
                last.then_inc(S["dT_done"], 1)
            pe.wait_ge(S["normed"], 4)
            transpose_tokens(xn, "x2T_done", lambda: None)
            pe.wait_ge(S["keys_in"], 32)
            pe.wait_ge(S["h2T"], 8)
            for w in range(2):
                last = pe.transpose(PS[:, 7, w * P:(w + 1) * P], flat(Z(48, 49))[:, w * P:(w + 1) * P], ident)
            last.then_inc(S["kT_done"], 1)
            project("wq")
            pe.wait_ge(S["proj_evac"], 77)
            pe.wait_ge(S["keysT"], 1)
            for tt in range(2):
                for q in range(4):
                    for c in range(4):
                        j = 4 * q + c
                        last = pe.matmul(PS[:, 4 * tt + q, c * P:(c + 1) * P], big[:, 32 + j, tt * P:(tt + 1) * P],
                                         keysT[:, (j % 2) * P:(j % 2 + 1) * P], start=True, stop=True)
                last.then_inc(S["s_done"], 1)

            def ut(it, k):
                pe.wait_ge(S[f"raw_in{k}"], it * 16 + 16 * (U0 // 4 + 1))
                for hh in range(2):
                    pe.wait_ge(S["unit_split"], it * 8 + (2 * (U0 + k) - 3 + hh))
                    for c in range(4):
                        last = pe.transpose(PS[:, 2 * (k % 2) + hh, c * P:(c + 1) * P],
                                            raw[:, k, (4 * hh + c) * P:(4 * hh + c + 1) * P], ident)
                    last.then_inc(S["uT_bank"], 1)

            def um(it, k):
                for hh in range(2):
                    pe.wait_ge(S["unit_split"], it * 8 + (2 * (U0 + k) + hh + 1))
                    if k % 2 == 0 and hh == 0:
                        wait_past(pe, S[f"gelu{k // 2}"], it)
                    for c in range(4):
                        kc = (k % 2) * 8 + 4 * hh + c
                        cols = slice((4 * hh + c) * P, (4 * hh + c + 1) * P)
                        last = mm3(PS[:, 4 + k // 2, 0:TOK], w_hi[:, k % 2, cols], w_lo[:, k % 2, cols],
                                   act_hi[:, kc, :], act_lo[:, kc, :], kc == 0, kc == 15)
                    last.then_inc(S["half_used"], 1)

            def gates_mm(i, k, part):
                par, seen = k % 2, i * (GATE_STEPS[part] // 2) + (GATE_BASE[part] + k // 2)
                lo_, hi_ = GATE_PARTS[part]
                pe.wait_ge(S[f"hot{par}"], seen + 1)
                wait_past(pe, S[f"gated{par}"], seen)
                for t in range(4):
                    last = pe.matmul(PS[:, 6 + par, t * P:t * P + hi_ - lo_], hotB[par][:, t, :], hotA[:, 4 * par + t, 0:hi_ - lo_],
                                     start=True, stop=True)
                last.then_inc(S[f"g_mm{par}"], 1)

            def u_blocks(it, gating=None, final=False):
                for k in range(4):
                    if k < 3:
                        ut(it, k + 1)
                    elif not final:
                        ut(it + 1, 0)
                    um(it, k)
                    if gating is not None:
                        gates_mm(gating, k, 0)
            pe.wait_ge(S["sc_copied"], 1)
            ut(0, 0)
            pe.wait_ge(S["sc_copied"], 2)
            run_loop(pe, 0, PICKED_AT, u_blocks)
            pe.wait_ge(S["picked"], 2)
            for w, src in enumerate((66, 68, 70)):
                for tt in range(2):
                    last = pe.transpose(PS[:, 6 + w // 2, (w % 2) * 256 + tt * P:(w % 2) * 256 + (tt + 1) * P],
                                        big[:, src + tt, 0:P], ident)
            last.then_inc(S["egT"], 1)
            with pe.Fori(PICKED_AT, GATE_AT) as it:
                u_blocks(it)
            pe.wait_ge(S["eg_done"], 2)
            u_blocks(GATE_AT, 0)
            with pe.Fori(1, 15) as i:
                u_blocks(i + GATE_AT, i)
            u_blocks(BLOCKS // 2 - 1, 15, True)

            pe.wait_ge(S["gelu0"], BLOCKS // 2)
            pe.wait_ge(S["gelu1"], BLOCKS // 2)

            def vm(h, it, k, start=False, stop=False):
                u = it * 8 + 2 * (V0 + h * BLOCKS + k)
                pe.wait_ge(S["act2_split"], it * 4 + (h * BLOCKS + k + 1))
                for hh in range(2):
                    pe.wait_ge(S["unit_split"], u + hh + 1)
                    for tt in range(2):
                        out = PS[:, 4 * h + 2 * tt + hh, :]
                        cols = slice(hh * 512, (hh + 1) * 512)
                        ah = act_hi[:, k % 2, tt * P:(tt + 1) * P]
                        al = act_lo[:, k % 2, tt * P:(tt + 1) * P]
                        pe.matmul(out, ah, w_hi[:, k % 2, cols], start=start, stop=False)
                        pe.matmul(out, ah, w_lo[:, k % 2, cols], start=False, stop=False)
                        last = pe.matmul(out, al, w_hi[:, k % 2, cols], start=False, stop=stop)
                    last.then_inc(S["half_used"], 1)
            for h in range(2):
                def v_blocks(it, first=False, final=False):
                    for k in range(4):
                        vm(h, it, k, first and k == 0, final and k == 3)

                def v_gating(i):
                    for u in range(4 * V_TURN):
                        vm(h, i * V_TURN + u // 4, u % 4, isinstance(i, int) and u == 0)
                        if u % 3 < 2:
                            gates_mm(i, u - u // 3, 1)
                if h == 0:
                    run_loop(pe, 0, 8, v_gating)
                else:
                    pe.wait_ge(S["gated0"], 64)
                    pe.wait_ge(S["gated1"], 64)
                    v_blocks(0, first=True)
                with pe.Fori(8 * V_TURN if h == 0 else 1, BLOCKS // 4 - 1) as it:
                    v_blocks(it)
                v_blocks(BLOCKS // 4 - 1, final=True)

        @block.scalar
        def _(act):
            ch = Chain(act, S["act_chain"])

            def hi(m, slot, hh, first=False):
                if hh == 0:
                    act.wait_ge(S[f"raw_in{slot}"], m * 16 + 16)
                if not first:
                    act.wait_ge(S["half_used"], m * 8 + (2 * slot - 3 + hh))
                act.activation(w_hi[:, slot % 2, hh * 512:(hh + 1) * 512], raw[:, slot, hh * 512:(hh + 1) * 512],
                               ACT.Copy).then_inc(S["unit_hi"], 1)

            def split_seg(name, evac=None, between=None):
                u0, g0, ng, ku, _ = SEG[name]

                def body(t, g, m, j):
                    for kq in range(ku):
                        slot = unit_slot(ku, j, kq)
                        first = name == "main_rwkv" and isinstance(t, int) and t == 0 and j == 0 and kq < 2
                        if name in operand and isinstance(g, int) and g == 0:
                            split_act(name, kq)
                        for hh in range(2):
                            hi(m, slot, hh, first)
                        if kq == 1 and evac and not (isinstance(g, int) and g == 0):
                            act.wait_ge(S["half_used"], m * 8 + (4 * j if ku == 2 else 0))
                            evac(g - 1, (g0 + j + 1) % 2)
                        if between and isinstance(g, int):
                            between(4 * g + kq)
                seg_loop(act, name, body, PEEL[name] if between else 1)
                if evac and name != "main_rwkv":
                    act.wait_ge(S["half_used"], 2 * (u0 + ng * ku))
                    evac(ng - 1, (g0 + ng - 1) % 2)

            def split_act(name, kq):
                pc = SEG[name][4] // 4 + kq
                if name in ("main_rwkv", "wq"):
                    act.wait_ge(S["hT" if name == "main_rwkv" else "h2T"], 5 + pc)
                if name in ("ret", "rwkv"):
                    act.wait_ge(S["orwkv"], 2)
                if name == "out":
                    act.wait_ge(S["merged"], 2 * pc + 2)
                    act.wait_ge(S["half_used"], 2 * SEG["rwkv" if pc < 2 else "out"][0])
                act.activation(act_hi[:, 4 * pc:4 * pc + 4, :], operand[name][:, 4 * pc:4 * pc + 4, :], ACT.Copy).then_inc(S["act_hi"], 1)

            def norm_root(src, junk, nth):
                for tt in range(2):
                    if nth == 0:
                        act.wait_ge(S[f"x_in{tt}"], 16)
                    act.activation(junk[tt], src[tt], ACT.Square, accum_out=ss[:, tt:tt + 1]).then_inc(S["norm_sum"], 1)
                act.wait_ge(S["norm_mean"], nth + 1)
                act.activation(rstd, ss, ACT.Sqrt).then_inc(S["norm_root"], 1)

            def norm(src, dst, nth):
                norm_root(src, dst, nth)
                act.wait_ge(S["norm_rstd"], nth + 1)
                for tt in range(2):
                    act.activation(dst[tt], src[tt], ACT.Copy, scale=rstd[:, tt:tt + 1]).then_inc(S["normed"], 1)

            xs = [flat(Z(90 + 8 * t, 98 + 8 * t)) for t in range(2)]
            xn = [flat(Z(106 + 8 * t, 114 + 8 * t)) for t in range(2)]
            norm(xs, xn, 0)

            def evac_copy(base):
                def evac(g, par):
                    act.activation(big[:, ds(g * 2 + base, 2), :] if not isinstance(g, int) else big[:, base + 2 * g:base + 2 * g + 2, :],
                                   PS[:, 2 * par:2 * par + 2, 0:TOK], ACT.Copy).then_inc(S["proj_evac"], 1)
                return evac

            def evac_sigmoid(base):
                def evac(g, par):
                    act.activation(big[:, ds(g * 2 + base, 2), :] if not isinstance(g, int) else big[:, base + 2 * g:base + 2 * g + 2, :],
                                   PS[:, 2 * par:2 * par + 2, 0:TOK], ACT.Sigmoid).then_inc(S["proj_evac"], 1)
                return evac
            split_seg("main_rwkv", evac_copy(32))

            pc = Z(98, 106).rearrange("p c (n t) -> p (c n) t", t=64)
            pp = Z(66, 74).rearrange("p c (n t) -> p (c n) t", t=64)

            def rwkv_between(unit):
                if unit == 1:
                    act.wait_ge(S["half_used"], 2 * SEG["main_ret"][0])
                    evac_copy(32)(SEG["main_rwkv"][2] - 1, 0)
                if unit == PREP_LORA_IN:
                    act.wait_ge(S["mixB"], 1)
                    act.activation(big[0:64, 56, :], big[0:64, 56, :], ACT.Tanh).then_inc(S["lora_in"], 1)
                    act.activation(Z(57, 58), Z(57, 58), ACT.Sigmoid).then_inc(S["xg_done"], 1)
                for start, name, done, dst, bias in ((PREP_DECAY, "lora_w", "sg_done", 90, "rwkv_w0"),
                                                     (PREP_A, "lora_a", "a_done", 74, "rwkv_a0")):
                    q = unit - start
                    if 0 <= q < 4:
                        act.wait_ge(S[name], q + 1)
                        for k in (2 * q, 2 * q + 1):
                            act.activation(big[:, dst + k, :], half(4 + q)[:, k % 2, :], ACT.Sigmoid, bias=v1(bias, k)).then_inc(S[done], 1)
                if unit == PREP_EXP:
                    act.wait_ge(S["sg_done"], 8)
                q = unit - PREP_EXP
                if 0 <= q < 2:
                    rows = Z(90 + 4 * q, 94 + 4 * q)
                    act.activation(rows, rows, ACT.Exp, scale=-float(np.exp(-0.5))).then_inc(S["dec_done"], 1)
                q = unit - PREP_SHIFT
                if 0 <= q < 2:
                    act.wait_ge(S["scan_done"], q + 1)
                    act.wait_ge(S["mixA"], 4)
                    act.activation(pp[:, 16 * q:16 * q + 16, 1:64], pc[:, 16 * q:16 * q + 16, 0:63], ACT.Copy).then_inc(S["pprev"], 1)
                q = unit - PREP_ROOT
                if 0 <= q < 2:
                    act.wait_ge(S["kn_done"], 1)
                    act.activation(flat(Z(82 + 4 * q, 86 + 4 * q)).rearrange("p (q n) -> p q n", q=2), PS[:, 4 + 2 * q:6 + 2 * q, :],
                                   ACT.Sqrt).then_inc(S["kn_read"], 1)
            split_seg("main_ret", evac_copy(0), rwkv_between)

            vtok = flat(Z(74, 82))
            act.wait_ge(S["rot_done"], 4)
            for bank in range(4):
                act.wait_ge(S["vT_done"], bank + 1)
                act.activation(vtok[:, bank * 512:(bank + 1) * 512], PS[:, bank, :], ACT.Copy).then_inc(S["vtok"], 1)
            act.wait_ge(S["proj_evac"], 29)
            act.activation(Z(24, 32), Z(24, 32), ACT.Silu).then_inc(S["silu"], 1)
            act.wait_ge(S["on_var"], 1)
            act.activation(rs8, rs8, ACT.Sqrt).then_inc(S["on_sqrt"], 1)

            with act.Fori(0, 4) as i:
                for g in range(2):
                    act.wait_ge(S[f"s2{g}"], i + 1)
                    for w, dst in enumerate((bn_, kn_)):
                        act.activation(dst[g], PS[:, 4 * g + 2 + w, :].rearrange("p (n c) -> p n c", n=4), ACT.Copy).then_inc(S[f"bk{g}"], 1)
                for g in range(2):
                    act.wait_ge(S[f"xp{g}"], i + 1)
                    act.activation(X[g], PS[:, 4 * g, :].rearrange("p (n c) -> p n c", n=4), ACT.Copy).then_inc(S[f"xc{g}"], 1)
                for lv in range(5):
                    for g in range(2):
                        act.wait_ge(S[f"xx{g}"], i * 5 + lv + 1)
                        if lv < 4:
                            act.activation(X[g], PS[:, 4 * g + 2, :].rearrange("p (n c) -> p n c", n=4), ACT.Copy).then_inc(S[f"xc{g}"], 1)
                        act.activation(Xt[g], PS[:, 4 * g + 3, :].rearrange("p (n c) -> p n c", n=4), ACT.Copy).then_inc(S[f"xc{g}"], 1)
                for g in range(2):
                    act.wait_ge(S[f"mv{g}"], i + 1)
                    act.activation(AM[g][:, :, 1, :], PS[:, 4 * g, :].rearrange("p (n c) -> p n c", n=4), ACT.Copy).then_inc(S[f"mvc{g}"], 1)
                for g in range(2):
                    act.wait_ge(S[f"as{g}"], i + 1)
                    for q in range(2):
                        act.activation(AS[g][:, 2 * q:2 * q + 2, :, :],
                                       PS[:, 4 * g + 1 + q, :].rearrange("p (n w c) -> p n w c", n=2, w=2), ACT.Copy,
                                       scale=-1.0).then_inc(S[f"asc{g}"], 1)
                for g in range(2):
                    act.wait_ge(S[f"y{g}"], i + 1)
                    for h in range(2):
                        rows = slice(64 * h, 64 * h + 64)
                        act.activation(big[rows, ds(i * 2 + (114 + g), 1), :].rearrange("p a (n t) -> p (a n) t", n=4),
                                       PS[rows, 4 * g + 2, :].rearrange("p (n w t) -> p n w t", n=4, w=2)[:, :, h, :],
                                       ACT.Copy).then_inc(S[f"ye{g}"], 1)

            def head_between(unit):
                q = unit - HEAD_SQUARE
                if 0 <= q < 2:
                    act.wait_ge(S["yc_done"], q + 1)
                    act.activation(Z(66 + 4 * q, 70 + 4 * q), Z(58 + 4 * q, 62 + 4 * q), ACT.Square).then_inc(S["ysq_done"], 1)
                q = unit - HEAD_ROOT
                if 0 <= q < 2:
                    act.wait_ge(S["yvar"], q + 1)
                    act.activation(Z(74 + 4 * q, 78 + 4 * q), Z(74 + 4 * q, 78 + 4 * q), ACT.Sqrt).then_inc(S["ystd"], 1)
            split_seg("gates", evac_sigmoid(82), head_between)
            split_seg("ret")
            split_seg("rwkv")
            split_seg("out", evac_copy(0))
            act.wait_ge(S["x1_done"], 8)
            norm(xs, xn, 1)
            split_seg("wq", evac_copy(32))
            act.wait_ge(S["kT_done"], 1)
            act.activation(keysT, PS[:, 7, 0:256], ACT.Copy).then_inc(S["keysT"], 1)
            for tt in range(2):
                act.wait_ge(S["s_done"], tt + 1)
                act.activation(flat(Z(50 + 8 * tt, 58 + 8 * tt)).rearrange("p (q n) -> p q n", q=4), PS[:, 4 * tt:4 * tt + 4, :],
                               ACT.Copy).then_inc(S["sc_copied"], 1)

            def u_hi(it, k):
                for hh in range(2):
                    act.wait_ge(S["uT_bank"], it * 8 + (2 * k + hh + 1))
                    act.wait_ge(S["half_used"], it * 8 + (2 * (U0 + k) - 3 + hh))
                    act.activation(w_hi[:, k % 2, hh * 512:(hh + 1) * 512], PS[:, 2 * (k % 2) + hh, :], ACT.Copy).then_inc(S["unit_hi"], 1)

            def gelu(it, b):
                act.wait_ge(S["half_used"], it * 8 + (2 * U0 + 4 * b + 4))
                dst = big[:, 2 * it + b, :] if isinstance(it, int) else big[:, ds(it * 2 + b, 1), :].rearrange("p a n -> p (a n)")
                act.activation(dst, PS[:, 4 + b, 0:TOK], ACT.Gelu).then_inc(S[f"gelu{b}"], 1)

            def u_blocks(it):
                for k in range(4):
                    u_hi(it, k)
                    if k == 0 and not (isinstance(it, int) and it == 0):
                        gelu(it - 1, 1)
                    if k == 2:
                        gelu(it, 0)
            run_loop(act, 0, EXP_AT, u_blocks)
            for tt in range(2):
                act.wait_ge(S["topm"], tt + 1)
                act.activation(big[:, 70 + tt, 0:P], big[:, 70 + tt, 0:P], ACT.Exp).then_inc(S["gexp"], 1)
            with act.Fori(EXP_AT, PICKED_AT + 4) as it:
                u_blocks(it)
            act.wait_ge(S["eg_done"], 2)
            with act.Fori(PICKED_AT + 4, BLOCKS // 2) as it:
                u_blocks(it)
            gelu(BLOCKS // 2 - 1, 1)
            for h in range(2):
                def v_hi(it):
                    for k in range(4):
                        u = it * 4 + (V0 + h * BLOCKS + k)
                        act.wait_ge(S["half_used"], u * 2 - 2)
                        act.activation(act_hi[:, k % 2, :], big[:, 4 * it + k, :] if isinstance(it, int) else
                                       big[:, ds(it * 4 + k, 1), :].rearrange("p a n -> p (a n)"), ACT.Copy).then_inc(S["act2_hi"], 1)
                        for hh in range(2):
                            hi(it + (V0 + h * BLOCKS) // 4, k, hh)
                if h == 0:
                    act.wait_ge(S["gated0"], 32)
                    act.wait_ge(S["gated1"], 32)
                    run_loop(act, 0, GATE_PARTS[1][0] // 4, v_hi)
                    act.wait_ge(S["gated0"], 64)
                    act.wait_ge(S["gated1"], 64)
                    with act.Fori(GATE_PARTS[1][0] // 4, BLOCKS // 4) as it:
                        v_hi(it)
                else:
                    run_loop(act, 0, BLOCKS // 4, v_hi)
            act.wait_ge(S["res_done"], 4)
            norm_root([flat(Z(8 * tt, 8 * tt + 8)) for tt in range(2)], [flat(Z(40, 48)), flat(Z(48, 56))], 2)

        @block.gpsimd
        def _(pool):
            ch = Chain(pool, S["pool_chain"])
            z, d = Z(48, 58), Z(74, 84)
            pool.wait_ge(S["proj_evac"], 13)
            pool.tensor_tensor(d[:, :, 1:TOK], z[:, :, 0:TOK - 1], z[:, :, 1:TOK], ALU.subtract)
            ch.link(pool.tensor_scalar(d[:, :, 0:1], z[:, :, 0:1], -1.0, None, ALU.mult))
            ch.link(pool.tensor_tensor(d, d, per_token("rwkv_mix", 16, 10), ALU.mult))
            pool.tensor_tensor(z, z, d, ALU.add).then_inc(S["mixB"], 1)
            pool.memset(Z(106, 114), 0.0).then_inc(S["d1_zero"], 1)
            pool.wait_ge(S["mixA"], 4)
            pp = Z(66, 74).rearrange("p c (n t) -> p (c n) t", t=64)
            pool.memset(pp[:, :, 0:1], 1.0).then_inc(S["pprev1"], 1)
            pool.wait_ge(S["a_done"], 8)
            for k in range(8):
                last = pool.tensor_scalar(big[:, 58 + k, :], big[:, 74 + k, :], 1.0, v1("rwkv_k_a", k), ALU.subtract, ALU.mult)
            last.then_inc(S["ka"], 1)

            pool.wait_ge(S["pre_done"], 1)
            pool.wait_ge(S["proj_evac"], 29)
            pool.wait_ge(S["const_in"], 16)
            for hp in range(2):
                pool.tensor_tensor(rot_part(66, hp), rot_half(hp, 1), rot_table(SIN), ALU.mult).then_inc(S["rot_sin"], 1)
                pool.tensor_tensor(rot_part(82, hp), rot_half(hp, 0), rot_table(SIN), ALU.mult).then_inc(S["rot_sin"], 1)
            pool.wait_ge(S["vT_done"], 4)
            pool.wait_ge(S["o_done"], 4)
            eye = bc(ident, 4)

            def level(lv):
                return bc(cst[:, LEVEL + (lv - 1) * P:LEVEL + lv * P], 4)
            n0 = ch.n

            def pairs(i):
                ch.n, ch.offset = n0, i * 2
                for g in range(2):
                    wait_past(pool, S[f"as{g}"], i)
                    if isinstance(i, int) and i == 0:
                        by_head(pool, i, g, 106, beta_bd)
                        by_head(pool, i, g, 98, kappa_bd)
                    by_head(pool, i, g, 48, v_bd)
                    by_head(pool, i, g, 114, alpha_bd).then_inc(S[f"prep{g}"], 1)
                for g in range(2):
                    pool.wait_ge(S[f"s1e{g}"], i * 4 + 2)
                    ch.link(pool.tensor_tensor(Lm[g], B1[g][:, :, 0, :], level(1), ALU.mult))
                    pool.wait_ge(S[f"s2{g}"], i + 1)
                    pool.tensor_tensor(Xt[g], eye, Lm[g], ALU.subtract).then_inc(S[f"xt1{g}"], 1)
                for lv in range(2, 7):
                    for g in range(2):
                        if lv == 2:
                            pool.wait_ge(S[f"xt1{g}"], i + 1)
                        else:
                            pool.wait_ge(S[f"w{g}"], i * 5 + lv - 2)
                        pool.tensor_tensor(Lm[g], B1[g][:, :, 0, :], level(lv), ALU.mult).then_inc(S[f"lm{g}"], 1)
                assert ch.n == n0 + 2
            run_loop(pool, 0, 4, pairs)
            ch.offset, ch.n = 0, n0 + 8
            ch.link(pool.tensor_tensor(Z(32, 40), Z(32, 40), Z(40, 48), ALU.mult))
            pool.tensor_tensor(Z(32, 40), Z(32, 40), per_token("rwkv_r_k"), ALU.mult).then_inc(S["rk_done"], 1)

        @block.vector
        def _(dve):
            ch = Chain(dve, S["dve_chain"])
            link = ch.link

            def lo(m, slot, hh):
                dve.wait_ge(S["unit_hi"], m * 8 + 2 * slot + hh + 1)
                cols = slice(hh * 512, (hh + 1) * 512)
                dve.tensor_tensor(w_lo[:, slot % 2, cols], raw[:, slot, cols], w_hi[:, slot % 2, cols].bitcast(f32),
                                  ALU.subtract).then_inc(S["unit_split"], 1)

            def split_seg(name, evac=None, between=None):
                u0, g0, ng, ku, _ = SEG[name]

                def body(t, g, m, j):
                    for kq in range(ku):
                        slot = unit_slot(ku, j, kq)
                        if name in operand and isinstance(g, int) and g == 0 and not (name == "out" and kq < 2):
                            split_act(name, kq)
                        for hh in range(2):
                            lo(m, slot, hh)
                        if kq == 1 and evac and not (isinstance(g, int) and g == 0):
                            dve.wait_ge(S["half_used"], m * 8 + (4 * j if ku == 2 else 0))
                            evac(g - 1, (g0 + j + 1) % 2)
                        if between and isinstance(g, int):
                            between(4 * g + kq)
                seg_loop(dve, name, body, PEEL[name] if between else 1)
                if name == "rwkv":
                    split_act("out", 0)
                    split_act("out", 1)
                if evac:
                    dve.wait_ge(S["half_used"], 2 * (u0 + ng * ku))
                    evac(ng - 1, (g0 + ng - 1) % 2)

            def split_act(name, kq):
                pc = SEG[name][4] // 4 + kq
                dve.wait_ge(S["act_hi"], 4 * nth_operand[name] + pc + 1)
                dve.tensor_tensor(act_lo[:, 4 * pc:4 * pc + 4, :], operand[name][:, 4 * pc:4 * pc + 4, :],
                                  act_hi[:, 4 * pc:4 * pc + 4, :].bitcast(f32), ALU.subtract).then_inc(S["act_split"], 1)

            def norm(nth):
                dve.wait_ge(S["norm_sum"], 2 * nth + 2)
                dve.tensor_scalar(ss, ss, 1.0 / DM, NORM_EPS, ALU.mult, ALU.add).then_inc(S["norm_mean"], 1)
                dve.wait_ge(S["norm_root"], nth + 1)
                dve.reciprocal(rstd, rstd).then_inc(S["norm_rstd"], 1)

            dve.wait_ge(S["vecT"], 1)
            dve.tensor_copy(vec[:, :], PS[:, 7, 0:NVEC]).then_inc(S["vec_done"], 1)
            dve.wait_ge(S["vec_done"], 1)
            norm(0)

            def to_channels(base, done, out_sem, weight):
                for gi in range(8):
                    tt, cg = gi // 4, gi % 4
                    dve.wait_ge(S[done], gi + 1)
                    w = vec[:, VEC[weight][0] + 4 * cg:VEC[weight][0] + 4 * cg + 4].unsqueeze(2).broadcast_to([P, 4, P])
                    dve.tensor_tensor(big[:, base + 4 * cg:base + 4 * cg + 4, tt * P:(tt + 1) * P],
                                      PS[:, gi, :].rearrange("p (c n) -> p c n", c=4), w, ALU.mult).then_inc(S[out_sem], 1)
            to_channels(58, "xT_done", "hT", "norm1_w")
            split_seg("main_rwkv")

            def cut(lo_, n=4):
                return [Z(lo_ + q, lo_ + q + n) for q in range(0, 8, n)]

            def shift_steps():
                dve.wait_ge(S["proj_evac"], 13)
                for q in range(0, 16, 4):
                    z, d = Z(32 + q, 36 + q), Z(58 + q, 62 + q)
                    dve.tensor_tensor(d[:, :, 1:TOK], z[:, :, 0:TOK - 1], z[:, :, 1:TOK], ALU.subtract)
                    link(dve.tensor_scalar(d[:, :, 0:1], z[:, :, 0:1], -1.0, None, ALU.mult))
                    yield
                    link(dve.tensor_tensor(d, d, per_token("rwkv_mix", q, 4), ALU.mult))
                    yield
                    dve.tensor_tensor(z, z, d, ALU.add).then_inc(S["mixA"], 1)
                    yield
                dve.wait_ge(S["mixA"], 4)
                for q in range(2):
                    link(dve.tensor_tensor(cut(114)[q], cut(40)[q], per_token("rwkv_k_k", 4 * q, 4), ALU.mult))
                    yield
                dve.wait_ge(S["mixB"], 1)
                for q in range(2):
                    dve.tensor_tensor(cut(82)[q], cut(114)[q], cut(114)[q], ALU.mult).then_inc(S["sq_done"], 1)
                    yield

            def decay_steps():
                dec = Z(90, 98).rearrange("p c (n t) -> p (c n) t", t=64)
                d1 = Z(106, 114).rearrange("p c (n t) -> p (c n) t", t=64)
                prod = Z(98, 106).rearrange("p c (n t) -> p (c n) t", t=64)
                dve.wait_ge(S["dec_done"], 2)
                dve.wait_ge(S["d1_zero"], 1)
                link(dve.tensor_copy(d1[:, :, 0:1], dec[:, :, 0:1]))
                link(dve.memset(dec[:, :, 0:1], 0.0))
                for q in range(2):
                    dve.tensor_tensor_scan(flat(cut(98)[q]), flat(cut(90)[q]), flat(cut(106)[q]), 0.0, ALU.mult,
                                           ALU.add).then_inc(S["scan_done"], 1)
                    yield
                dve.wait_ge(S["scan_done"], 2)
                dve.tensor_copy(pend, prod[:, :, 63])
                for q in range(2):
                    dve.tensor_tensor(cut(90)[q], cut(98)[q], cut(32)[q], ALU.mult)
                    yield
                for q in range(8):
                    link(dve.reciprocal(cut(106, 1)[q], cut(98, 1)[q]))
                    yield
                dve.wait_ge(S["kn_read"], 2)
                for q in range(2):
                    link(dve.tensor_scalar(cut(82)[q], cut(82)[q], 1e-12, None, ALU.max))
                    yield
                for q in range(8):
                    link(dve.reciprocal(cut(82, 1)[q], cut(82, 1)[q]))
                    yield
                for q in range(2):
                    link(dve.tensor_tensor(cut(114)[q], cut(114)[q], cut(82)[q], ALU.mult))
                    yield
                dve.wait_ge(S["ka"], 1)
                for q in range(2):
                    link(dve.scalar_tensor_tensor(flat(cut(40)[q]), flat(cut(58)[q]), 1.0, flat(cut(40)[q]), ALU.add, ALU.mult))
                    yield
                for q in range(2):
                    link(dve.tensor_tensor(cut(74)[q], cut(74)[q], cut(114)[q], ALU.mult))
                    yield
                dve.wait_ge(S["pprev"], 2)
                dve.wait_ge(S["pprev1"], 1)
                for q in range(2):
                    link(dve.tensor_tensor(cut(98)[q], cut(40)[q], cut(106)[q], ALU.mult))
                    yield
                for q in range(2):
                    dve.tensor_tensor(cut(106)[q], cut(74)[q], cut(106)[q], ALU.mult)
                    yield
                for q in range(2):
                    last = dve.tensor_tensor(cut(114)[q], cut(114)[q], cut(66)[q], ALU.mult)
                    yield
                last.then_inc(S["pre_done"], 1)
            shift, decay = shift_steps(), decay_steps()

            def rwkv_between(unit):
                if unit >= PREP_MIX:
                    next(shift, None)
                if unit >= PREP_SCAN:
                    next(decay, None)
            split_seg("main_ret", None, rwkv_between)
            assert next(decay, "ended") == "ended" and next(shift, "ended") == "ended"

            dve.wait_ge(S["proj_evac"], 29)
            for hp in range(2):
                dve.tensor_tensor(rot_part(58, hp), rot_half(hp, 0), rot_table(COS), ALU.mult).then_inc(S["rot_cos"], 1)
                dve.tensor_tensor(rot_part(74, hp), rot_half(hp, 1), rot_table(COS), ALU.mult).then_inc(S["rot_cos"], 1)
                dve.wait_ge(S["rot_cos"], 2 * hp + 2)
                dve.wait_ge(S["rot_sin"], 2 * hp + 2)
                dve.tensor_tensor(rot_half(hp, 0), rot_part(58, hp), rot_part(66, hp), ALU.subtract).then_inc(S["rot_done"], 1)
                dve.tensor_tensor(rot_half(hp, 1), rot_part(74, hp), rot_part(82, hp), ALU.add).then_inc(S["rot_done"], 1)
            dve.wait_ge(S["decay_in"], 16)
            for h in range(HEADS):
                dve.wait_ge(S["sc_done"], h + 1)
                dve.wait_ge(S["rot_done"], 4)
                dve.tensor_tensor(Z(66 + 2 * h, 68 + 2 * h), half(4 + h), Z(82 + 2 * h, 84 + 2 * h), ALU.mult).then_inc(S["st_done"], 1)
            for h in range(HEADS):
                dve.wait_ge(S["o_done"], h + 1)
                for nt in range(2):
                    link(dve.bn_stats(bnst, half(h)[:, nt, :]))
                    link(dve.bn_aggr(mv[:, 2 * h + nt, :], bnst))
            dve.tensor_scalar(rs8, mv[:, :, 1], NORM_EPS, None, ALU.add).then_inc(S["on_var"], 1)
            dve.wait_ge(S["on_sqrt"], 1)
            link(dve.reciprocal(rs8, rs8))
            for k in range(8):
                dve.tensor_scalar(big[:, 58 + k, :], half(k // 2)[:, k % 2, :], mv[:, k, 0:1], rs8[:, k:k + 1], ALU.subtract,
                                  ALU.mult).then_inc(S["on_done"], 1)
            for k in range(8):
                dve.wait_ge(S["oT_done"], k // 2 + 1)
                dve.tensor_scalar(big[:, 66 + k, :], half(4 + k // 2)[:, k % 2, :], v1("ret_gn_w", k), v1("ret_gn_b", k),
                                  ALU.mult, ALU.add).then_inc(S["oret_pre"], 1)
            dve.wait_ge(S["oret_pre"], 8)
            dve.wait_ge(S["silu"], 1)
            dve.tensor_tensor(Z(0, 8), Z(66, 74), Z(24, 32), ALU.mult).then_inc(S["oret"], 1)

            s1mask = bc(cst[:, S1MASK:S1MASK + 256], 2)
            eye4 = bc(ident, 4)
            dve.wait_ge(S["oret"], 1)
            def pairs(i):
                if not isinstance(i, int):
                    for g in range(2):
                        dve.wait_ge(S[f"y{g}"], i)
                        by_head(dve, i, g, 106, beta_bd)
                        by_head(dve, i, g, 98, kappa_bd).then_inc(S[f"prep_bk{g}"], 1)
                for g in range(2):
                    dve.wait_ge(S[f"s1{g}"], i + 1)
                    for q, dst in enumerate((B1, B2)):
                        for n2 in range(2):
                            dve.tensor_tensor(dst[g][:, 2 * n2:2 * n2 + 2, :, :].rearrange("p n w c -> p n (w c)"),
                                              half(4 * g + 2 * q + n2), s1mask, ALU.mult).then_inc(S[f"s1e{g}"], 1)
                for g in range(2):
                    dve.wait_ge(S[f"s2{g}"], i + 1)
                    for w, dst in enumerate((Vn[g], AM[g][:, :, 0, :])):
                        dve.tensor_copy(dst, one(PS[:, 4 * g + w, :])).then_inc(S[f"va{g}"], 1)
                for lv in range(5):
                    for g in range(2):
                        dve.wait_ge(S[f"w{g}"], i * 5 + lv + 1)
                        dve.tensor_tensor(Wn[g], eye4, one(PS[:, 4 * g + 1, :]), ALU.subtract).then_inc(S[f"wn{g}"], 1)
                for g in range(2):
                    dve.wait_ge(S[f"f{g}"], i + 1)
                    dve.tensor_tensor(Lm[g], one(PS[:, 4 * g + 3, :]), eye4, ALU.add).then_inc(S[f"fe{g}"], 1)
                    pe4 = pend[:, ds(i * 8 + 4 * g, 4)].unsqueeze(2).broadcast_to([P, 4, P])
                    dve.tensor_tensor(B1[g][:, :, 0, :], one(PS[:, 4 * g, :]), pe4, ALU.mult).then_inc(S[f"fe{g}"], 1)
                    for h in range(2):
                        rows = slice(64 * h, 64 * h + 64)
                        dve.tensor_tensor(B2[g][rows, :, 0, 64 * h:64 * h + 64], one(PS[rows, 4 * g + 1, :])[:, :, 64 * h:64 * h + 64],
                                          big[rows, ds(i * 2 + (90 + g), 1), :].rearrange("p a (n t) -> p (a n) t", n=4),
                                          ALU.add).then_inc(S[f"fe{g}"], 1)
                for n in (1, 2):
                    for g in range(2):
                        dve.wait_ge(S[f"ch{g}"], i * 2 + n)
                        if n == 1:
                            dve.wait_ge(S[f"fe{g}"], i * 4 + 4)
                        dve.scalar_tensor_tensor(St[g][:, n - 1, :], PS[:, 4 * g + 3, n * P:(n + 1) * P],
                                                 pend[:, ds(i * 8 + (4 * g + n), 1)], B1[g][:, n, 0, :], ALU.mult,
                                                 ALU.add).then_inc(S[f"st{g}"], 1)
            run_loop(dve, 0, 4, pairs)
            def banks(lo_, q):
                return flat(Z(lo_ + 4 * q, lo_ + 4 * q + 4)).rearrange("p (q n) -> p q n", q=2)

            def mean_steps():
                dve.wait_ge(S["ym_done"], 1)
                for q in range(2):
                    dve.scalar_tensor_tensor(banks(58, q), PS[:, 4 + 2 * q:6 + 2 * q, :], -1.0 / 64, banks(114, q), ALU.mult,
                                             ALU.add).then_inc(S["yc_done"], 1)
                    yield

            def var_steps():
                dve.wait_ge(S["yv_done"], 1)
                for q in range(2):
                    dve.tensor_scalar(banks(74, q), PS[:, 4 + 2 * q:6 + 2 * q, :], 1.0 / 64, GN_EPS, ALU.mult,
                                      ALU.add).then_inc(S["yvar"], 1)
                    yield

            def bonus_steps():
                dve.wait_ge(S["bonus"], 1)
                for q in range(2):
                    dve.tensor_tensor(banks(66, q), PS[:, 4 + 2 * q:6 + 2 * q, :], banks(48, q), ALU.mult).then_inc(S["bonus_read"], 1)
                    yield

            def rest_steps():
                dve.wait_ge(S["ystd"], 2)
                for q in range(8):
                    link(dve.reciprocal(cut(74, 1)[q], cut(74, 1)[q]))
                    yield
                for q in range(2):
                    link(dve.tensor_tensor(cut(58)[q], cut(58)[q], cut(74)[q], ALU.mult))
                    yield
                for k in range(8):
                    last = dve.tensor_scalar(big[:, 58 + k, :], big[:, 58 + k, :], v1("rwkv_ln_w", k), v1("rwkv_ln_b", k), ALU.mult, ALU.add)
                    if k % 2:
                        link(last)
                        yield
                dve.wait_ge(S["bonus_read"], 2)
                for q in range(2):
                    link(dve.tensor_tensor(cut(58)[q], cut(58)[q], cut(66)[q], ALU.add))
                    yield
                dve.wait_ge(S["gate_up"], 1)
                for q in range(2):
                    dve.tensor_tensor(banks(8, q), banks(58, q), PS[:, 4 + 2 * q:6 + 2 * q, :], ALU.mult).then_inc(S["orwkv"], 1)
                    yield
            stages = [(0, mean_steps()), (HEAD_VAR, var_steps()), (HEAD_BONUS, bonus_steps()), (HEAD_REST, rest_steps())]

            def head_between(unit):
                for start, steps in stages:
                    if unit >= start:
                        next(steps, None)
            split_seg("gates", None, head_between)
            for _, steps in stages:
                assert next(steps, "ended") == "ended"

            def chunks2(g, base):
                return big[:, base + 2 * g:base + 2 * g + 2, :] if isinstance(g, int) else big[:, ds(g * 2 + base, 2), :]

            def evac_ret(g, par):
                dve.tensor_tensor(chunks2(g, 82), PS[:, 2 * par:2 * par + 2, 0:TOK], chunks2(g, 82), ALU.mult).then_inc(S["proj_evac"], 1)

            def evac_rwkv(g, par):
                dve.tensor_tensor(chunks2(g, 98), PS[:, 2 * par:2 * par + 2, 0:TOK], chunks2(g, 98), ALU.mult).then_inc(S["proj_evac"], 1)
                dve.wait_ge(S["proj_evac"], g + (SEG["rwkv"][1] + 1))
                dve.tensor_tensor(chunks2(g, 58), chunks2(g, 82), chunks2(g, 98), ALU.add).then_inc(S["merged"], 1)
            dve.wait_ge(S["proj_evac"], 45)
            split_seg("ret", evac_ret)
            split_seg("rwkv", evac_rwkv)
            split_seg("out")
            dve.wait_ge(S["x_again"], 16)
            for gi in range(8):
                dve.wait_ge(S["dT_done"], gi + 1)
                cols = slice(gi * 512, (gi + 1) * 512)
                dve.tensor_tensor(flat(Z(90, 106))[:, cols], flat(Z(90, 106))[:, cols], PS[:, gi, :], ALU.add).then_inc(S["x1_done"], 1)
            norm(1)
            to_channels(16, "x2T_done", "h2T", "norm2_w")
            split_seg("wq")

            def places(tt):
                v16 = flat(Z(72 + tt, 73 + tt)).rearrange("p (j k) -> p j k", k=16)
                i16 = flat(Z(74 + tt, 75 + tt)).bitcast(u32).rearrange("p (j k) -> p j k", k=16)
                i16f = flat(Z(76 + tt, 77 + tt)).rearrange("p (j k) -> p j k", k=16)
                top = big[:, 70 + tt, 0:P].rearrange("p (h k) -> p h k", k=16)
                tix = big[:, 78 + tt, 0:P].bitcast(u32).rearrange("p (h k) -> p h k", k=16)
                return v16, i16, i16f, top, tix

            def top16(src, n, vout, iout):
                for r in range(2):
                    for j in range(n):
                        last = dve.max(vout[:, j, 8 * r:8 * r + 8], src[:, j, :])
                        if j % 8 == 7:
                            link(last)
                            yield
                    for j in range(n):
                        last = dve.max_index(iout[:, j, 8 * r:8 * r + 8], vout[:, j, 8 * r:8 * r + 8], src[:, j, :])
                        if j % 8 == 7:
                            link(last)
                            yield
                    for j in range(n if r == 0 else 0):
                        last = dve.match_replace(src[:, j, :], vout[:, j, 0:8], src[:, j, :], -3.0e38)
                        if j % 8 == 7:
                            link(last)
                            yield

            def pick_steps():
                dve.wait_ge(S["x1_out"], 16)
                for tt in range(2):
                    v16, i16, i16f, top, tix = places(tt)
                    tmp_i = [big[:, 80 + tt, w * P:(w + 1) * P].bitcast(u32) for w in range(2)]
                    tmp_f = [big[:, 82 + tt, w * P:(w + 1) * P] for w in range(2)]
                    dve.wait_ge(S["sc_copied"], tt + 1)
                    yield from top16(SC[tt], 16, v16, i16)
                    link(dve.tensor_copy(i16f, i16))
                    cand = flat(Z(84, 92)).rearrange("p (h i j) -> p h i j", h=8, i=16)
                    vv = v16.rearrange("p (h w) k -> p h w k", w=2)
                    link(dve.tensor_tensor(cand, vv[:, :, 0, :].unsqueeze(3).broadcast_to([P, 8, 16, 16]),
                                           vv[:, :, 1, :].unsqueeze(2).broadcast_to([P, 8, 16, 16]), ALU.add))
                    yield
                    yield from top16(cand.rearrange("p h i j -> p h (i j)"), 8, top, tix)
                    tflat = tix.rearrange("p h k -> p (h k)")
                    dve.tensor_scalar(tmp_i[0], tflat, 4, None, ALU.logical_shift_right)
                    link(dve.tensor_scalar(tmp_i[1], tflat, 15, None, ALU.bitwise_and))
                    dve.tensor_copy(tmp_f[0], tmp_i[0])
                    link(dve.tensor_copy(tmp_f[1], tmp_i[1]))
                    ii = i16f.rearrange("p (h w) k -> p h w k", w=2)
                    oh = flat(Z(92, 100)).rearrange("p (h k i) -> p h k i", h=8, k=16)
                    for w in range(2):
                        link(dve.tensor_tensor(oh, tmp_f[w].rearrange("p (h k) -> p h k", h=8).unsqueeze(3).broadcast_to([P, 8, 16, 16]),
                                               iota[:, 0:16].unsqueeze(1).unsqueeze(1).broadcast_to([P, 8, 16, 16]), ALU.is_equal))
                        yield
                        link(dve.tensor_tensor(oh, oh, ii[:, :, w, :].unsqueeze(2).broadcast_to([P, 8, 16, 16]), ALU.mult))
                        yield
                        link(dve.tensor_reduce(big[:, 66 + 2 * w + tt, 0:P].rearrange("p (h k) -> p h k", h=8), oh, AX.X, ALU.add))
                        yield
                    link(dve.tensor_copy(sums[:, 8 * tt:8 * tt + 8], top[:, :, 0]))
                    dve.tensor_tensor(top, top, sums[:, 8 * tt:8 * tt + 8].unsqueeze(2).broadcast_to([P, 8, 16]),
                                      ALU.subtract).then_inc(S["topm"], 1)

            def softmax_rest(tt):
                top = places(tt)[3]
                total = sums[:, 8 * tt:8 * tt + 8]
                dve.wait_ge(S["gexp"], tt + 1)
                link(dve.tensor_reduce(total, top, AX.X, ALU.add))
                link(dve.reciprocal(total, total))
                dve.tensor_tensor(top, top, total.unsqueeze(2).broadcast_to([P, 8, 16]), ALU.mult).then_inc(S["picked"], 1)

            def u_lo(it, k, between=iter(())):
                for hh in range(2):
                    dve.wait_ge(S["unit_hi"], it * 8 + (2 * (U0 + k) + hh + 1))
                    cols = slice(hh * 512, (hh + 1) * 512)
                    dve.tensor_tensor(w_lo[:, k % 2, cols], PS[:, 2 * (k % 2) + hh, :], w_hi[:, k % 2, cols].bitcast(f32),
                                      ALU.subtract).then_inc(S["unit_split"], 1)
                    next(between, None)

            def gate_in(i, k, part):
                par, seen = k % 2, i * (GATE_STEPS[part] // 2) + (GATE_BASE[part] + k // 2)
                lo_, hi_ = GATE_PARTS[part]
                n0 = i * (4 * GATE_STEPS[part]) + 4 * k
                g = big[:, lo_:hi_, n0:n0 + 4] if isinstance(n0, int) else big[:, lo_:hi_, ds(n0, 4)]
                dve.wait_ge(S[f"g_mm{par}"], seen + 1)
                dve.tensor_tensor(g, PS[:, 6 + par, :].rearrange("p (t e) -> p e t", t=4)[:, 0:hi_ - lo_, :], g,
                                  ALU.mult).then_inc(S[f"gated{par}"], 1)

            def gate_step(i, k, part):
                par, seen = k % 2, i * (GATE_STEPS[part] // 2) + (GATE_BASE[part] + k // 2)
                lo_, hi_ = GATE_PARTS[part]
                wait_past(dve, S[f"g_mm{par}"], seen)
                dve.tensor_tensor(hotB[par], bc(iota, 4), bc(eg[:, 1, ds(i * (4 * GATE_STEPS[part]) + 4 * k, 4)], P, 2), ALU.is_equal)
                yield
                for t in range(4):
                    last = dve.tensor_scalar(hotA[:, 4 * par + t, 0:hi_ - lo_], iota[:, lo_:hi_], eg[:, 0, ds(i * (4 * GATE_STEPS[part]) + (4 * k + t), 1)],
                                             eg[:, 2, ds(i * (4 * GATE_STEPS[part]) + (4 * k + t), 1)], ALU.is_equal, ALU.mult)
                last.then_inc(S[f"hot{par}"], 1)
                if k > 0:
                    gate_in(i, k - 1, part)
                elif not (isinstance(i, int) and i == 0):
                    gate_in(i - 1, GATE_STEPS[part] - 1, part)

            def gate_turn(it, i):
                for k in range(4):
                    if isinstance(i, int) and i == 0 and k == 1:
                        dve.wait_ge(S["gelu0"], GATE_AT)
                        dve.wait_ge(S["gelu1"], GATE_AT)
                    u_lo(it, k, gate_step(i, k, 0))
            picks = pick_steps()
            for unit in range(4 * PICKED_AT + 4):
                u_lo(unit // 4, unit % 4)
                if unit < 4 * EXP_AT:
                    next(picks, None)
                if unit == 4 * EXP_AT - 1:
                    assert next(picks, "ended") == "ended"
                if unit == 4 * EXP_AT + 6:
                    softmax_rest(0)
                    softmax_rest(1)
            dve.wait_ge(S["egT"], 1)
            dve.tensor_copy(eg[:, 0:2, :], half(6)).then_inc(S["eg_done"], 1)
            dve.tensor_copy(eg[:, 2, :], PS[:, 7, 0:256]).then_inc(S["eg_done"], 1)
            dve.wait_ge(S["eg_done"], 2)
            with dve.Fori(PICKED_AT + 1, GATE_AT) as it:
                for k in range(4):
                    u_lo(it, k)
            gate_turn(GATE_AT, 0)
            with dve.Fori(1, 16) as i:
                gate_turn(i + GATE_AT, i)
            gate_in(15, 3, 0)
            for h in range(2):
                def v_lo(it, gating=None, first_unit=0):
                    for k in range(4):
                        g = big[:, 4 * it + k, :] if isinstance(it, int) else big[:, ds(it * 4 + k, 1), :].rearrange("p a n -> p (a n)")
                        dve.wait_ge(S["act2_hi"], it * 4 + (h * BLOCKS + k + 1))
                        dve.tensor_tensor(act_lo[:, k % 2, :], g, act_hi[:, k % 2, :].bitcast(f32), ALU.subtract).then_inc(S["act2_split"], 1)
                        u = first_unit + k
                        step = gate_step(gating, u - u // 3, 1) if gating is not None and u % 3 < 2 else iter(())
                        for hh in range(2):
                            lo(it + (V0 + h * BLOCKS) // 4, k, hh)
                            next(step, None)

                def v_gating(i):
                    for j in range(V_TURN):
                        v_lo(i * V_TURN + j, i, 4 * j)
                if h == 0:
                    run_loop(dve, 0, 8, v_gating)
                    gate_in(7, GATE_STEPS[1] - 1, 1)
                    with dve.Fori(8 * V_TURN, BLOCKS // 4) as it:
                        v_lo(it)
                else:
                    run_loop(dve, 0, BLOCKS // 4, v_lo)
            dve.wait_ge(S["x1_in"], 16)
            dve.wait_ge(S["half_used"], 2 * (V0 + 2 * BLOCKS))
            for tt in range(2):
                x1 = flat(Z(8 * tt, 8 * tt + 8)).rearrange("p (h q n) -> p h q n", h=2, q=2)
                for h in range(2):
                    dve.tensor_tensor(x1[:, h], x1[:, h], PS[:, 4 * h + 2 * tt:4 * h + 2 * tt + 2, :], ALU.add).then_inc(S["res_done"], 1)
            norm(2)
            dve.wait_ge(S["norm_rstd"], 3)
            dve.wait_ge(S["fw_in"], 16)
            for tt in range(2):
                dve.scalar_tensor_tensor(flat(Z(24 + 8 * tt, 32 + 8 * tt)), flat(Z(8 * tt, 8 * tt + 8)), rstd[:, tt:tt + 1],
                                         flat(Z(16, 24)), ALU.mult, ALU.mult).then_inc(S["y_ready"], 1)


def shape_constants():
    c = np.zeros((P, NCONST), np.float32)
    i = np.arange(P)
    c[:, IDENT:IDENT + P] = np.eye(P)
    c[:, IOTA:IOTA + P] = i[None, :]
    head, s = i // 64, i % 64
    same = head[:, None] == head[None, :]
    before = s[:, None] < s[None, :]
    c[:, S1MASK:S1MASK + P] = same & before
    c[:, S1MASK + P:S1MASK + 2 * P] = same & (before | (s[:, None] == s[None, :]))
    c[:, BDMASK:BDMASK + P] = same
    for lv in range(1, 7):
        whole = (s[:, None] >> lv) == (s[None, :] >> lv)
        parts = (s[:, None] >> (lv - 1)) != (s[None, :] >> (lv - 1))
        c[:, LEVEL + (lv - 1) * P:LEVEL + lv * P] = same & before & whole & parts
    c[:, ONES:ONES + P] = same
    t = np.arange(TOK)
    inv_freq = np.float32(10000.0) ** (-np.arange(P, dtype=np.float32) * np.float32(2.0) / np.float32(256))
    ang = t.astype(np.float32)[None, :] * inv_freq[:, None].astype(np.float32)
    c[:, COS:COS + TOK] = np.cos(ang)
    c[:, SIN:SIN + TOK] = np.sin(ang)
    m, n = t[:, None], t[None, :]
    decay = np.zeros((P, HEADS, 2, TOK), np.float32)
    for h in range(HEADS):
        log_g = np.log(1.0 - 2.0 ** (-5.0 - h))
        w = np.where((m // 64 == n // 64) | (m < n), np.exp(log_g * np.abs(n - m)), 0.0) / 16.0
        decay[:, h] = w.reshape(2, P, TOK).transpose(1, 0, 2)
    return c, decay.reshape(P, -1)


_INS = ["x", "norm1_w", "w_in", "ret_gn_w", "ret_gn_b", "rwkv_mix", "rwkv_w0", "rwkv_w_up", "rwkv_a0", "rwkv_a_up",
        "rwkv_g_up", "rwkv_k_k", "rwkv_k_a", "rwkv_r_k", "rwkv_ln_w", "rwkv_ln_b", "w_ret_branch", "w_rwkv_branch",
        "w_out", "norm2_w", "peer_w_q", "peer_keys_1", "peer_keys_2", "peer_u", "peer_v", "final_norm_w"]


def kernel(**inputs):
    import numpy as _np
    import concourse.bacc as _bacc
    from concourse import mybir as _mybir
    from concourse.bass_utils import run_bass_kernel_spmd as _run

    nc = _bacc.Bacc("TRN2", target_bir_lowering=False, num_devices=1)
    arrays, args = {}, {}
    for name in _INS:
        arrays[f"in_{name}"] = _np.ascontiguousarray(inputs[name])
    arrays["in_consts"], arrays["in_ret_decay"] = shape_constants()
    for key, v in arrays.items():
        args[key[3:]] = nc.dram_tensor(key, v.shape, _mybir.dt.from_np(v.dtype), kind="ExternalInput").ap()
    args["out"] = nc.dram_tensor("out_0", (1, TOK, DM), _mybir.dt.float32, kind="ExternalOutput").ap()
    hybrid_block_kernel(nc, args)
    r = _run(nc, [arrays], core_ids=[0])
    return r.results[0]["out_0"]
```
